# Optimizing a Trainium2 kernel written in Bass

```python
import math
import jax, jax.numpy as jnp
from jax import lax
import numpy as np

D_MODEL = 1024
BATCH = 1
SEQ = 256
DEPTH = 1

HEAD_DIM = 64
N_HEADS = D_MODEL // 128
ATTN_WIDTH = N_HEADS * HEAD_DIM
Q_BLOCK = 128
CONV_WIDTH = D_MODEL // 2
CONV_K = 31
IN_COLS = 3 * ATTN_WIDTH + N_HEADS + 2 * CONV_WIDTH + 2 * D_MODEL
N_EXPERTS = 32
TOP_K = 4
EXPERT_FF = D_MODEL
SWIGLU_LIMIT = 7.0
SWIGLU_ALPHA = 1.702
GROUP_BLOCK = 128
PLE_DIM = 256

RMS_EPS = 1e-6
LN_EPS = 1e-5
NEG_INF = -1e30

kernel_name = "gated_fox_conformer_moe_block"

def rmsnorm(x, g):
    xf = x.astype(jnp.float32)
    y = xf * lax.rsqrt(jnp.mean(xf * xf, axis=-1, keepdims=True) + RMS_EPS)
    return (y * g.astype(jnp.float32)).astype(x.dtype)

def layernorm(x, g, b):
    xf = x.astype(jnp.float32)
    mu = jnp.mean(xf, axis=-1, keepdims=True)
    var = jnp.mean(jnp.square(xf - mu), axis=-1, keepdims=True)
    y = (xf - mu) * lax.rsqrt(var + LN_EPS)
    return (y * g.astype(jnp.float32) + b.astype(jnp.float32)).astype(x.dtype)

def fox_attention(q, k, v, log_f):
    B, S, H, dh = q.shape
    n_blk = S // Q_BLOCK
    scale = 1.0 / math.sqrt(dh)
    c = jnp.cumsum(log_f, axis=1).transpose(0, 2, 1)
    qh = q.transpose(0, 2, 1, 3)
    kh = k.transpose(0, 2, 1, 3)
    vh = v.transpose(0, 2, 1, 3)
    q_blocks = qh.reshape(B, H, n_blk, Q_BLOCK, dh).transpose(2, 0, 1, 3, 4)
    c_blocks = c.reshape(B, H, n_blk, Q_BLOCK).transpose(2, 0, 1, 3)
    key_pos = jnp.arange(S)

    def one_block(args):
        qi, cqi, bi = args
        s = jnp.einsum('bhqd,bhkd->bhqk', qi, kh).astype(jnp.float32) * scale
        s = s + cqi[..., :, None] - c[:, :, None, :]
        q_pos = bi * Q_BLOCK + jnp.arange(Q_BLOCK)
        s = jnp.where(key_pos[None, :] <= q_pos[:, None], s, NEG_INF)
        pr = jax.nn.softmax(s, axis=-1).astype(vh.dtype)
        return jnp.einsum('bhqk,bhkd->bhqd', pr, vh)

    o = lax.map(one_block, (q_blocks, c_blocks, jnp.arange(n_blk)))
    return o.transpose(1, 0, 3, 2, 4).reshape(B, S, H * dh)

def conformer_conv(u, conv_w, conv_b, ln_g, ln_b, w_out):
    a, gate = jnp.split(u, 2, axis=-1)
    z = a * jax.nn.sigmoid(gate)
    z = lax.conv_general_dilated(
        z, conv_w[:, None, :], window_strides=(1,), padding=[(CONV_K - 1, 0)],
        dimension_numbers=('NWC', 'WIO', 'NWC'), feature_group_count=CONV_WIDTH) + conv_b
    z = jax.nn.silu(layernorm(z, ln_g, ln_b))
    return z @ w_out

def moe_ffn(xn, w_router, b_router, w_gate, b_gate, w_up, b_up, w_down, b_down):
    Bsz, S, D = xn.shape
    T = Bsz * S
    xt = xn.reshape(T, D)
    logits = (xt @ w_router + b_router).astype(jnp.float32)
    top_val, top_idx = lax.top_k(logits, TOP_K)
    gates = jax.nn.softmax(top_val, axis=-1)

    n_assign = T * TOP_K
    e_flat = top_idx.reshape(-1)
    order = jnp.argsort(e_flat, stable=True)
    e_sorted = e_flat[order]
    tok_sorted = order // TOP_K
    counts = jnp.bincount(e_flat, length=N_EXPERTS)
    padded = ((counts + GROUP_BLOCK - 1) // GROUP_BLOCK) * GROUP_BLOCK
    start = jnp.cumsum(counts) - counts
    pad_end = jnp.cumsum(padded)
    pad_start = pad_end - padded
    dest = pad_start[e_sorted] + (jnp.arange(n_assign) - start[e_sorted])

    n_blocks = -(-n_assign // GROUP_BLOCK) + N_EXPERTS
    n_rows = n_blocks * GROUP_BLOCK
    x_pad = jnp.zeros((n_rows, D), xt.dtype).at[dest].set(xt[tok_sorted])
    block_expert = jnp.clip(
        jnp.searchsorted(pad_end, jnp.arange(n_blocks) * GROUP_BLOCK, side='right'),
        0, N_EXPERTS - 1)

    def expert_block(args):
        xb, e = args
        g = xb @ w_gate[e] + b_gate[e]
        u = xb @ w_up[e] + b_up[e]
        g = jnp.minimum(g, SWIGLU_LIMIT)
        u = jnp.clip(u, -SWIGLU_LIMIT, SWIGLU_LIMIT)
        glu = g * jax.nn.sigmoid(SWIGLU_ALPHA * g)
        return ((u + 1.0) * glu) @ w_down[e] + b_down[e]

    y_pad = lax.map(expert_block, (x_pad.reshape(n_blocks, GROUP_BLOCK, D), block_expert))
    y_sorted = y_pad.reshape(n_rows, D)[dest]
    w_sorted = gates.reshape(-1)[order].astype(y_sorted.dtype)
    out = jax.ops.segment_sum(y_sorted * w_sorted[:, None], tok_sorted, num_segments=T)
    return out.reshape(Bsz, S, D)

def setup_inputs(seed: int = 0) -> dict:
    key = jax.random.key(seed)
    ks = jax.random.split(key, 32)
    L, D, E, F = DEPTH, D_MODEL, N_EXPERTS, EXPERT_FF
    f32 = jnp.float32

    def nrm(k, shape, fan_in):
        return jax.random.normal(k, shape, f32) * (fan_in ** -0.5)

    def gain(k, shape):
        return 1.0 + 0.05 * jax.random.normal(k, shape, f32)

    def small(k, shape):
        return 0.02 * jax.random.normal(k, shape, f32)

    return {
        "x": jax.random.normal(ks[0], (BATCH, SEQ, D), f32),
        "p": jax.random.normal(ks[1], (DEPTH, BATCH, SEQ, PLE_DIM), f32),
        "norm_mix": gain(ks[2], (L, D)),
        "w_in": nrm(ks[3], (L, D, IN_COLS), D),
        "b_forget": jax.random.uniform(ks[4], (L, N_HEADS), f32, 1.0, 6.0),
        "w_attn_out": nrm(ks[5], (L, ATTN_WIDTH, D), ATTN_WIDTH),
        "conv_w": nrm(ks[6], (L, CONV_K, CONV_WIDTH), CONV_K),
        "conv_b": small(ks[7], (L, CONV_WIDTH)),
        "conv_ln_g": gain(ks[8], (L, CONV_WIDTH)),
        "conv_ln_b": small(ks[9], (L, CONV_WIDTH)),
        "w_conv_out": nrm(ks[10], (L, CONV_WIDTH, D), CONV_WIDTH),
        "w_o": nrm(ks[11], (L, D, D), D),
        "norm_ffn": gain(ks[12], (L, D)),
        "w_router": nrm(ks[13], (L, D, E), D),
        "b_router": 0.01 * jax.random.normal(ks[14], (L, E), f32),
        "w_gate": nrm(ks[15], (L, E, D, F), D),
        "b_gate": small(ks[16], (L, E, F)),
        "w_up": nrm(ks[17], (L, E, D, F), D),
        "b_up": small(ks[18], (L, E, F)),
        "w_down": nrm(ks[19], (L, E, F, D), F),
        "b_down": small(ks[20], (L, E, D)),
        "norm_ple": gain(ks[21], (L, D)),
        "w_ple_gate": nrm(ks[22], (L, D, D), D),
        "w_ple_proj": nrm(ks[23], (L, PLE_DIM, D), PLE_DIM),
        "norm_final": gain(ks[24], (D,)),
    }

def reference(x, p, norm_mix, w_in, b_forget, w_attn_out, conv_w, conv_b, conv_ln_g, conv_ln_b,
              w_conv_out, w_o, norm_ffn, w_router, b_router, w_gate, b_gate, w_up, b_up,
              w_down, b_down, norm_ple, w_ple_gate, w_ple_proj, norm_final):
    B, S, D = x.shape
    split_at = np.cumsum([ATTN_WIDTH, ATTN_WIDTH, ATTN_WIDTH, N_HEADS, 2 * CONV_WIDTH, D_MODEL])
    h = x
    for i in range(DEPTH):
        xn = rmsnorm(h, norm_mix[i])
        proj = xn @ w_in[i]
        q, k, v, f_logit, conv_in, g_attn, g_conv = jnp.split(proj, list(split_at), axis=-1)
        log_f = jax.nn.log_sigmoid((f_logit + b_forget[i]).astype(jnp.float32))
        attn = fox_attention(q.reshape(B, S, N_HEADS, HEAD_DIM),
                             k.reshape(B, S, N_HEADS, HEAD_DIM),
                             v.reshape(B, S, N_HEADS, HEAD_DIM), log_f)
        branch_a = attn @ w_attn_out[i]
        branch_c = conformer_conv(conv_in, conv_w[i], conv_b[i], conv_ln_g[i], conv_ln_b[i],
                                  w_conv_out[i])
        merged = jax.nn.sigmoid(g_attn) * branch_a + jax.nn.sigmoid(g_conv) * branch_c
        h = h + merged @ w_o[i]
        h = h + moe_ffn(rmsnorm(h, norm_ffn[i]), w_router[i], b_router[i], w_gate[i], b_gate[i],
                        w_up[i], b_up[i], w_down[i], b_down[i])
        pg = jax.nn.sigmoid(rmsnorm(h, norm_ple[i]) @ w_ple_gate[i])
        h = h + pg * (p[i] @ w_ple_proj[i])
    return rmsnorm(h, norm_final)


_drawn_inputs = setup_inputs


def setup_inputs(seed=0):
    import zlib

    import numpy as np

    out = dict(_drawn_inputs(seed))
    spreads = {}
    factors = {'b_gate': 7.093, 'b_up': 8.0, 'b_down': 6.724, 'norm_ple': 6.775}
    for name, (base, spread) in spreads.items():
        noise = np.random.default_rng([zlib.crc32(name.encode()), seed]).standard_normal(out[name].shape)
        drawn = base * np.exp(spread * noise) if base else spread * noise
        out[name] = __import__('jax').numpy.asarray(drawn.astype(out[name].dtype))
    for name, factor in factors.items():
        out[name] = (out[name] * factor).astype(out[name].dtype)
    return out
```

```python
from contextlib import ExitStack

import concourse.bass as bass
from concourse import mybir

F32 = mybir.dt.float32
BF16 = mybir.dt.bfloat16
I32 = mybir.dt.int32
ALU = mybir.AluOpType
ACT = mybir.ActivationFunctionType
AX_X = mybir.AxisListType.X

P = 128
NEG_INF = -1e30
RMS_EPS = 1e-6
LN_EPS = 1e-5
SWIGLU_LIMIT = 7.0
SWIGLU_ALPHA = 1.702


def build_block(nc, x, p, norm_mix, w_in, b_forget, w_attn_out, conv_w, conv_b, conv_ln_g, conv_ln_b,
                w_conv_out, w_o, norm_ffn, w_router, b_router, w_gate, b_gate, w_up, b_up,
                w_down, b_down, norm_ple, w_ple_gate, w_ple_proj, norm_final, out):
    _, T, D = x.shape
    E = w_router.shape[2]
    H = b_forget.shape[1]
    AW = w_attn_out.shape[1]
    CW = w_conv_out.shape[1]
    TAPS = conv_w.shape[1]
    PLE = w_ple_proj.shape[1]
    HD = AW // H
    NT, KD, KA, KP = T // P, D // P, AW // P, PLE // P
    HALF = D // 2
    SCALE = float(HD) ** -0.5
    SLOTS = 64
    CHUNKS = T // SLOTS
    BLK = 256
    RING = 12
    PER_MAT = RING // 3
    assert (NT, KD, KA, KP, E, H, HD) == (2, 8, 4, 2, 32, 8, 64) and w_gate.shape[3] == D and CW == AW

    col_q, col_k, col_v, col_f = 0, AW, 2 * AW, 3 * AW
    col_ca = col_f + H
    col_cg = col_ca + CW
    col_ga = col_cg + CW
    col_gc = col_ga + D
    BLOCKS = [("ca", 0), ("cg", 0), ("ca", 1), ("cg", 1), ("q", 0), ("k", 0), ("q", 1), ("k", 1), ("v", 0), ("v", 1)]
    FIRST_GATE = len(BLOCKS)
    BLOCKS += [("ga", b) for b in range(4)] + [("gc", b) for b in range(4)]
    NB = len(BLOCKS)
    COL0 = {"q": col_q, "k": col_k, "v": col_v, "ca": col_ca, "cg": col_cg, "ga": col_ga, "gc": col_gc}
    AO_SLOT, CO_SLOT = NB % RING, (NB + 2) % RING
    assert AO_SLOT == 6 and CO_SLOT == 8

    with ExitStack() as ctx:
        def sb(name, shape, dt):
            return ctx.enter_context(nc.sbuf_tensor(name, shape, dt))

        def sem(name):
            return ctx.enter_context(nc.semaphore(name))

        ring = sb("ring", [P, RING, 2048], F32)
        wide = sb("wide", [P, 8192], F32)
        reg_a = sb("reg_a", [P, 3072], F32)
        reg_b = sb("reg_b", [P, 2048], F32)
        reg_c = sb("reg_c", [P, 1024], F32)
        reg_d = sb("reg_d", [P, 2176], F32)
        reg_e = sb("reg_e", [P, 4096], F32)
        reg_f = sb("reg_f", [P, 1536], F32)
        h = sb("h", [P, NT, D], F32)
        hnT = sb("hnT", [P, KD, T], F32)

        def view(reg, lo, hi, spec, **kw):
            return reg[:, lo:hi].rearrange(spec, **kw)

        w_o_sb = view(wide, 0, 8192, "p (k n) -> p k n", k=KD)
        x_parts = wide[:, 0:3072].bitcast(BF16).rearrange("p (t s d) -> p t s d", t=NT, s=3)
        xT = view(wide, 3072, 3584, "p (k s) -> p k s", k=KD)
        g_clip = wide[:, 3584:4096]
        g_sig = wide[:, 4096:4608]
        u_clip = wide[:, 4608:5120]
        hT = view(wide, 5120, 5632, "p (j s) -> p j s", j=4)
        y_sb = wide[:, 5632:6144]
        selT = view(wide, 6144, 6656, "p (b t) -> p b t", b=2)
        h_act = wide[:, 6656:7168]
        g_final = wide[:, 7168:8192]

        qT = view(reg_a, 0, 1024, "p (j t) -> p j t", j=KA)
        kT = view(reg_a, 1024, 2048, "p (j t) -> p j t", j=KA)
        v_sb = view(reg_a, 2048, 3072, "p (t c) -> p t c", t=NT)
        ln_out = view(reg_a, 1024, 2048, "p (t c) -> p t c", t=NT)
        b_down_sb = reg_a[0:E, 0:1024]
        gatesT = reg_a[0:E, 1024:1280]
        bias3 = reg_a[0:3 * E, 2048:3072].bitcast(BF16)

        glu_sig = view(reg_b, 0, 512, "p (j t) -> p j t", j=2)
        f_tmp = reg_b[0:H, 512:2048].rearrange("p (n t) -> p n t", n=6)
        probs = view(reg_b, 0, 1024, "p (b h k) -> p b h k", b=2, h=2)
        probsT = view(reg_b, 1024, 2048, "p (b j q) -> p b j q", b=2, j=4)
        ple_v = view(reg_b, 0, 2048, "p (t d) -> p t d", t=NT)

        taps_in = reg_c[0:TAPS, 0:CW]
        attnT = view(reg_c, 0, 1024, "p (j t) -> p j t", j=KA)
        p_sb = view(reg_c, 0, 512, "p (t d) -> p t d", t=NT)
        pT = view(reg_c, 512, 1024, "p (k t) -> p k t", k=KP)

        PAD = TAPS - 1
        ZW = PAD + T
        z_pad = view(reg_d, 0, 4 * ZW, "p (j t) -> p j t", j=4)
        conv = view(reg_d, 4 * ZW, 4 * ZW + 1024, "p (j t) -> p j t", j=4)
        silu_sig = view(reg_d, 0, 1024, "p (j t) -> p j t", j=4)
        bias_in = reg_d[0:3 * E, 0:2048]

        sig_a = view(reg_e, 0, 2048, "p (j t) -> p j t", j=KD)
        sig_c = view(reg_e, 2048, 4096, "p (j t) -> p j t", j=KD)
        w_proj_sb = view(reg_e, 2048, 4096, "p (k n) -> p k n", k=KP)
        tok_tmp = view(reg_e, 0, 2048, "p (t d) -> p t d", t=NT)
        tok_tmp2 = view(reg_e, 2048, 4096, "p (t d) -> p t d", t=NT)

        cum_base = reg_f[:, 0:256]
        cum_key = reg_f[:, 256:512]
        cum_q = view(reg_f, 512, 1536, "p (b h t) -> p b h t", b=2, h=2)

        ident = sb("ident", [P, P], F32)
        ident_b = sb("ident_b", [P, P], BF16)
        causal_b = sb("causal_b", [P, P], BF16)
        before_b = sb("before_b", [P, P], BF16)
        ones_b = sb("ones_b", [P, P], BF16)
        ones_r = sb("ones_r", [1, P], F32)
        head_hot = sb("head_hot", [P, H], F32)
        params_in = sb("params_in", [36, P], F32)
        params = sb("params", [P, 36 + 4 * TAPS], F32)
        w_f = sb("w_f", [P, KD, H], F32)
        b_f = sb("b_f", [H, 1], F32)
        w_router_sb = sb("w_router_sb", [P, KD, E], F32)
        b_router_sb = sb("b_router_sb", [1, E], F32)
        slot_id = sb("slot_id", [P, CHUNKS, 2, SLOTS], BF16)
        expert_hot = sb("expert_hot", [3 * E, E], F32)
        hot = sb("hot", [3 * E, 2, SLOTS], BF16)
        sel = sb("sel", [P, 2, NT, 2, SLOTS], BF16)
        ranks = sb("ranks", [P, NT, E], F32)
        gates3 = sb("gates3", [P, NT, E, 3], BF16)
        gate_slot = sb("gate_slot", [P, 2], F32)
        gate_parts = sb("gate_parts", [P, 3], F32)
        stat = sb("stat", [P, 32], F32)
        mhalf = sb("mhalf", [P, 2], F32)
        sm_stat = sb("sm_stat", [P, 2, 6], F32)
        top8 = sb("top8", [P, NT, 8], F32)
        flag = sb("flag", [1, 1], I32)
        flag_f = sb("flag_f", [1, 1], F32)
        g_mix, g_ffn, g_ple = params[:, 0:8], params[:, 8:16], params[:, 16:24]
        cb, lg, lb = params[:, 24:28], params[:, 28:32], params[:, 32:36]


        logits, above, ties, tie_no, gate_w, rest = (
            view(reg_e, 2048 + n * NT * E, 2048 + (n + 1) * NT * E, "p (t e) -> p t e", t=NT) for n in range(6))
        hot_mask = sb("routed", [P, NT, E], BF16)

        def tap(j, m):
            return params[:, 36 + m * TAPS + j:37 + m * TAPS + j]

        bank = [ctx.enter_context(nc.psum_tensor(f"bank{i}", [P, HALF], F32)) for i in range(8)]
        acc_bank = [[bank[0], bank[1]], [bank[2], bank[3]]]
        bank_g, bank_u, bank_y, bank_x = bank[4:8]

        x_in, params_dma, forget_dma, wo_dma, p_dma, proj_dma = [sem(n) for n in (
            "x_in", "params_dma", "forget_dma", "wo_dma", "p_dma", "proj_dma")]
        bias_dma, bdown_dma, final_dma, router_dma, out_dma = [sem(n) for n in (
            "bias_dma", "bdown_dma", "final_dma", "router_dma", "out_dma")]
        block_dma = [sem(f"block_dma{n}") for n in range(NB)]
        ao_dma, co_dma = sem("ao_dma"), sem("co_dma")
        chunk_dma = [sem(f"chunk_dma{n}") for n in range(RING)]
        pgate_dma = [sem(f"pgate_dma{n}") for n in range(PER_MAT)]
        names = """consts params_turned params_ready sumsq mean_sq rstd normed x_turned hnT_ready
            block_done block_out forget_done f_neg f_exp f_ln f_steps cum_steps cum_q_ready glu_ready z_ready
            conv_step head_scored scores_done row_max probs_exp probs_norm rows_recip probs_turned probsT_ready pv_done attn_ready
            conv_turned ln_step ln_pow ln_ready ln_back silu_arg silu_ready gates_sig
            branch_a branch_c merge_step merged wo_done h_mid
            pple_turned pT_ready proj_done ple_ready part_step part_a part_b
            logits_done route_step route_exp rank_done rank_ready gatesT_done gatesT_ready counts_done flag_ready
            bias_part bias_part_a bias_ready bdown_done parts_ready
            sel_ready gathered xT_ready gslot_ready selT_ready gclip_ready gsig_ready gglu uclip h_ready
            turned hT_ready y_ready combined chunk_used
            tail_h tail_turned tail_T tail_pg tail_sig tail_step out_ready""".split()
        s = {n: sem(n) for n in names}

        def bcast(ap, n):
            return ap.unsqueeze(len(ap.shape)).broadcast_to(list(ap.shape) + [n])

        N_CONST = 21
        N_PARAM = 7
        w_in_k = w_in[0].rearrange("(k p) n -> p k n", p=P)
        mats = [w_gate, w_up, w_down]
        ROWS = D // PER_MAT


        def load_chunks(sp, i, e):
            for c in range(RING):
                if not isinstance(i, int) or i > 0:
                    sp.wait_ge(s["chunk_used"], (i - 1) * RING + (c + 1))
                rows = mats[c // PER_MAT][0, e, (c % PER_MAT) * ROWS:(c % PER_MAT + 1) * ROWS, :]
                sp.dma_start(ring[:, c, :].rearrange("p (k n) -> p k n", n=D),
                             rows.rearrange("(k p) n -> p k n", p=P)).then_inc(chunk_dma[c], 16)

        def pe_gather(pe, i, b):
            pe.wait_ge(s["sel_ready"], i + 1)
            for k in range(KD):
                for n in range(3 * NT):
                    t, part = n // 3, n % 3
                    nc.tensor.matmul(bank_x[:, k * SLOTS:(k + 1) * SLOTS], x_parts[:, t, part, k * P:(k + 1) * P],
                                     sel[:, b, t, 0, :], start=n == 0, stop=n == 3 * NT - 1)
            for t in range(NT):
                nc.tensor.transpose(bank_y[:, t * 64:(t + 1) * 64].bitcast(BF16),
                                    sel[:, b, t].rearrange("p a s -> p (a s)"), ident_b[:])

        def pe_gather_gates(i, e, b):
            for t in range(NT):
                last = nc.tensor.matmul(bank_y[:, 256:259], sel[:, b, t].rearrange("p a s -> p (a s)"),
                                        gates3[:, t, e, :], start=t == 0, stop=t == NT - 1)
            last.then_inc(s["gathered"], 1)

        def pe_expand(pe, i, b, which):
            dst = bank_u if which else bank_g
            for n in range(2):
                nc.tensor.matmul(dst[n * 64:(n + 1) * 64, :], hot[:, b, :],
                                 bias3[:, which * D + n * HALF:which * D + (n + 1) * HALF], start=True, stop=False)
            for c in range(PER_MAT):
                slot = which * PER_MAT + c
                pe.wait_ge(chunk_dma[slot], (i + 1) * 16)
                for kk in range(2):
                    for n in range(2):
                        last = nc.tensor.matmul(dst[n * 64:(n + 1) * 64, :], xT[:, 2 * c + kk, :],
                                                ring[:, slot, kk * D + n * HALF:kk * D + (n + 1) * HALF],
                                                start=False, stop=c == PER_MAT - 1 and kk == 1)
                last.then_inc(s["chunk_used"], 1)

        def pe_gate(pe, i, b):
            pe.wait_ge(s["xT_ready"], i + 1)
            pe_expand(pe, i, b, 0)

        def pe_up(pe, i, b):
            pe_expand(pe, i, b, 1)

        def pe_turn(pe, i):
            pe.wait_ge(s["h_ready"], i + 1)
            for j in range(4):
                last = nc.tensor.transpose(bank_u[:, j * P:(j + 1) * P], h_act[:, j * P:(j + 1) * P], ident[:])
            last.then_inc(s["turned"], 1)

        def pe_down(pe, i, prepared):
            pe.wait_ge(s["hT_ready"], i + 1)
            pe.wait_ge(s["selT_ready"], prepared)
            pe.wait_ge(s["gslot_ready"], prepared)
            for c in range(PER_MAT):
                slot = 2 * PER_MAT + c
                pe.wait_ge(chunk_dma[slot], (i + 1) * 16)
                for kk in range(2):
                    k = 2 * c + kk
                    for n in range(2):
                        last = nc.tensor.matmul(bank_y[n * 64:(n + 1) * 64, :],
                                                hT[:, k % 4, (k // 4) * 64:(k // 4 + 1) * 64],
                                                ring[:, slot, kk * D + n * HALF:kk * D + (n + 1) * HALF],
                                                start=k == 0, stop=k == KD - 1)
                last.then_inc(s["chunk_used"], 1)

        def pe_combine(pe, i, b):
            pe.wait_ge(s["y_ready"], i + 1)
            for t in range(NT):
                for n in range(2):
                    last = nc.tensor.matmul(acc_bank[t][n][:, :], selT[n * 64:(n + 1) * 64, b, t * P:(t + 1) * P],
                                            y_sb[n * 64:(n + 1) * 64, :], start=False, stop=True,
                                            skip_group_check=True)
            last.then_inc(s["combined"], 1)

        def dve_select(dve, i, e, b, chunk, back):
            if not isinstance(i, int) or i >= back:
                dve.wait_ge(s["gathered"], i - (back - 1))
                dve.wait_ge(s["chunk_used"], (i - back) * RING + 2 * PER_MAT)
            nc.vector.tensor_scalar(hot[:, b, :], expert_hot[:, bass.ds(e, 1)].broadcast_to([3 * E, SLOTS]), 1.0, None,
                                    ALU.mult)
            for t in range(NT):
                last = nc.vector.tensor_scalar(sel[:, b, t].rearrange("p a s -> p (a s)"),
                                               slot_id[:, chunk].rearrange("p a s -> p (a s)"),
                                               ranks[:, t, bass.ds(e, 1)], None, ALU.is_equal)
            last.then_inc(s["sel_ready"], 1)

        def dve_take(dve, i, b):
            dve.wait_ge(s["gathered"], i + 1)
            nc.vector.tensor_tensor(xT, bank_x[:, :].rearrange("p (k s) -> p k s", k=KD), bcast(g_ffn, SLOTS),
                                    ALU.mult).then_inc(s["xT_ready"], 1)

        def dve_activate(dve, i):
            dve.wait_ge(s["chunk_used"], i * RING + PER_MAT)
            nc.vector.tensor_scalar(g_clip, bank_g[:, :], SWIGLU_LIMIT, None, ALU.min).then_inc(s["gclip_ready"], 1)
            dve.wait_ge(s["gsig_ready"], i + 1)
            nc.vector.tensor_tensor(g_clip, g_clip, g_sig, ALU.mult).then_inc(s["gglu"], 1)
            dve.wait_ge(s["chunk_used"], i * RING + 2 * PER_MAT)
            nc.vector.tensor_scalar(u_clip, bank_u[:, :], SWIGLU_LIMIT, -SWIGLU_LIMIT, ALU.min,
                                    ALU.max).then_inc(s["uclip"], 1)
            dve.wait_ge(s["uclip"], i + 1)
            dve.wait_ge(s["gglu"], i + 1)
            nc.vector.scalar_tensor_tensor(out=h_act, in0=u_clip, scalar=1.0, in1=g_clip, op0=ALU.add,
                                           op1=ALU.mult).then_inc(s["h_ready"], 1)

        def act_sigmoid(act, i):
            act.wait_ge(s["gclip_ready"], i + 1)
            nc.scalar.activation(g_sig, g_clip, ACT.Sigmoid, scale=SWIGLU_ALPHA).then_inc(s["gsig_ready"], 1)

        def act_selT(act, i, b):
            act.wait_ge(s["gathered"], i + 1)
            nc.scalar.activation(selT[:, b, :], bank_y[:, 0:P].bitcast(BF16), ACT.Copy).then_inc(s["selT_ready"], 1)
            nc.scalar.activation(gate_parts[:], bank_y[:, 256:259], ACT.Copy,
                                 accum_out=gate_slot[:, b:b + 1]).then_inc(s["gslot_ready"], 1)

        def act_hT(act, i):
            act.wait_ge(s["turned"], i + 1)
            nc.scalar.activation(hT.rearrange("p j s -> p (j s)"), bank_u[:, :], ACT.Copy).then_inc(s["hT_ready"], 1)

        def act_y(act, i, b):
            act.wait_ge(s["chunk_used"], (i + 1) * RING)
            act.wait_ge(s["gslot_ready"], i + 1)
            nc.scalar.activation(y_sb, bank_y[:, :], ACT.Copy, scale=gate_slot[:, b:b + 1]).then_inc(s["y_ready"], 1)

        def take_attention(dve, u):
            dve.wait_ge(s["pv_done"], u + 1)
            nc.vector.tensor_copy(attnT[:, u // 2, (u % 2) * P:(u % 2 + 1) * P],
                                  bank[7][:, 0:P]).then_inc(s["attn_ready"], 1)

        def over_passes(eng, first, body, last):
            first()
            body(0, 0, 0)
            with eng.Fori(0, E // 2 - 1) as pair:
                body(pair * 2 + 1, pair * 2 + 1, 1)
                body(pair * 2 + 2, pair * 2 + 2, 0)
            last()

        def overflow(eng, body):
            eng.wait_ge(s["flag_ready"], 1)
            n = eng.value_load(flag[0:1, 0:1], min_val=0, max_val=T)
            with eng.If(n > SLOTS):
                with eng.Fori(0, E) as e:
                    for chunk in range(1, CHUNKS):
                        body(e * (CHUNKS - 1) + (E + chunk - 1), e, chunk)
            with eng.Else():
                pass

        block = ctx.enter_context(nc.Block())

        @block.sync
        def _(sp):
            sp.dma_start(h[:], x[0].rearrange("(t p) d -> p t d", p=P)).then_inc(x_in, 16)

            def load_block(n):
                kind, b = BLOCKS[n]
                c0 = COL0[kind] + b * BLK
                if n >= RING:
                    sp.wait_ge(s["block_done"], n - RING + 1)
                sp.dma_start(ring[:, n % RING, :].rearrange("p (k c) -> p k c", k=KD),
                             w_in_k[:, :, c0:c0 + BLK]).then_inc(block_dma[n], 16)

            for n in range(RING):
                load_block(n)
            sp.dma_start(w_o_sb, w_o[0].rearrange("(k p) n -> p k n", p=P)).then_inc(wo_dma, 16)
            for n in range(RING, NB):
                load_block(n)
            for slot, src, got in ((AO_SLOT, w_attn_out, ao_dma), (CO_SLOT, w_conv_out, co_dma)):
                sp.wait_ge(s["block_done"], slot + 2)
                sp.dma_start(ring[:, slot:slot + 2, :].rearrange("p s (k n) -> p (s k) n", n=D),
                             src[0].rearrange("(k p) n -> p k n", p=P)).then_inc(got, 16)
            for c in range(RING):
                if c < AO_SLOT:
                    sp.wait_ge(s["block_done"], RING + c + 1)
                elif c < CO_SLOT:
                    sp.wait_ge(s["branch_a"], 1)
                elif c < CO_SLOT + 2:
                    sp.wait_ge(s["branch_c"], 4)
                if c == AO_SLOT:
                    sp.dma_start(p_sb, p[0, 0].rearrange("(t p) d -> p t d", p=P)).then_inc(p_dma, 16)
                    sp.dma_start(b_down_sb, b_down[0]).then_inc(bdown_dma, 16)
                if c == CO_SLOT:
                    for part in range(3):
                        for m, bias in enumerate((b_gate, b_up)):
                            sp.dma_start(bias_in[part * E:(part + 1) * E, m * D:(m + 1) * D],
                                         bias[0]).then_inc(bias_dma, 16)
                    sp.wait_ge(s["merged"], 4)
                    sp.dma_start(w_proj_sb, w_ple_proj[0].rearrange("(k p) n -> p k n", p=P)).then_inc(proj_dma, 16)
                rows = mats[c // PER_MAT][0, 0, (c % PER_MAT) * ROWS:(c % PER_MAT + 1) * ROWS, :]
                sp.dma_start(ring[:, c, :].rearrange("p (k n) -> p k n", n=D),
                             rows.rearrange("(k p) n -> p k n", p=P)).then_inc(chunk_dma[c], 16)
            sp.wait_ge(s["wo_done"], 1)
            sp.dma_start(g_final, norm_final.rearrange("(a d) -> a d", a=1).partition_broadcast(P)
                         ).then_inc(final_dma, 16)
            with sp.Fori(1, E) as i:
                load_chunks(sp, i, i)
            overflow(sp, lambda i, e, chunk: load_chunks(sp, i, e))
            for c in range(PER_MAT):
                sp.wait_ge(s["chunk_used"], (E - 1) * RING + c + 1)
                sp.dma_start(ring[:, c, :].rearrange("p (k n) -> p k n", n=D),
                             w_ple_gate[0, c * ROWS:(c + 1) * ROWS, :].rearrange("(k p) n -> p k n", p=P)
                             ).then_inc(pgate_dma[c], 16)
            for t in range(NT):
                sp.wait_ge(s["out_ready"], t + 1)
                sp.dma_start(out[0, t * P:(t + 1) * P, :], tok_tmp[:, t, :]).then_inc(out_dma, 16)
            sp.wait_ge(out_dma, 16 * NT)

        @block.gpsimd
        def _(pool):
            n = [0]

            def const(ins):
                n[0] += 1
                ins.then_inc(s["consts"], 1)
                pool.wait_ge(s["consts"], n[0])

            def masked(t, op, fill, base, pattern, mult):
                const(nc.gpsimd.affine_select(out=t, in_=t, compare_op=op, fill=fill, base=base, pattern=pattern,
                                              channel_multiplier=mult))

            const(nc.gpsimd.memset(mhalf[:], -0.5))
            for t in (ident, ident_b):
                const(nc.gpsimd.memset(t[:], 0.0))
                masked(t[:], ALU.not_equal, 1.0, 0, [[-1, P]], 1)
            const(nc.gpsimd.memset(ones_b[:], 1.0))
            const(nc.gpsimd.memset(ones_r[:], 1.0))
            const(nc.gpsimd.memset(z_pad[:, :, 0:PAD], 0.0))
            const(nc.gpsimd.memset(head_hot[:], 0.0))
            masked(head_hot[:], ALU.not_equal, 1.0, 0, [[-1, H]], 1)
            masked(head_hot[:], ALU.not_equal, 1.0, -32, [[-1, H]], 1)
            const(nc.gpsimd.memset(causal_b[:], 0.0))
            masked(causal_b[:], ALU.is_ge, NEG_INF, 0, [[-1, P]], 1)
            const(nc.gpsimd.memset(before_b[:], 1.0))
            masked(before_b[:], ALU.is_gt, 0.0, 0, [[1, P]], -1)
            const(nc.gpsimd.iota(slot_id[:].rearrange("p c a s -> p (c a s)"),
                                 pattern=[[SLOTS, CHUNKS], [0, 2], [1, SLOTS]], base=0, channel_multiplier=0,
                                 allow_small_or_imprecise_dtypes=True))
            const(nc.gpsimd.memset(expert_hot[:], 0.0))
            for part in range(3):
                masked(expert_hot[:], ALU.not_equal, 1.0, -part * E, [[-1, E]], 1)
            const(nc.gpsimd.memset(reg_f[:, 0:512], 0.0))
            assert n[0] == N_CONST, n[0]

            def power(ready, count, out, in_, done):
                pool.wait_ge(s[ready], count)
                nc.gpsimd.tensor_tensor(out, in_, mhalf[:, 0:out.shape[1]], ALU.pow).then_inc(s[done], 1)

            power("mean_sq", 1, stat[:, 4:6], stat[:, 2:4], "rstd")
            power("ln_step", 4, stat[:, 28:30], stat[:, 26:28], "ln_pow")
            power("mean_sq", 2, stat[:, 4:6], stat[:, 2:4], "rstd")
            for t in range(NT):
                power("mean_sq", 3 + t, stat[:, 4 + t:5 + t], stat[:, 2 + t:3 + t], "rstd")
            for t in range(NT):
                power("mean_sq", 3 + NT + t, stat[:, 4 + t:5 + t], stat[:, 2 + t:3 + t], "rstd")

        @block.tensor
        def _(pe):
            pe.wait_ge(s["consts"], 3)
            pe.wait_ge(params_dma, 16 * N_PARAM)
            nc.tensor.transpose(bank[0][:, 0:36], params_in[:], ident[0:36, 0:36])
            for m in range(4):
                last = nc.tensor.transpose(bank[0][:, 36 + m * TAPS:36 + (m + 1) * TAPS],
                                           taps_in[:, m * P:(m + 1) * P], ident[0:TAPS, 0:TAPS])
            last.then_inc(s["params_turned"], 1)

            def turn_tokens(src, first_bank, ready, first_count, done, tiles=range(NT)):
                for g in (2 * t + half for t in tiles for half in range(2)):
                    t = g // 2
                    pe.wait_ge(s[ready], first_count + t)
                    for c in range(4):
                        k = (g % 2) * 4 + c
                        last = nc.tensor.transpose(bank[first_bank + g][:, c * P:(c + 1) * P],
                                                   src[:, t, k * P:(k + 1) * P], ident[:])
                    last.then_inc(s[done], 1)

            turn_tokens(tok_tmp, 4, "normed", 1, "x_turned")

            def project(n):
                kind, _ = BLOCKS[n]
                dst = bank[n % 2]
                pe.wait_ge(block_dma[n], 16)
                if n >= 2:
                    pe.wait_ge(s["block_out"], n - 1)
                else:
                    pe.wait_ge(s["params_ready"], 1)
                w = ring[:, n % RING, :].rearrange("p (k c) -> p k c", k=KD)
                for j in range(2):
                    for k in range(KD):
                        a, b = w[:, k, j * P:(j + 1) * P], hnT[:, k, :]
                        if kind == "v":
                            a, b = hnT[:, k, j * P:(j + 1) * P], w[:, k, :]
                        last = nc.tensor.matmul(dst[:, j * BLK:(j + 1) * BLK], a, b, start=k == 0, stop=k == KD - 1)
                last.then_inc(s["block_done"], 1)

            pe.wait_ge(s["hnT_ready"], 4)
            for n in range(4):
                project(n)
            pe.wait_ge(forget_dma, 16 * 2)
            for k in range(KD):
                last = nc.tensor.matmul(bank[2][0:H, 0:T], w_f[:, k, :], hnT[:, k, :], start=k == 0, stop=k == KD - 1)
            last.then_inc(s["forget_done"], 1)
            for n in range(4, FIRST_GATE):
                project(n)

            def scores(u):
                hp, qb = u // 2, u % 2
                dst = bank[4 + u % 2]
                nk = (qb + 1) * P
                pe.wait_ge(s["cum_q_ready"], hp + 1)
                if u == 0:
                    pe.wait_ge(s["block_out"], FIRST_GATE)
                if u >= 2:
                    pe.wait_ge(s["probs_exp"], 2 * (u - 1))
                for hh in range(2):
                    row = slice(hh * HD, (hh + 1) * HD)
                    if hh:
                        pe.wait_ge(s["head_scored"], u + 1)
                    o = dst[:, hh * 256:hh * 256 + nk]
                    nc.tensor.matmul(o, qT[row, hp, qb * P:(qb + 1) * P], kT[row, hp, 0:nk], start=True, stop=False)
                    nc.tensor.matmul(o, cum_q[:, hp % 2, hh, qb * P:(qb + 1) * P], cum_key[:, 0:nk],
                                     start=False, stop=False)
                    last = nc.tensor.matmul(dst[:, hh * 256 + qb * P:hh * 256 + nk], ident_b[:], causal_b[:],
                                            start=False, stop=True)
                    last.then_inc(s["scores_done" if hh else "head_scored"], 1)

            def turn_probs(u):
                qb = u % 2
                pe.wait_ge(s["probs_norm"], u + 1)
                if u >= 1:
                    pe.wait_ge(s["probsT_ready"], u)
                for hh in range(2):
                    for kb in range(qb + 1):
                        last = nc.tensor.transpose(bank[6][:, (2 * hh + kb) * P:(2 * hh + kb + 1) * P],
                                                   probs[:, u % 2, hh, kb * P:(kb + 1) * P], ident[:])
                last.then_inc(s["probs_turned"], 1)

            def attend(u):
                hp, qb = u // 2, u % 2
                pe.wait_ge(s["probsT_ready"], u + 1)
                if u >= 1:
                    pe.wait_ge(s["attn_ready"], u)
                for kb in range(qb + 1):
                    for hh in range(2):
                        last = nc.tensor.matmul(bank[7][hh * HD:(hh + 1) * HD, 0:P],
                                                v_sb[:, kb, hp * P + hh * HD:hp * P + (hh + 1) * HD],
                                                probsT[:, u % 2, 2 * hh + kb, :], start=kb == 0, stop=kb == qb)
                last.then_inc(s["pv_done"], 1)

            def conv_to_tokens():
                pe.wait_ge(s["conv_step"], 4 * TAPS)
                for t in range(NT):
                    for m in range(4):
                        last = nc.tensor.transpose(bank[2 + t][:, m * P:(m + 1) * P], conv[:, m, t * P:(t + 1) * P],
                                                   ident[:])
                    last.then_inc(s["conv_turned"], 1)

            def conv_to_channels():
                pe.wait_ge(s["ln_ready"], 2)
                for m in range(4):
                    for t in range(NT):
                        last = nc.tensor.transpose(bank[2 + m // 2][:, (m % 2) * T + t * P:(m % 2) * T + (t + 1) * P],
                                                   ln_out[:, t, m * P:(m + 1) * P], ident[:])
                    if m % 2:
                        last.then_inc(s["ln_back"], 1)

            scores(0)
            for u in range(8):
                project(FIRST_GATE + u)
                if u < 7:
                    scores(u + 1)
                turn_probs(u)
                if u >= 1:
                    attend(u - 1)
            conv_to_tokens()
            attend(7)

            def branch(first_bank, slot, src, got, ready, count, done):
                pe.wait_ge(got, 16)
                pe.wait_ge(s[ready], count)
                w = ring[:, slot:slot + 2, :].rearrange("p s (k n) -> p (s k) n", n=D)
                for m in range(KD):
                    for k in range(KA):
                        last = nc.tensor.matmul(bank[first_bank + m // 2][:, (m % 2) * T:(m % 2 + 1) * T],
                                                w[:, k, m * P:(m + 1) * P], src[:, k, :], start=k == 0,
                                                stop=k == KA - 1)
                    if m % 2 and done == "branch_c":
                        last.then_inc(s[done], 1)
                if done == "branch_a":
                    last.then_inc(s[done], 1)

            branch(4, AO_SLOT, attnT, ao_dma, "attn_ready", 8, "branch_a")
            conv_to_channels()
            pe.wait_ge(s["block_out"], NB)
            branch(0, CO_SLOT, conv, co_dma, "silu_ready", 1, "branch_c")
            pe.wait_ge(wo_dma, 16)
            pe.wait_ge(s["merge_step"], 4)
            for d in range(4):
                pe.wait_ge(s["merged"], d + 1)
                for k in (2 * d, 2 * d + 1):
                    for t in range(NT):
                        for n in range(2):
                            last = nc.tensor.matmul(bank[4 + 2 * t + n][:, :], sig_a[:, k, t * P:(t + 1) * P],
                                                    w_o_sb[:, k, n * HALF:(n + 1) * HALF], start=k == 0,
                                                    stop=k == KD - 1)
            last.then_inc(s["wo_done"], 1)

            pe.wait_ge(p_dma, 16)
            for k in range(KP):
                for t in range(NT):
                    last = nc.tensor.transpose(bank[0][:, k * T + t * P:k * T + (t + 1) * P],
                                               p_sb[:, t, k * P:(k + 1) * P], ident[:])
            last.then_inc(s["pple_turned"], 1)
            pe.wait_ge(s["pT_ready"], 1)
            pe.wait_ge(proj_dma, 16)
            for t in range(NT):
                for n in range(2):
                    for k in range(KP):
                        last = nc.tensor.matmul(bank[2 * t + n][:, :], pT[:, k, t * P:(t + 1) * P],
                                                w_proj_sb[:, k, n * HALF:(n + 1) * HALF], start=k == 0,
                                                stop=k == KP - 1)
            last.then_inc(s["proj_done"], 1)

            turn_tokens(tok_tmp, 4, "normed", 1 + NT, "x_turned")
            pe.wait_ge(s["hnT_ready"], 8)
            pe.wait_ge(router_dma, 32)
            pe.wait_ge(s["ple_ready"], 1)
            for t in range(NT):
                o = bank[0][:, t * E:(t + 1) * E]
                nc.tensor.matmul(o, ones_r[:], b_router_sb[:], start=True, stop=False)
                for k in range(KD):
                    last = nc.tensor.matmul(o, hnT[:, k, t * P:(t + 1) * P], w_router_sb[:, k, :],
                                            start=False, stop=k == KD - 1)
            last.then_inc(s["logits_done"], 1)
            pe.wait_ge(s["rank_ready"], 1)
            routed = hot_mask
            nc.tensor.matmul(bank[1][:, 0:E], before_b[:], routed[:, 0, :], start=True, stop=True)
            nc.tensor.matmul(bank[1][:, E:2 * E], ones_b[:], routed[:, 0, :], start=True, stop=False)
            nc.tensor.matmul(bank[1][:, E:2 * E], before_b[:], routed[:, 1, :], start=False, stop=True)
            for t in range(NT):
                last = nc.tensor.matmul(bank[2][0:1, 0:E], ones_b[:, 0:1], routed[:, t, :], start=t == 0,
                                        stop=t == NT - 1)
            last.then_inc(s["rank_done"], 1)
            pe.wait_ge(s["rank_ready"], 2)
            for t in range(NT):
                last = nc.tensor.transpose(bank[3][0:E, t * P:(t + 1) * P], gate_w[:, t, :], ident[:])
            last.then_inc(s["gatesT_done"], 1)

            def gather(i, e, b):
                pe_gather(pe, i, b)
                pe_gather_gates(i, e, b)

            def first():
                pe.wait_ge(s["parts_ready"], 1)
                gather(0, 0, 0)
                pe.wait_ge(s["gatesT_ready"], 1)
                pe.wait_ge(s["rank_ready"], 3)
                pe.wait_ge(s["flag_ready"], 1)
                pe.wait_ge(bdown_dma, 16)
                for t in range(NT):
                    for n in range(2):
                        nc.tensor.matmul(acc_bank[t][n][:, :], gatesT[:, t * P:(t + 1) * P],
                                         b_down_sb[:, n * HALF:(n + 1) * HALF], start=True, stop=True)
                pe.wait_ge(s["bias_ready"], 1)

            def one(i, e, b):
                pe_gate(pe, i, b)
                pe_up(pe, i, b)
                if isinstance(i, int) and i == 0:
                    pe.wait_ge(s["gslot_ready"], 1)
                else:
                    pe_combine(pe, i - 1, 1 - b)
                gather(i + 1, e + 1, 1 - b)
                pe_turn(pe, i)
                pe_down(pe, i, i + 2)

            def last_one():
                i, b = E - 1, 1
                pe_gate(pe, i, b)
                pe_up(pe, i, b)
                pe_combine(pe, i - 1, 0)
                pe_turn(pe, i)
                pe_down(pe, i, E)
                pe_combine(pe, i, b)

            over_passes(pe, first, one, last_one)

            def further(i, e, chunk):
                gather(i, e, 0)
                pe_gate(pe, i, 0)
                pe_up(pe, i, 0)
                pe_turn(pe, i)
                pe_down(pe, i, i + 1)
                pe_combine(pe, i, 0)

            overflow(pe, further)

            for t in range(NT):
                turn_tokens(tok_tmp, 4, "normed", 1 + 2 * NT, "x_turned", (t,))
                pe.wait_ge(s["hnT_ready"], 10 + 2 * t)
                for k in range(KD):
                    pe.wait_ge(pgate_dma[k // 2], 16)
                    for n in range(2):
                        last = nc.tensor.matmul(acc_bank[t][n][:, :], hnT[:, k, t * P:(t + 1) * P],
                                                ring[:, k // 2, (k % 2) * D + n * HALF:(k % 2) * D + (n + 1) * HALF],
                                                start=k == 0, stop=k == KD - 1)
                last.then_inc(s["tail_pg"], 1)


        @block.scalar
        def _(act):
            row = 0
            for v, n in ((norm_mix, KD), (norm_ffn, KD), (norm_ple, KD), (conv_b, 4), (conv_ln_g, 4), (conv_ln_b, 4)):
                act.dma_start(params_in[row:row + n, :], v[0].rearrange("(c p) -> c p", p=P)).then_inc(params_dma, 16)
                row += n
            act.dma_start(taps_in, conv_w[0]).then_inc(params_dma, 16)
            act.dma_start(w_f[:], w_in_k[:, :, col_f:col_f + H]).then_inc(forget_dma, 16)
            act.dma_start(b_f[:], b_forget[0].rearrange("(h a) -> h a", a=1)).then_inc(forget_dma, 16)
            act.dma_start(w_router_sb[:], w_router[0].rearrange("(k p) e -> p k e", p=P)).then_inc(router_dma, 16)
            act.dma_start(b_router_sb[:], b_router).then_inc(router_dma, 16)

            def square(t, dump):
                nc.scalar.activation(dump, h[:, t, :], ACT.Square, accum_out=stat[:, t:t + 1]).then_inc(s["sumsq"], 1)

            act.wait_ge(x_in, 16)
            for t in range(NT):
                square(t, tok_tmp[:, t, :])

            def read_out(n):
                kind, b = BLOCKS[n]
                act.wait_ge(s["block_done"], n + 1)
                src = bank[n % 2][:, :].rearrange("p (j t) -> p j t", j=2)
                if kind == "v":
                    dst = v_sb[:, :, b * BLK:(b + 1) * BLK]
                elif kind == "ca":
                    dst = z_pad[:, 2 * b:2 * b + 2, PAD:]
                elif kind == "cg":
                    dst = glu_sig
                else:
                    dst = {"q": qT, "k": kT, "ga": sig_a, "gc": sig_c}[kind][:, 2 * b:2 * b + 2, :]
                if kind == "cg" and b:
                    act.wait_ge(s["z_ready"], b)
                nc.scalar.activation(dst, src, ACT.Sigmoid if kind == "cg" else ACT.Copy).then_inc(s["block_out"], 1)

            for n in range(4):
                read_out(n)
            act.wait_ge(s["f_steps"], 3)
            nc.scalar.activation(f_tmp[:, 3, :], f_tmp[:, 2, :], ACT.Exp, scale=-1.0).then_inc(s["f_exp"], 1)
            act.wait_ge(s["f_exp"], 1)
            nc.scalar.activation(f_tmp[:, 4, :], f_tmp[:, 3, :], ACT.Ln, bias=1.0).then_inc(s["f_ln"], 1)
            for n in range(4, FIRST_GATE):
                read_out(n)

            for u in range(8):
                nk = (u % 2 + 1) * P
                act.wait_ge(s["row_max"], u + 1)
                if u >= 2:
                    act.wait_ge(s["probs_turned"], u - 1)
                for hh in range(2):
                    nc.scalar.activation(probs[:, u % 2, hh, 0:nk], bank[4 + u % 2][:, hh * 256:hh * 256 + nk],
                                         ACT.Exp, bias=sm_stat[:, u % 2, 2 + hh:3 + hh], scale=SCALE,
                                         accum_out=sm_stat[:, u % 2, 4 + hh:5 + hh]).then_inc(s["probs_exp"], 1)
                read_out(FIRST_GATE + u)
                act.wait_ge(s["probs_turned"], u + 1)
                if u >= 2:
                    act.wait_ge(s["pv_done"], u - 1)
                kbs = u % 2 + 1
                nc.scalar.activation(probsT[:, u % 2].rearrange("p (a k) q -> p a k q", a=2)[:, :, 0:kbs, :],
                                     bank[6][:, :].rearrange("p (a k q) -> p a k q", a=2, k=2)[:, :, 0:kbs, :],
                                     ACT.Copy).then_inc(s["probsT_ready"], 1)

            act.wait_ge(s["block_out"], NB)
            for t_ in (sig_a, sig_c):
                v = t_.rearrange("p j t -> p (j t)")
                nc.scalar.activation(v, v, ACT.Sigmoid).then_inc(s["gates_sig"], 1)
            for m in range(4):
                act.wait_ge(s["ln_step"], 5 + m)
                nc.scalar.activation(silu_sig[:, m, :], conv[:, m, :], ACT.Sigmoid).then_inc(s["silu_arg"], 1)

            act.wait_ge(s["pple_turned"], 1)
            nc.scalar.activation(pT.rearrange("p k t -> p (k t)"), bank[0][:, :], ACT.Copy).then_inc(s["pT_ready"], 1)
            for t in range(NT):
                act.wait_ge(s["h_mid"], 2 * (t + 1))
                square(t, tok_tmp[:, t, :])
            act.wait_ge(s["proj_done"], 1)
            for t in range(NT):
                for n in range(2):
                    last = nc.scalar.activation(ple_v[:, t, n * HALF:(n + 1) * HALF], bank[2 * t + n][:, :], ACT.Copy)
            last.then_inc(s["ple_ready"], 1)

            act.wait_ge(s["normed"], 2 * NT)
            nc.scalar.activation(x_parts[:, :, 0, :], tok_tmp, ACT.Copy).then_inc(s["part_a"], 1)
            act.wait_ge(s["part_step"], 1)
            nc.scalar.activation(x_parts[:, :, 1, :], tok_tmp, ACT.Copy).then_inc(s["part_a"], 1)
            act.wait_ge(s["f_neg"], 1)
            nc.scalar.activation(rest, rest, ACT.Exp).then_inc(s["route_exp"], 1)
            act.wait_ge(s["gatesT_done"], 1)
            nc.scalar.activation(gatesT, bank[3][0:E, 0:T], ACT.Copy).then_inc(s["gatesT_ready"], 1)

            def first():
                act_selT(act, 0, 0)

            def one(i, e, b):
                act_sigmoid(act, i)
                act_selT(act, i + 1, 1 - b)
                act_hT(act, i)
                act_y(act, i, b)

            def last_one():
                act_sigmoid(act, E - 1)
                act_hT(act, E - 1)
                act_y(act, E - 1, 1)

            over_passes(act, first, one, last_one)

            def further(i, e, chunk):
                act_selT(act, i, 0)
                act_sigmoid(act, i)
                act_hT(act, i)
                act_y(act, i, 0)

            overflow(act, further)

            for t in range(NT):
                act.wait_ge(s["tail_h"], t + 1)
                square(t, tok_tmp[:, t, :])
            for t in range(NT):
                act.wait_ge(s["tail_pg"], t + 1)
                for n in range(2):
                    last = nc.scalar.activation(tok_tmp2[:, t, n * HALF:(n + 1) * HALF], acc_bank[t][n][:, :],
                                                ACT.Sigmoid)
                last.then_inc(s["tail_sig"], 1)
                act.wait_ge(s["tail_step"], 2 * t + 2)
                square(t, tok_tmp2[:, t, :])

        @block.vector
        def _(dve):
            n_mean = [0]

            def mean_square(t0, t1, count):
                dve.wait_ge(s["sumsq"], count)
                nc.vector.tensor_scalar(stat[:, 2 + t0:2 + t1], stat[:, t0:t1], 1.0 / D, RMS_EPS, ALU.mult,
                                        ALU.add).then_inc(s["mean_sq"], 1)
                n_mean[0] += 1

            def normalise(t, count):
                dve.wait_ge(s["rstd"], count)
                nc.vector.tensor_scalar(tok_tmp[:, t, :], h[:, t, :], stat[:, 4 + t:5 + t], None,
                                        ALU.mult).then_inc(s["normed"], 1)

            def take_turned(g, gain, count):
                t, half = g // 2, g % 2
                dve.wait_ge(s["x_turned"], count)
                nc.vector.tensor_tensor(hnT[:, half * 4:half * 4 + 4, t * P:(t + 1) * P],
                                        bank[4 + g][:, :].rearrange("p (c q) -> p c q", c=4),
                                        bcast(gain[:, half * 4:half * 4 + 4], P), ALU.mult).then_inc(s["hnT_ready"], 1)

            mean_square(0, NT, NT)
            for t in range(NT):
                normalise(t, 1)
            dve.wait_ge(s["params_turned"], 1)
            nc.vector.tensor_copy(params[:], bank[0][:, 0:36 + 4 * TAPS]).then_inc(s["params_ready"], 1)
            dve.wait_ge(s["params_ready"], 1)
            for g in range(4):
                take_turned(g, g_mix, g + 1)

            dve.wait_ge(s["consts"], N_CONST)
            nc.vector.memset(cum_base[0:H, :], 1.0).then_inc(s["cum_steps"], 1)
            nc.vector.memset(cum_key[32:32 + H, :], 1.0).then_inc(s["cum_steps"], 1)

            def convolve(b):
                dve.wait_ge(s["block_out"], 2 * b + 2)
                z = z_pad[:, 2 * b:2 * b + 2, PAD:]
                nc.vector.tensor_tensor(z, z, glu_sig, ALU.mult).then_inc(s["z_ready"], 1)
                dve.wait_ge(s["z_ready"], b + 1)
                for j in range(TAPS):
                    for m in (2 * b, 2 * b + 1):
                        n = 2 * TAPS * b + 2 * j + m % 2
                        if j:
                            dve.wait_ge(s["conv_step"], n - 1)
                            ins = nc.vector.scalar_tensor_tensor(out=conv[:, m, :], in0=z_pad[:, m, j:j + T],
                                                                 scalar=tap(j, m), in1=conv[:, m, :], op0=ALU.mult,
                                                                 op1=ALU.add)
                        else:
                            ins = nc.vector.tensor_scalar(conv[:, m, :], z_pad[:, m, 0:T], tap(0, m), cb[:, m:m + 1],
                                                          ALU.mult, ALU.add)
                        ins.then_inc(s["conv_step"], 1)

            convolve(0)

            dve.wait_ge(s["forget_done"], 1)
            nc.vector.tensor_scalar(f_tmp[:, 0, :], bank[2][0:H, 0:T], b_f[:, 0:1], None,
                                    ALU.add).then_inc(s["f_steps"], 1)
            dve.wait_ge(s["f_steps"], 1)
            nc.vector.tensor_scalar(f_tmp[:, 1, :], f_tmp[:, 0, :], 0.0, None, ALU.min).then_inc(s["f_steps"], 1)
            nc.vector.scalar_tensor_tensor(out=f_tmp[:, 2, :], in0=f_tmp[:, 0, :], scalar=-1.0, in1=f_tmp[:, 0, :],
                                           op0=ALU.mult, op1=ALU.max).then_inc(s["f_steps"], 1)
            dve.wait_ge(s["f_ln"], 1)
            nc.vector.tensor_tensor(f_tmp[:, 5, :], f_tmp[:, 1, :], f_tmp[:, 4, :],
                                    ALU.subtract).then_inc(s["f_steps"], 1)
            dve.wait_ge(s["f_steps"], 4)
            dve.wait_ge(s["cum_steps"], 2)
            nc.vector.tensor_tensor_scan(f_tmp[:, 0, :], cum_base[0:H, :], f_tmp[:, 5, :], 0.0, ALU.mult,
                                         ALU.add).then_inc(s["f_steps"], 1)
            dve.wait_ge(s["f_steps"], 5)
            nc.vector.tensor_scalar(cum_base[32:32 + H, :], f_tmp[:, 0, :], 1.0 / SCALE, None,
                                    ALU.mult).then_inc(s["cum_steps"], 1)
            nc.vector.tensor_scalar(cum_key[0:H, :], f_tmp[:, 0, :], -1.0 / SCALE, None,
                                    ALU.mult).then_inc(s["cum_steps"], 1)
            dve.wait_ge(s["cum_steps"], 4)

            def spread(hp):
                if hp >= 2:
                    dve.wait_ge(s["scores_done"], 2 * (hp - 1))
                for hh in range(2):
                    last = nc.vector.tensor_scalar(cum_q[:, hp % 2, hh, :], cum_base, head_hot[:, 2 * hp + hh:2 * hp + hh + 1],
                                                   None, ALU.mult)
                last.then_inc(s["cum_q_ready"], 1)

            spread(0)
            spread(1)
            convolve(1)

            for u in range(8):
                b, hp, qb = u % 2, u // 2, u % 2
                nk = (qb + 1) * P
                dve.wait_ge(s["scores_done"], u + 1)
                nc.vector.tensor_reduce(sm_stat[:, b, 0:2],
                                        bank[4 + b][:, :].rearrange("p (a k) -> p a k", a=2)[:, :, 0:nk], AX_X,
                                        ALU.max).then_inc(s["rows_recip"], 1)
                dve.wait_ge(s["rows_recip"], 2 * u + 1)
                nc.vector.tensor_scalar(sm_stat[:, b, 2:4], sm_stat[:, b, 0:2], -SCALE, None,
                                        ALU.mult).then_inc(s["row_max"], 1)
                if qb and hp + 2 < 4:
                    spread(hp + 2)
                dve.wait_ge(s["probs_exp"], 2 * u + 2)
                nc.vector.reciprocal(sm_stat[:, b, 0:2], sm_stat[:, b, 4:6]).then_inc(s["rows_recip"], 1)
                dve.wait_ge(s["rows_recip"], 2 * u + 2)
                for hh in range(2):
                    last = nc.vector.tensor_scalar(probs[:, b, hh, 0:nk], probs[:, b, hh, 0:nk],
                                                   sm_stat[:, b, hh:hh + 1], None, ALU.mult)
                last.then_inc(s["probs_norm"], 1)
                if u:
                    take_attention(dve, u - 1)

            def ln_stats():
                for t in range(NT):
                    dve.wait_ge(s["conv_turned"], t + 1)
                    nc.vector.bn_stats(stat[:, 8 + 6 * t:14 + 6 * t], bank[2 + t][:, :]).then_inc(s["ln_step"], 1)
                dve.wait_ge(s["ln_step"], 2)
                for t in range(NT):
                    last = nc.vector.bn_aggr(stat[:, 20 + 2 * t:22 + 2 * t], stat[:, 8 + 6 * t:14 + 6 * t])
                last.then_inc(s["ln_step"], 1)
                dve.wait_ge(s["ln_step"], 3)
                nc.vector.tensor_scalar(stat[:, 26:28], stat[:, 20:24].rearrange("p (t v) -> p t v", v=2)[:, :, 1],
                                        LN_EPS, None, ALU.add).then_inc(s["ln_step"], 1)

            ln_stats()
            take_attention(dve, 7)
            dve.wait_ge(s["ln_pow"], 1)
            for t in range(NT):
                nc.vector.tensor_scalar(ln_out[:, t, :], bank[2 + t][:, :], stat[:, 20 + 2 * t:21 + 2 * t],
                                        stat[:, 28 + t:29 + t], ALU.subtract, ALU.mult).then_inc(s["ln_ready"], 1)
            for m in range(4):
                dve.wait_ge(s["ln_back"], m // 2 + 1)
                nc.vector.tensor_scalar(conv[:, m, :], bank[2 + m // 2][:, (m % 2) * T:(m % 2 + 1) * T],
                                        lg[:, m:m + 1], lb[:, m:m + 1], ALU.mult, ALU.add).then_inc(s["ln_step"], 1)
            dve.wait_ge(s["silu_arg"], 4)
            dve.wait_ge(s["ln_step"], 8)
            nc.vector.tensor_tensor(conv, conv, silu_sig, ALU.mult).then_inc(s["silu_ready"], 1)

            dve.wait_ge(s["branch_a"], 1)
            dve.wait_ge(s["gates_sig"], 2)
            for m in range(4):
                v = sig_a[:, 2 * m:2 * m + 2, :].rearrange("p j t -> p (j t)")
                nc.vector.tensor_tensor(v, v, bank[4 + m][:, :], ALU.mult).then_inc(s["merge_step"], 1)
            for m in range(4):
                va = sig_a[:, 2 * m:2 * m + 2, :].rearrange("p j t -> p (j t)")
                vc = sig_c[:, 2 * m:2 * m + 2, :].rearrange("p j t -> p (j t)")
                dve.wait_ge(s["branch_c"], m + 1)
                nc.vector.tensor_tensor(vc, vc, bank[m][:, :], ALU.mult).then_inc(s["merge_step"], 1)
                dve.wait_ge(s["merge_step"], 5 + m)
                nc.vector.tensor_tensor(va, va, vc, ALU.add).then_inc(s["merged"], 1)

            bstep = [0]

            def link(ins, name, count):
                count[0] += 1
                ins.then_inc(s[name], 1)
                dve.wait_ge(s[name], count[0])

            dve.wait_ge(bias_dma, 16 * 6)
            link(nc.vector.tensor_copy(bias3, bias_in), "bias_part", bstep)
            link(nc.vector.tensor_tensor(bias_in, bias_in, bias3, ALU.subtract), "bias_part", bstep)
            link(nc.vector.tensor_copy(bias3[E:2 * E], bias_in[E:2 * E]), "bias_part", bstep)
            link(nc.vector.tensor_copy(bias3[2 * E:3 * E], bias_in[2 * E:3 * E]), "bias_part", bstep)
            link(nc.vector.tensor_tensor(bias_in[2 * E:3 * E], bias_in[2 * E:3 * E], bias3[2 * E:3 * E],
                                         ALU.subtract), "bias_part", bstep)
            nc.vector.tensor_copy(bias3[2 * E:3 * E], bias_in[2 * E:3 * E]).then_inc(s["bias_ready"], 1)

            dve.wait_ge(s["wo_done"], 1)
            for t in range(NT):
                for n in range(2):
                    v = h[:, t, n * HALF:(n + 1) * HALF]
                    nc.vector.tensor_tensor(v, v, bank[4 + 2 * t + n][:, :], ALU.add).then_inc(s["h_mid"], 1)
            mean_square(0, NT, 2 * NT)
            for t in range(NT):
                normalise(t, 2)
            for g in range(4):
                take_turned(g, g_ffn, 5 + g)
            dve.wait_ge(s["part_a"], 1)
            nc.vector.tensor_tensor(tok_tmp, tok_tmp, x_parts[:, :, 0, :], ALU.subtract).then_inc(s["part_step"], 1)

            rstep = [0]

            def route(ins):
                link(ins, "route_step", rstep)

            def wide_of(col):
                return col.broadcast_to([P, NT, E])

            dve.wait_ge(s["logits_done"], 1)
            dve.wait_ge(s["ple_ready"], 1)
            route(nc.vector.tensor_copy(logits.rearrange("p t e -> p (t e)"), bank[0][:, 0:NT * E]))
            for t in range(NT):
                route(nc.vector.max(top8[:, t, :], logits[:, t, :]))
            route(nc.vector.memset(rest, 1.0))
            route(nc.vector.tensor_tensor(above, logits, wide_of(top8[:, :, 3:4]), ALU.is_gt))
            route(nc.vector.tensor_tensor(ties, logits, wide_of(top8[:, :, 3:4]), ALU.is_equal))
            route(nc.vector.reduce_sum(stat[:, 6:8], above, AX_X))
            for t in range(NT):
                route(nc.vector.tensor_tensor_scan(tie_no[:, t, :], rest[:, t, :], ties[:, t, :], stat[:, 6 + t:7 + t],
                                                   ALU.mult, ALU.add))
            route(nc.vector.scalar_tensor_tensor(out=ties, in0=tie_no, scalar=4.0, in1=ties, op0=ALU.is_le,
                                                 op1=ALU.mult))
            route(nc.vector.tensor_tensor(above, above, ties, ALU.add))
            nc.vector.tensor_copy(hot_mask[:], above).then_inc(s["rank_ready"], 1)
            nc.vector.tensor_tensor(rest, logits, wide_of(top8[:, :, 0:1]), ALU.subtract).then_inc(s["f_neg"], 1)
            dve.wait_ge(s["route_exp"], 1)
            route(nc.vector.tensor_tensor(gate_w, rest, above, ALU.mult))
            route(nc.vector.reduce_sum(stat[:, 6:8], gate_w, AX_X))
            route(nc.vector.reciprocal(stat[:, 24:26], stat[:, 6:8]))
            nc.vector.tensor_tensor(gate_w, gate_w, wide_of(stat[:, 24:26].unsqueeze(2)),
                                    ALU.mult).then_inc(s["rank_ready"], 1)
            dve.wait_ge(s["rank_done"], 1)
            route(nc.vector.scalar_tensor_tensor(out=ranks[:], in0=bank[1][:, 0:NT * E].rearrange("p (t e) -> p t e", t=NT),
                                                 scalar=1.0, in1=above, op0=ALU.add, op1=ALU.mult))
            nc.vector.tensor_scalar(ranks[:], ranks[:], -1.0, None, ALU.add).then_inc(s["rank_ready"], 1)
            route(nc.vector.reduce_max(flag_f[:], bank[2][0:1, 0:E], AX_X))
            nc.vector.tensor_copy(flag[:], flag_f[:]).then_inc(s["flag_ready"], 1)
            dve.wait_ge(s["rank_ready"], 3)
            route(nc.vector.tensor_copy(gates3[:, :, :, 0], gate_w))
            route(nc.vector.tensor_tensor(rest, gate_w, gates3[:, :, :, 0], ALU.subtract))
            route(nc.vector.tensor_copy(gates3[:, :, :, 1], rest))
            route(nc.vector.tensor_tensor(gates3[:, :, :, 2], rest, gates3[:, :, :, 1], ALU.subtract))
            dve.wait_ge(s["part_a"], 2)
            nc.vector.tensor_tensor(x_parts[:, :, 2, :], tok_tmp, x_parts[:, :, 1, :],
                                    ALU.subtract).then_inc(s["parts_ready"], 1)

            def first():
                dve_select(dve, 0, 0, 0, 0, 2)
                dve_take(dve, 0, 0)

            def one(i, e, b):
                dve_select(dve, i + 1, e + 1, 1 - b, 0, 2)
                dve_activate(dve, i)
                dve_take(dve, i + 1, 1 - b)

            over_passes(dve, first, one, lambda: dve_activate(dve, E - 1))

            def further(i, e, chunk):
                dve_select(dve, i, e, 0, chunk, 1)
                dve_take(dve, i, 0)
                dve_activate(dve, i)

            overflow(dve, further)

            dve.wait_ge(s["combined"], E)
            for t in range(NT):
                for n in range(2):
                    v = h[:, t, n * HALF:(n + 1) * HALF]
                    last = nc.vector.tensor_tensor(v, v, acc_bank[t][n][:, :], ALU.add)
                last.then_inc(s["tail_h"], 1)
            for t in range(NT):
                mean_square(t, t + 1, 2 * NT + t + 1)
            for t in range(NT):
                normalise(t, 3 + t)
            for g in range(4):
                take_turned(g, g_ple, 9 + g)
            for t in range(NT):
                dve.wait_ge(s["tail_sig"], t + 1)
                nc.vector.tensor_tensor(tok_tmp2[:, t, :], tok_tmp2[:, t, :], ple_v[:, t, :],
                                        ALU.mult).then_inc(s["tail_step"], 1)
                dve.wait_ge(s["tail_step"], 2 * t + 1)
                nc.vector.tensor_tensor(h[:, t, :], h[:, t, :], tok_tmp2[:, t, :], ALU.add).then_inc(s["tail_step"], 1)
                mean_square(t, t + 1, 3 * NT + t + 1)
                dve.wait_ge(s["rstd"], 3 + NT + t)
                dve.wait_ge(final_dma, 16)
                nc.vector.scalar_tensor_tensor(out=tok_tmp[:, t, :], in0=h[:, t, :], scalar=stat[:, 4 + t:5 + t],
                                               in1=g_final, op0=ALU.mult, op1=ALU.mult).then_inc(s["out_ready"], 1)


_INS = ["x", "p", "norm_mix", "w_in", "b_forget", "w_attn_out", "conv_w", "conv_b", "conv_ln_g", "conv_ln_b",
        "w_conv_out", "w_o", "norm_ffn", "w_router", "b_router", "w_gate", "b_gate", "w_up", "b_up",
        "w_down", "b_down", "norm_ple", "w_ple_gate", "w_ple_proj", "norm_final"]


def kernel(**inputs):
    import numpy as _np
    import concourse.bacc as _bacc
    from concourse.bass_utils import run_bass_kernel_spmd as _run

    nc = _bacc.Bacc("TRN2", target_bir_lowering=False, num_devices=1)
    arrays, args = {}, []
    for name in _INS:
        a = _np.ascontiguousarray(inputs[name])
        arrays[f"in_{name}"] = a
        args.append(nc.dram_tensor(f"in_{name}", a.shape, mybir.dt.from_np(a.dtype), kind="ExternalInput").ap())
    shape = tuple(inputs["x"].shape)
    args.append(nc.dram_tensor("out_block", shape, F32, kind="ExternalOutput").ap())
    build_block(nc, *args)
    return _run(nc, [arrays], core_ids=[0]).results[0]["out_block"]
```

```python
from contextlib import ExitStack

import concourse.bass as bass
from concourse import mybir

F32 = mybir.dt.float32
BF16 = mybir.dt.bfloat16
I32 = mybir.dt.int32
ALU = mybir.AluOpType
ACT = mybir.ActivationFunctionType
AX_X = mybir.AxisListType.X

P = 128
NEG_INF = -1e30
RMS_EPS = 1e-6
LN_EPS = 1e-5
SWIGLU_LIMIT = 7.0
SWIGLU_ALPHA = 1.702


def build_block(nc, x, p, norm_mix, w_in, b_forget, w_attn_out, conv_w, conv_b, conv_ln_g, conv_ln_b,
                w_conv_out, w_o, norm_ffn, w_router, b_router, w_gate, b_gate, w_up, b_up,
                w_down, b_down, norm_ple, w_ple_gate, w_ple_proj, norm_final, out):
    _, T, D = x.shape
    E = w_router.shape[2]
    H = b_forget.shape[1]
    AW = w_attn_out.shape[1]
    CW = w_conv_out.shape[1]
    TAPS = conv_w.shape[1]
    PLE = w_ple_proj.shape[1]
    HD = AW // H
    NT, KD, KA, KP = T // P, D // P, AW // P, PLE // P
    HALF = D // 2
    SCALE = float(HD) ** -0.5
    SLOTS = 64
    CHUNKS = T // SLOTS
    BLK = 256
    RING = 12
    PER_MAT = RING // 3
    assert (NT, KD, KA, KP, E, H, HD) == (2, 8, 4, 2, 32, 8, 64) and w_gate.shape[3] == D and CW == AW

    col_q, col_k, col_v, col_f = 0, AW, 2 * AW, 3 * AW
    col_ca = col_f + H
    col_cg = col_ca + CW
    col_ga = col_cg + CW
    col_gc = col_ga + D
    BLOCKS = [("ca", 0), ("cg", 0), ("ca", 1), ("cg", 1), ("q", 0), ("k", 0), ("q", 1), ("k", 1), ("v", 0), ("v", 1)]
    FIRST_GATE = len(BLOCKS)
    BLOCKS += [("ga", b) for b in range(4)] + [("gc", b) for b in range(4)]
    NB = len(BLOCKS)
    COL0 = {"q": col_q, "k": col_k, "v": col_v, "ca": col_ca, "cg": col_cg, "ga": col_ga, "gc": col_gc}
    AO_SLOT, CO_SLOT = NB % RING, (NB + 2) % RING
    assert AO_SLOT == 6 and CO_SLOT == 8

    with ExitStack() as ctx:
        def sb(name, shape, dt):
            return ctx.enter_context(nc.sbuf_tensor(name, shape, dt))

        def sem(name):
            return ctx.enter_context(nc.semaphore(name))

        ring = sb("ring", [P, RING, 2048], F32)
        wide = sb("wide", [P, 8192], F32)
        reg_a = sb("reg_a", [P, 3072], F32)
        reg_b = sb("reg_b", [P, 2048], F32)
        reg_c = sb("reg_c", [P, 1024], F32)
        reg_d = sb("reg_d", [P, 2176], F32)
        reg_e = sb("reg_e", [P, 4096], F32)
        reg_f = sb("reg_f", [P, 1536], F32)
        h = sb("h", [P, NT, D], F32)
        hnT = sb("hnT", [P, KD, T], F32)

        def view(reg, lo, hi, spec, **kw):
            return reg[:, lo:hi].rearrange(spec, **kw)

        w_o_sb = view(wide, 0, 8192, "p (k n) -> p k n", k=KD)
        x_parts = wide[:, 0:3072].bitcast(BF16).rearrange("p (t s d) -> p t s d", t=NT, s=3)
        xT = view(wide, 3072, 3584, "p (k s) -> p k s", k=KD)
        g_clip = wide[:, 3584:4096]
        g_sig = wide[:, 4096:4608]
        u_clip = wide[:, 4608:5120]
        hT = view(wide, 5120, 5632, "p (j s) -> p j s", j=4)
        y_sb = wide[:, 5632:6144]
        selT = view(wide, 6144, 6656, "p (b t) -> p b t", b=2)
        h_act = wide[:, 6656:7168]
        g_final = wide[:, 7168:8192]

        qT = view(reg_a, 0, 1024, "p (j t) -> p j t", j=KA)
        kT = view(reg_a, 1024, 2048, "p (j t) -> p j t", j=KA)
        v_sb = view(reg_a, 2048, 3072, "p (t c) -> p t c", t=NT)
        ln_out = view(reg_a, 1024, 2048, "p (t c) -> p t c", t=NT)
        b_down_sb = reg_a[0:E, 0:1024]
        gatesT = reg_a[0:E, 1024:1280]
        bias3 = reg_a[0:3 * E, 2048:3072].bitcast(BF16)

        glu_sig = view(reg_b, 0, 512, "p (j t) -> p j t", j=2)
        f_tmp = reg_b[0:H, 512:2048].rearrange("p (n t) -> p n t", n=6)
        probs = view(reg_b, 0, 1024, "p (b h k) -> p b h k", b=2, h=2)
        probsT = view(reg_b, 1024, 2048, "p (b j q) -> p b j q", b=2, j=4)
        ple_v = view(reg_b, 0, 2048, "p (t d) -> p t d", t=NT)

        taps_in = reg_c[0:TAPS, 0:CW]
        attnT = view(reg_c, 0, 1024, "p (j t) -> p j t", j=KA)
        p_sb = view(reg_c, 0, 512, "p (t d) -> p t d", t=NT)
        pT = view(reg_c, 512, 1024, "p (k t) -> p k t", k=KP)

        PAD = TAPS - 1
        ZW = PAD + T
        z_pad = view(reg_d, 0, 4 * ZW, "p (j t) -> p j t", j=4)
        conv = view(reg_d, 4 * ZW, 4 * ZW + 1024, "p (j t) -> p j t", j=4)
        silu_sig = view(reg_d, 0, 1024, "p (j t) -> p j t", j=4)
        bias_in = reg_d[0:3 * E, 0:2048]

        sig_a = view(reg_e, 0, 2048, "p (j t) -> p j t", j=KD)
        sig_c = view(reg_e, 2048, 4096, "p (j t) -> p j t", j=KD)
        w_proj_sb = view(reg_e, 2048, 4096, "p (k n) -> p k n", k=KP)
        tok_tmp = view(reg_e, 0, 2048, "p (t d) -> p t d", t=NT)
        tok_tmp2 = view(reg_e, 2048, 4096, "p (t d) -> p t d", t=NT)

        rows_in = [tok_tmp[:, t, :] for t in range(NT)]
        rows_ffn = [reg_a[:, 1024:2048], tok_tmp[:, 1, :]]

        cum_base = reg_f[:, 0:256]
        cum_key = reg_f[:, 256:512]
        cum_q = view(reg_f, 512, 1536, "p (b h t) -> p b h t", b=2, h=2)

        ident = sb("ident", [P, P], F32)
        ident_b = sb("ident_b", [P, P], BF16)
        causal_b = sb("causal_b", [P, P], BF16)
        before_b = sb("before_b", [P, P], BF16)
        ones_b = sb("ones_b", [P, P], BF16)
        ones_r = sb("ones_r", [1, P], F32)
        head_hot = sb("head_hot", [P, H], F32)
        params_in = sb("params_in", [36, P], F32)
        params = sb("params", [P, 36 + 4 * TAPS], F32)
        w_f = sb("w_f", [P, KD, H], F32)
        b_f = sb("b_f", [H, 1], F32)
        w_router_sb = sb("w_router_sb", [P, KD, E], F32)
        b_router_sb = sb("b_router_sb", [1, E], F32)
        slot_id = sb("slot_id", [P, CHUNKS, 2, SLOTS], BF16)
        expert_hot = sb("expert_hot", [3 * E, E], F32)
        hot = sb("hot", [3 * E, 2, SLOTS], BF16)
        sel = sb("sel", [P, 2, NT, 2, SLOTS], BF16)
        ranks = sb("ranks", [P, NT, E], F32)
        gates3 = sb("gates3", [P, NT, E, 3], BF16)
        gate_slot = sb("gate_slot", [P, 2], F32)
        gate_parts = sb("gate_parts", [P, 3], F32)
        stat = sb("stat", [P, 32], F32)
        mhalf = sb("mhalf", [P, 2], F32)
        sm_stat = sb("sm_stat", [P, 2, 6], F32)
        top8 = sb("top8", [P, NT, 8], F32)
        flag = sb("flag", [1, 1], I32)
        flag_f = sb("flag_f", [1, 1], F32)
        g_mix, g_ffn, g_ple = params[:, 0:8], params[:, 8:16], params[:, 16:24]
        cb, lg, lb = params[:, 24:28], params[:, 28:32], params[:, 32:36]


        ones_e, above, ties, tie_no, gate_w, rest = (
            view(reg_f, n * NT * E, (n + 1) * NT * E, "p (t e) -> p t e", t=NT) for n in range(6))
        routed = sb("routed", [P, NT, E], BF16)

        def tap(j, m):
            return params[:, 36 + m * TAPS + j:37 + m * TAPS + j]

        bank = [ctx.enter_context(nc.psum_tensor(f"bank{i}", [P, HALF], F32)) for i in range(8)]
        acc_bank = [[bank[0], bank[1]], [bank[2], bank[3]]]
        bank_g, bank_u, bank_y, bank_x = bank[4:8]

        params_dma, forget_dma, wo_dma, p_dma, proj_dma = [sem(n) for n in (
            "params_dma", "forget_dma", "wo_dma", "p_dma", "proj_dma")]
        bias_dma, bdown_dma, final_dma, router_dma, out_dma = [sem(n) for n in (
            "bias_dma", "bdown_dma", "final_dma", "router_dma", "out_dma")]
        block_dma = [sem(f"block_dma{n}") for n in range(NB)]
        x_dma = [sem(f"x_dma{t}") for t in range(NT)]
        ao_dma, co_dma = sem("ao_dma"), sem("co_dma")
        chunk_dma = [sem(f"chunk_dma{n}") for n in range(RING)]
        pgate_dma = [sem(f"pgate_dma{n}") for n in range(PER_MAT)]
        names = """consts params_turned params_ready sumsq mean_sq rstd normed x_turned hnT_ready
            block_done block_out forget_done f_neg f_exp f_ln f_steps cum_steps cum_q_ready glu_ready z_ready
            conv_step head_scored scores_done row_max probs_exp probs_norm rows_recip probs_turned probsT_ready pv_done attn_ready
            conv_turned ln_step ln_pow ln_ready ln_back silu_arg silu_ready gates_sig
            branch_a branch_c merge_step merged wo_done h_mid
            pple_turned pT_ready proj_done ple_ready part_step part_a part_b
            logits_done routed_ready gates3_ready route_step rank_done ranks_ready route_exp gatesT_done gatesT_ready counts_done flag_ready
            bias_part bias_part_a bias_ready bdown_done parts_ready
            sel_ready gathered xT_ready gslot_ready selT_ready gclip_ready gsig_ready gglu uclip h_ready
            turned hT_ready y_ready combined chunk_used
            tile_combined tail_h tail_pg tail_sig tail_step tail_row tail_sq tail_gain tail_mean out_ready last_ready""".split()
        s = {n: sem(n) for n in names}

        def bcast(ap, n):
            return ap.unsqueeze(len(ap.shape)).broadcast_to(list(ap.shape) + [n])

        N_CONST = 21
        N_PARAM = 7
        w_in_k = w_in[0].rearrange("(k p) n -> p k n", p=P)
        mats = [w_gate, w_up, w_down]
        ROWS = D // PER_MAT


        def load_chunks(sp, i, e):
            for c in range(RING):
                if not isinstance(i, int) or i > 0:
                    sp.wait_ge(s["chunk_used"], (i - 1) * RING + (c + 1))
                rows = mats[c // PER_MAT][0, e, (c % PER_MAT) * ROWS:(c % PER_MAT + 1) * ROWS, :]
                sp.dma_start(ring[:, c, :].rearrange("p (k n) -> p k n", n=D),
                             rows.rearrange("(k p) n -> p k n", p=P)).then_inc(chunk_dma[c], 16)

        def pe_gather(pe, i, b):
            pe.wait_ge(s["sel_ready"], i + 1)
            for k in range(KD):
                for n in range(3 * NT):
                    t, part = n // 3, n % 3
                    nc.tensor.matmul(bank_x[:, k * SLOTS:(k + 1) * SLOTS], x_parts[:, t, part, k * P:(k + 1) * P],
                                     sel[:, b, t, 0, :], start=n == 0, stop=n == 3 * NT - 1)
            for t in range(NT):
                nc.tensor.transpose(bank_y[:, t * 64:(t + 1) * 64].bitcast(BF16),
                                    sel[:, b, t].rearrange("p a s -> p (a s)"), ident_b[:])

        def pe_gather_gates(i, e, b):
            for t in range(NT):
                last = nc.tensor.matmul(bank_y[:, 256:259], sel[:, b, t].rearrange("p a s -> p (a s)"),
                                        gates3[:, t, e, :], start=t == 0, stop=t == NT - 1)
            last.then_inc(s["gathered"], 1)

        def pe_expand(pe, i, b, which):
            dst = bank_u if which else bank_g
            for n in range(2):
                nc.tensor.matmul(dst[n * 64:(n + 1) * 64, :], hot[:, b, :],
                                 bias3[:, which * D + n * HALF:which * D + (n + 1) * HALF], start=True, stop=False)
            for c in range(PER_MAT):
                slot = which * PER_MAT + c
                pe.wait_ge(chunk_dma[slot], (i + 1) * 16)
                for kk in range(2):
                    for n in range(2):
                        last = nc.tensor.matmul(dst[n * 64:(n + 1) * 64, :], xT[:, 2 * c + kk, :],
                                                ring[:, slot, kk * D + n * HALF:kk * D + (n + 1) * HALF],
                                                start=False, stop=c == PER_MAT - 1 and kk == 1)
                last.then_inc(s["chunk_used"], 1)

        def pe_gate(pe, i, b):
            pe.wait_ge(s["xT_ready"], i + 1)
            pe_expand(pe, i, b, 0)

        def pe_up(pe, i, b):
            pe_expand(pe, i, b, 1)

        def pe_turn(pe, i):
            pe.wait_ge(s["h_ready"], i + 1)
            for j in range(4):
                last = nc.tensor.transpose(bank_u[:, j * P:(j + 1) * P], h_act[:, j * P:(j + 1) * P], ident[:])
            last.then_inc(s["turned"], 1)

        def pe_down(pe, i, prepared):
            pe.wait_ge(s["hT_ready"], i + 1)
            pe.wait_ge(s["selT_ready"], prepared)
            pe.wait_ge(s["gslot_ready"], prepared)
            for c in range(PER_MAT):
                slot = 2 * PER_MAT + c
                pe.wait_ge(chunk_dma[slot], (i + 1) * 16)
                for kk in range(2):
                    k = 2 * c + kk
                    for n in range(2):
                        last = nc.tensor.matmul(bank_y[n * 64:(n + 1) * 64, :],
                                                hT[:, k % 4, (k // 4) * 64:(k // 4 + 1) * 64],
                                                ring[:, slot, kk * D + n * HALF:kk * D + (n + 1) * HALF],
                                                start=k == 0, stop=k == KD - 1)
                last.then_inc(s["chunk_used"], 1)

        def pe_combine(pe, i, b, first_tile=None):
            pe.wait_ge(s["y_ready"], i + 1)
            for t in range(NT):
                for n in range(2):
                    last = nc.tensor.matmul(acc_bank[t][n][:, :], selT[n * 64:(n + 1) * 64, b, t * P:(t + 1) * P],
                                            y_sb[n * 64:(n + 1) * 64, :], start=False, stop=True,
                                            skip_group_check=True)
                if t == 0 and first_tile:
                    last.then_inc(s[first_tile], 1)
            last.then_inc(s["combined"], 1)

        def dve_select(dve, i, e, b, chunk, back):
            if not isinstance(i, int) or i >= back:
                dve.wait_ge(s["gathered"], i - (back - 1))
                dve.wait_ge(s["chunk_used"], (i - back) * RING + 2 * PER_MAT)
            nc.vector.tensor_scalar(hot[:, b, :], expert_hot[:, bass.ds(e, 1)].broadcast_to([3 * E, SLOTS]), 1.0, None,
                                    ALU.mult)
            for t in range(NT):
                last = nc.vector.tensor_scalar(sel[:, b, t].rearrange("p a s -> p (a s)"),
                                               slot_id[:, chunk].rearrange("p a s -> p (a s)"),
                                               ranks[:, t, bass.ds(e, 1)], None, ALU.is_equal)
            last.then_inc(s["sel_ready"], 1)

        def dve_take(dve, i, b):
            dve.wait_ge(s["gathered"], i + 1)
            nc.vector.tensor_tensor(xT, bank_x[:, :].rearrange("p (k s) -> p k s", k=KD), bcast(g_ffn, SLOTS),
                                    ALU.mult).then_inc(s["xT_ready"], 1)

        def dve_activate(dve, i):
            dve.wait_ge(s["chunk_used"], i * RING + PER_MAT)
            nc.vector.tensor_scalar(g_clip, bank_g[:, :], SWIGLU_LIMIT, None, ALU.min).then_inc(s["gclip_ready"], 1)
            dve.wait_ge(s["gsig_ready"], i + 1)
            nc.vector.tensor_tensor(g_clip, g_clip, g_sig, ALU.mult).then_inc(s["gglu"], 1)
            dve.wait_ge(s["chunk_used"], i * RING + 2 * PER_MAT)
            nc.vector.tensor_scalar(u_clip, bank_u[:, :], SWIGLU_LIMIT, -SWIGLU_LIMIT, ALU.min,
                                    ALU.max).then_inc(s["uclip"], 1)
            dve.wait_ge(s["uclip"], i + 1)
            dve.wait_ge(s["gglu"], i + 1)
            nc.vector.scalar_tensor_tensor(out=h_act, in0=u_clip, scalar=1.0, in1=g_clip, op0=ALU.add,
                                           op1=ALU.mult).then_inc(s["h_ready"], 1)

        def act_sigmoid(act, i):
            act.wait_ge(s["gclip_ready"], i + 1)
            nc.scalar.activation(g_sig, g_clip, ACT.Sigmoid, scale=SWIGLU_ALPHA).then_inc(s["gsig_ready"], 1)

        def act_selT(act, i, b):
            act.wait_ge(s["gathered"], i + 1)
            nc.scalar.activation(selT[:, b, :], bank_y[:, 0:P].bitcast(BF16), ACT.Copy).then_inc(s["selT_ready"], 1)
            nc.scalar.activation(gate_parts[:], bank_y[:, 256:259], ACT.Copy,
                                 accum_out=gate_slot[:, b:b + 1]).then_inc(s["gslot_ready"], 1)

        def act_hT(act, i):
            act.wait_ge(s["turned"], i + 1)
            nc.scalar.activation(hT.rearrange("p j s -> p (j s)"), bank_u[:, :], ACT.Copy).then_inc(s["hT_ready"], 1)

        def act_y(act, i, b):
            act.wait_ge(s["chunk_used"], (i + 1) * RING)
            act.wait_ge(s["gslot_ready"], i + 1)
            nc.scalar.activation(y_sb, bank_y[:, :], ACT.Copy, scale=gate_slot[:, b:b + 1]).then_inc(s["y_ready"], 1)

        def take_attention(dve, u):
            dve.wait_ge(s["pv_done"], u + 1)
            nc.vector.tensor_copy(attnT[:, u // 2, (u % 2) * P:(u % 2 + 1) * P],
                                  bank[7][:, 0:P]).then_inc(s["attn_ready"], 1)

        def over_passes(eng, first, body, last):
            first()
            body(0, 0, 0)
            with eng.Fori(0, E // 2 - 1) as pair:
                body(pair * 2 + 1, pair * 2 + 1, 1)
                body(pair * 2 + 2, pair * 2 + 2, 0)
            last()

        def overflow(eng, body, end=None):
            eng.wait_ge(s["flag_ready"], 1)
            n = eng.value_load(flag[0:1, 0:1], min_val=0, max_val=T)
            with eng.If(n > SLOTS):
                with eng.Fori(0, E) as e:
                    for chunk in range(1, CHUNKS):
                        body(e * (CHUNKS - 1) + (E + chunk - 1), e, chunk)
                if end:
                    end()
            with eng.Else():
                pass

        block = ctx.enter_context(nc.Block())

        @block.sync
        def _(sp):
            row = 0
            for v, n in ((norm_mix, KD), (norm_ffn, KD), (norm_ple, KD), (conv_b, 4), (conv_ln_g, 4), (conv_ln_b, 4)):
                sp.dma_start(params_in[row:row + n, :], v[0].rearrange("(c p) -> c p", p=P)).then_inc(params_dma, 16)
                row += n
            sp.dma_start(taps_in, conv_w[0]).then_inc(params_dma, 16)

            def load_block(n):
                kind, b = BLOCKS[n]
                c0 = COL0[kind] + b * BLK
                if n >= RING:
                    sp.wait_ge(s["block_done"], n - RING + 1)
                sp.dma_start(ring[:, n % RING, :].rearrange("p (k c) -> p k c", k=KD),
                             w_in_k[:, :, c0:c0 + BLK]).then_inc(block_dma[n], 16)

            for n in range(RING):
                load_block(n)
                if n == 1:
                    sp.dma_start(w_f[:], w_in_k[:, :, col_f:col_f + H]).then_inc(forget_dma, 16)
                    sp.dma_start(b_f[:], b_forget[0].rearrange("(h a) -> h a", a=1)).then_inc(forget_dma, 16)
            sp.dma_start(w_router_sb[:], w_router[0].rearrange("(k p) e -> p k e", p=P)).then_inc(router_dma, 16)
            sp.dma_start(b_router_sb[:], b_router).then_inc(router_dma, 16)
            sp.dma_start(w_o_sb, w_o[0].rearrange("(k p) n -> p k n", p=P)).then_inc(wo_dma, 16)
            for n in range(RING, NB):
                load_block(n)
            for slot, src, got in ((AO_SLOT, w_attn_out, ao_dma), (CO_SLOT, w_conv_out, co_dma)):
                sp.wait_ge(s["block_done"], slot + 2)
                sp.dma_start(ring[:, slot:slot + 2, :].rearrange("p s (k n) -> p (s k) n", n=D),
                             src[0].rearrange("(k p) n -> p k n", p=P)).then_inc(got, 16)
            for c in range(RING):
                if c < AO_SLOT:
                    sp.wait_ge(s["block_done"], RING + c + 1)
                elif c < CO_SLOT:
                    sp.wait_ge(s["branch_a"], 1)
                elif c < CO_SLOT + 2:
                    sp.wait_ge(s["branch_c"], 4)
                if c == AO_SLOT:
                    sp.dma_start(p_sb, p[0, 0].rearrange("(t p) d -> p t d", p=P)).then_inc(p_dma, 16)
                    sp.dma_start(b_down_sb, b_down[0]).then_inc(bdown_dma, 16)
                if c == CO_SLOT:
                    for part in range(3):
                        for m, bias in enumerate((b_gate, b_up)):
                            sp.dma_start(bias_in[part * E:(part + 1) * E, m * D:(m + 1) * D],
                                         bias[0]).then_inc(bias_dma, 16)
                    sp.wait_ge(s["merged"], 4)
                    sp.dma_start(w_proj_sb, w_ple_proj[0].rearrange("(k p) n -> p k n", p=P)).then_inc(proj_dma, 16)
                rows = mats[c // PER_MAT][0, 0, (c % PER_MAT) * ROWS:(c % PER_MAT + 1) * ROWS, :]
                sp.dma_start(ring[:, c, :].rearrange("p (k n) -> p k n", n=D),
                             rows.rearrange("(k p) n -> p k n", p=P)).then_inc(chunk_dma[c], 16)
            sp.wait_ge(s["wo_done"], NT)
            sp.dma_start(g_final, norm_final.rearrange("(a d) -> a d", a=1).partition_broadcast(P)
                         ).then_inc(final_dma, 16)
            with sp.Fori(1, E) as i:
                load_chunks(sp, i, i)
            overflow(sp, lambda i, e, chunk: load_chunks(sp, i, e),
                     lambda: sp.wait_ge(s["chunk_used"], E * CHUNKS * RING))
            for c in range(PER_MAT):
                sp.wait_ge(s["chunk_used"], (E - 1) * RING + c + 1)
                sp.dma_start(ring[:, c, :].rearrange("p (k n) -> p k n", n=D),
                             w_ple_gate[0, c * ROWS:(c + 1) * ROWS, :].rearrange("(k p) n -> p k n", p=P)
                             ).then_inc(pgate_dma[c], 16)
            sp.wait_ge(s["out_ready"], 2)
            sp.dma_start(out[0, 0:P, :], tok_tmp[:, 0, :]).then_inc(out_dma, 16)
            for n, done, count in ((0, "out_ready", 3), (1, "last_ready", 1)):
                sp.wait_ge(s[done], count)
                half = slice(n * HALF, (n + 1) * HALF)
                sp.dma_start(out[0, P:T, half], tok_tmp[:, 1, half]).then_inc(out_dma, 16)
            sp.wait_ge(out_dma, 16 * 3)

        @block.gpsimd
        def _(pool):
            n = [0]

            def const(ins):
                n[0] += 1
                ins.then_inc(s["consts"], 1)
                pool.wait_ge(s["consts"], n[0])

            def masked(t, op, fill, base, pattern, mult):
                const(nc.gpsimd.affine_select(out=t, in_=t, compare_op=op, fill=fill, base=base, pattern=pattern,
                                              channel_multiplier=mult))

            const(nc.gpsimd.memset(mhalf[:], -0.5))
            for t in (ident, ident_b):
                const(nc.gpsimd.memset(t[:], 0.0))
                masked(t[:], ALU.not_equal, 1.0, 0, [[-1, P]], 1)
            def power(ready, count, out, in_, done):
                pool.wait_ge(s[ready], count)
                nc.gpsimd.tensor_tensor(out, in_, mhalf[:, 0:out.shape[1]], ALU.pow).then_inc(s[done], 1)

            def power_rows(norm):
                for t in range(NT):
                    power("mean_sq", norm * NT + t + 1, stat[:, 4 + t:5 + t], stat[:, 2 + t:3 + t], "rstd")

            power_rows(0)
            const(nc.gpsimd.memset(ones_b[:], 1.0))
            const(nc.gpsimd.memset(ones_r[:], 1.0))
            const(nc.gpsimd.memset(z_pad[:, :, 0:PAD], 0.0))
            const(nc.gpsimd.memset(head_hot[:], 0.0))
            masked(head_hot[:], ALU.not_equal, 1.0, 0, [[-1, H]], 1)
            masked(head_hot[:], ALU.not_equal, 1.0, -32, [[-1, H]], 1)
            const(nc.gpsimd.memset(causal_b[:], 0.0))
            masked(causal_b[:], ALU.is_ge, NEG_INF, 0, [[-1, P]], 1)
            const(nc.gpsimd.memset(before_b[:], 1.0))
            masked(before_b[:], ALU.is_gt, 0.0, 0, [[1, P]], -1)
            const(nc.gpsimd.iota(slot_id[:].rearrange("p c a s -> p (c a s)"),
                                 pattern=[[SLOTS, CHUNKS], [0, 2], [1, SLOTS]], base=0, channel_multiplier=0,
                                 allow_small_or_imprecise_dtypes=True))
            const(nc.gpsimd.memset(expert_hot[:], 0.0))
            for part in range(3):
                masked(expert_hot[:], ALU.not_equal, 1.0, -part * E, [[-1, E]], 1)
            const(nc.gpsimd.memset(reg_f[:, 0:512], 0.0))
            assert n[0] == N_CONST, n[0]

            power("ln_step", 4, stat[:, 28:30], stat[:, 26:28], "ln_pow")
            for norm in range(1, 4):
                power_rows(norm)

        @block.tensor
        def _(pe):
            pe.wait_ge(s["consts"], 3)
            pe.wait_ge(params_dma, 16 * N_PARAM)
            nc.tensor.transpose(bank[0][:, 0:36], params_in[:], ident[0:36, 0:36])
            for m in range(4):
                last = nc.tensor.transpose(bank[0][:, 36 + m * TAPS:36 + (m + 1) * TAPS],
                                           taps_in[:, m * P:(m + 1) * P], ident[0:TAPS, 0:TAPS])
            last.then_inc(s["params_turned"], 1)

            def turn_tokens(src, first_bank, ready, first_count, done, tiles=range(NT)):
                for g in (2 * t + half for t in tiles for half in range(2)):
                    t = g // 2
                    pe.wait_ge(s[ready], first_count + t)
                    for c in range(4):
                        k = (g % 2) * 4 + c
                        last = nc.tensor.transpose(bank[first_bank + g][:, c * P:(c + 1) * P],
                                                   src[t][:, k * P:(k + 1) * P], ident[:])
                    last.then_inc(s[done], 1)

            turn_tokens(rows_in, 4, "normed", 1, "x_turned")

            def project(n):
                kind, _ = BLOCKS[n]
                dst = bank[n % 2]
                pe.wait_ge(block_dma[n], 16)
                if n >= 2:
                    pe.wait_ge(s["block_out"], n - 1)
                else:
                    pe.wait_ge(s["params_ready"], 1)
                w = ring[:, n % RING, :].rearrange("p (k c) -> p k c", k=KD)
                for j in range(2):
                    for k in range(KD):
                        a, b = w[:, k, j * P:(j + 1) * P], hnT[:, k, :]
                        if kind == "v":
                            a, b = hnT[:, k, j * P:(j + 1) * P], w[:, k, :]
                        last = nc.tensor.matmul(dst[:, j * BLK:(j + 1) * BLK], a, b, start=k == 0, stop=k == KD - 1)
                last.then_inc(s["block_done"], 1)

            pe.wait_ge(s["hnT_ready"], 4)
            for n in range(4):
                project(n)
            pe.wait_ge(forget_dma, 16 * 2)
            for k in range(KD):
                last = nc.tensor.matmul(bank[2][0:H, 0:T], w_f[:, k, :], hnT[:, k, :], start=k == 0, stop=k == KD - 1)
            last.then_inc(s["forget_done"], 1)
            for n in range(4, FIRST_GATE):
                project(n)

            def scores(u, hh):
                hp, qb = u // 2, u % 2
                dst = bank[4 + u % 2]
                nk = (qb + 1) * P
                if hh:
                    pe.wait_ge(s["head_scored"], u + 1)
                else:
                    pe.wait_ge(s["cum_q_ready"], hp + 1)
                    if u == 0:
                        pe.wait_ge(s["block_out"], FIRST_GATE)
                    if u >= 2:
                        pe.wait_ge(s["probs_exp"], 2 * (u - 1))
                row = slice(hh * HD, (hh + 1) * HD)
                o = dst[:, hh * 256:hh * 256 + nk]
                nc.tensor.matmul(o, qT[row, hp, qb * P:(qb + 1) * P], kT[row, hp, 0:nk], start=True, stop=False)
                nc.tensor.matmul(o, cum_q[:, hp % 2, hh, qb * P:(qb + 1) * P], cum_key[:, 0:nk],
                                 start=False, stop=False)
                nc.tensor.matmul(dst[:, hh * 256 + qb * P:hh * 256 + nk], ident_b[:], causal_b[:], start=False,
                                 stop=True).then_inc(s["scores_done" if hh else "head_scored"], 1)

            def turn_probs(u):
                qb = u % 2
                pe.wait_ge(s["probs_norm"], u + 1)
                if u >= 1:
                    pe.wait_ge(s["probsT_ready"], u)
                for hh in range(2):
                    for kb in range(qb + 1):
                        last = nc.tensor.transpose(bank[6][:, (2 * hh + kb) * P:(2 * hh + kb + 1) * P],
                                                   probs[:, u % 2, hh, kb * P:(kb + 1) * P], ident[:])
                last.then_inc(s["probs_turned"], 1)

            def attend(u):
                hp, qb = u // 2, u % 2
                pe.wait_ge(s["probsT_ready"], u + 1)
                if u >= 1:
                    pe.wait_ge(s["attn_ready"], u)
                for kb in range(qb + 1):
                    for hh in range(2):
                        last = nc.tensor.matmul(bank[7][hh * HD:(hh + 1) * HD, 0:P],
                                                v_sb[:, kb, hp * P + hh * HD:hp * P + (hh + 1) * HD],
                                                probsT[:, u % 2, 2 * hh + kb, :], start=kb == 0, stop=kb == qb)
                last.then_inc(s["pv_done"], 1)

            def conv_to_tokens():
                pe.wait_ge(s["conv_step"], 4 * TAPS)
                for t in range(NT):
                    for m in range(4):
                        last = nc.tensor.transpose(bank[2 + t][:, m * P:(m + 1) * P], conv[:, m, t * P:(t + 1) * P],
                                                   ident[:])
                    last.then_inc(s["conv_turned"], 1)

            def conv_to_channels():
                pe.wait_ge(s["ln_ready"], 2)
                for m in range(4):
                    for t in range(NT):
                        last = nc.tensor.transpose(bank[2 + m // 2][:, (m % 2) * T + t * P:(m % 2) * T + (t + 1) * P],
                                                   ln_out[:, t, m * P:(m + 1) * P], ident[:])
                    if m % 2:
                        last.then_inc(s["ln_back"], 1)

            scores(0, 0)
            scores(0, 1)
            for u in range(8):
                project(FIRST_GATE + u)
                if u < 7:
                    scores(u + 1, 0)
                turn_probs(u)
                if u < 7:
                    scores(u + 1, 1)
                if u >= 1:
                    attend(u - 1)
                if u == 5:
                    conv_to_tokens()
            conv_to_channels()
            attend(7)

            def branch(first_bank, slot, src, got, ready, count, done):
                pe.wait_ge(got, 16)
                pe.wait_ge(s[ready], count)
                w = ring[:, slot:slot + 2, :].rearrange("p s (k n) -> p (s k) n", n=D)
                for m in range(KD):
                    for k in range(KA):
                        last = nc.tensor.matmul(bank[first_bank + m // 2][:, (m % 2) * T:(m % 2 + 1) * T],
                                                w[:, k, m * P:(m + 1) * P], src[:, k, :], start=k == 0,
                                                stop=k == KA - 1)
                    if m % 2 and done == "branch_c":
                        last.then_inc(s[done], 1)
                if done == "branch_a":
                    last.then_inc(s[done], 1)

            branch(4, AO_SLOT, attnT, ao_dma, "attn_ready", 8, "branch_a")
            pe.wait_ge(s["block_out"], NB)
            branch(0, CO_SLOT, conv, co_dma, "silu_ready", 1, "branch_c")
            pe.wait_ge(wo_dma, 16)
            pe.wait_ge(s["merge_step"], 4)

            def project_out(t, pairs):
                for d in pairs:
                    pe.wait_ge(s["merged"], d + 1)
                    for k in (2 * d, 2 * d + 1):
                        for n in range(2):
                            last = nc.tensor.matmul(bank[4 + 2 * t + n][:, :], sig_a[:, k, t * P:(t + 1) * P],
                                                    w_o_sb[:, k, n * HALF:(n + 1) * HALF], start=k == 0,
                                                    stop=k == KD - 1)
                return last

            def route_logits(t):
                pe.wait_ge(s["hnT_ready"], 6 + 2 * t)
                o = bank[t][:, 0:E]
                nc.tensor.matmul(o, ones_r[:], b_router_sb[:], start=True, stop=False)
                for k in range(KD):
                    last = nc.tensor.matmul(o, hnT[:, k, t * P:(t + 1) * P], w_router_sb[:, k, :],
                                            start=False, stop=k == KD - 1)
                last.then_inc(s["logits_done"], 1)

            def ple_project(t, first_bank):
                for n in range(2):
                    for k in range(KP):
                        last = nc.tensor.matmul(bank[first_bank + n][:, :], pT[:, k, t * P:(t + 1) * P],
                                                w_proj_sb[:, k, n * HALF:(n + 1) * HALF], start=k == 0,
                                                stop=k == KP - 1)
                last.then_inc(s["proj_done"], 1)

            project_out(0, range(4)).then_inc(s["wo_done"], 1)
            pe.wait_ge(p_dma, 16)
            for k in range(KP):
                for t in range(NT):
                    last = nc.tensor.transpose(bank[3][:, k * T + t * P:k * T + (t + 1) * P],
                                               p_sb[:, t, k * P:(k + 1) * P], ident[:])
            last.then_inc(s["pple_turned"], 1)
            project_out(1, range(2))
            turn_tokens(rows_ffn, 4, "normed", 1 + NT, "x_turned", (0,))
            project_out(1, range(2, 4)).then_inc(s["wo_done"], 1)
            pe.wait_ge(router_dma, 32)
            route_logits(0)
            pe.wait_ge(s["pT_ready"], 1)
            pe.wait_ge(proj_dma, 16)
            ple_project(0, 2)
            turn_tokens(rows_ffn, 4, "normed", 1 + NT, "x_turned", (1,))
            route_logits(1)
            ple_project(1, 4)
            pe.wait_ge(s["ple_ready"], 1)
            pe.wait_ge(s["routed_ready"], 2)
            nc.tensor.matmul(bank[2][:, 0:E], before_b[:], routed[:, 0, :], start=True, stop=True)
            nc.tensor.matmul(bank[2][:, E:2 * E], ones_b[:], routed[:, 0, :], start=True, stop=False)
            nc.tensor.matmul(bank[2][:, E:2 * E], before_b[:], routed[:, 1, :], start=False, stop=True)
            for t in range(NT):
                last = nc.tensor.matmul(bank[2][0:1, 2 * E:3 * E], ones_b[:, 0:1], routed[:, t, :], start=t == 0,
                                        stop=t == NT - 1)
            last.then_inc(s["rank_done"], 1)

            def gather(i, e, b):
                pe_gather(pe, i, b)
                pe_gather_gates(i, e, b)

            def first():
                pe.wait_ge(s["parts_ready"], 2)
                pe_gather(pe, 0, 0)
                pe.wait_ge(s["gates3_ready"], 1)
                pe_gather_gates(0, 0, 0)
                for t in range(NT):
                    last = nc.tensor.transpose(bank[3][0:E, t * P:(t + 1) * P], gate_w[:, t, :], ident[:])
                last.then_inc(s["gatesT_done"], 1)
                pe.wait_ge(s["bias_ready"], 1)
                pe.wait_ge(s["ple_ready"], 2)

            def start_sums():
                pe.wait_ge(s["gatesT_ready"], 1)
                pe.wait_ge(s["flag_ready"], 1)
                pe.wait_ge(bdown_dma, 16)
                for t in range(NT):
                    for n in range(2):
                        nc.tensor.matmul(acc_bank[t][n][:, :], gatesT[:, t * P:(t + 1) * P],
                                         b_down_sb[:, n * HALF:(n + 1) * HALF], start=True, stop=True)

            def one(i, e, b):
                pe_gate(pe, i, b)
                pe_up(pe, i, b)
                if isinstance(i, int) and i == 0:
                    start_sums()
                    pe.wait_ge(s["gslot_ready"], 1)
                else:
                    pe_combine(pe, i - 1, 1 - b)
                gather(i + 1, e + 1, 1 - b)
                pe_turn(pe, i)
                pe_down(pe, i, i + 2)

            def last_one():
                i, b = E - 1, 1
                pe_gate(pe, i, b)
                pe_up(pe, i, b)
                pe_combine(pe, i - 1, 0)
                pe_turn(pe, i)
                pe_down(pe, i, E)
                pe_combine(pe, i, b, "tile_combined")

            over_passes(pe, first, one, last_one)

            def further(i, e, chunk):
                gather(i, e, 0)
                pe_gate(pe, i, 0)
                pe_up(pe, i, 0)
                pe_turn(pe, i)
                pe_down(pe, i, i + 1)
                pe_combine(pe, i, 0)

            overflow(pe, further)

            def turn_tail(t):
                for half in range(2):
                    pe.wait_ge(s["tail_h"], 2 * t + half + 1)
                    for c in range(4):
                        k = half * 4 + c
                        last = nc.tensor.transpose(bank[4 + 2 * t + half][:, c * P:(c + 1) * P],
                                                   h[:, t, k * P:(k + 1) * P], ident[:])
                    last.then_inc(s["x_turned"], 1)

            def ple_gate(t, k, n):
                return nc.tensor.matmul(acc_bank[t][n][:, :], hnT[:, k, t * P:(t + 1) * P],
                                        ring[:, k // 2, (k % 2) * D + n * HALF:(k % 2) * D + (n + 1) * HALF],
                                        start=k == 0, stop=k == KD - 1)

            turn_tail(0)
            for k in range(KD):
                pe.wait_ge(pgate_dma[k // 2], 16)
                if k % 4 == 0:
                    pe.wait_ge(s["hnT_ready"], 9 + k // 4)
                if k == 4:
                    turn_tail(1)
                for n in range(2):
                    last = ple_gate(0, k, n)
            last.then_inc(s["tail_pg"], 1)
            for n in range(2):
                for k in range(KD):
                    if n == 0 and k % 4 == 0:
                        pe.wait_ge(s["hnT_ready"], 11 + k // 4)
                    last = ple_gate(1, k, n)
                last.then_inc(s["tail_pg"], 1)

        @block.scalar
        def _(act):
            for t in range(NT):
                act.dma_start(h[:, t, :], x[0, t * P:(t + 1) * P, :]).then_inc(x_dma[t], 16)

            def square(t, dump):
                nc.scalar.activation(dump, h[:, t, :], ACT.Square, accum_out=stat[:, t:t + 1]).then_inc(s["sumsq"], 1)

            for t in range(NT):
                act.wait_ge(x_dma[t], 16)
                square(t, tok_tmp[:, t, :])

            def read_out(n):
                kind, b = BLOCKS[n]
                act.wait_ge(s["block_done"], n + 1)
                src = bank[n % 2][:, :].rearrange("p (j t) -> p j t", j=2)
                if kind == "v":
                    dst = v_sb[:, :, b * BLK:(b + 1) * BLK]
                elif kind == "ca":
                    dst = z_pad[:, 2 * b:2 * b + 2, PAD:]
                elif kind == "cg":
                    dst = glu_sig
                else:
                    dst = {"q": qT, "k": kT, "ga": sig_a, "gc": sig_c}[kind][:, 2 * b:2 * b + 2, :]
                if kind == "cg" and b:
                    act.wait_ge(s["z_ready"], b)
                nc.scalar.activation(dst, src, ACT.Sigmoid if kind == "cg" else ACT.Copy).then_inc(s["block_out"], 1)

            for n in range(4):
                read_out(n)
            act.wait_ge(s["f_steps"], 3)
            nc.scalar.activation(f_tmp[:, 3, :], f_tmp[:, 2, :], ACT.Exp, scale=-1.0).then_inc(s["f_exp"], 1)
            act.wait_ge(s["f_exp"], 1)
            nc.scalar.activation(f_tmp[:, 4, :], f_tmp[:, 3, :], ACT.Ln, bias=1.0).then_inc(s["f_ln"], 1)
            for n in range(4, FIRST_GATE):
                read_out(n)

            for u in range(8):
                nk = (u % 2 + 1) * P
                act.wait_ge(s["row_max"], u + 1)
                if u >= 2:
                    act.wait_ge(s["probs_turned"], u - 1)
                for hh in range(2):
                    nc.scalar.activation(probs[:, u % 2, hh, 0:nk], bank[4 + u % 2][:, hh * 256:hh * 256 + nk],
                                         ACT.Exp, bias=sm_stat[:, u % 2, 2 + hh:3 + hh], scale=SCALE,
                                         accum_out=sm_stat[:, u % 2, 4 + hh:5 + hh]).then_inc(s["probs_exp"], 1)
                read_out(FIRST_GATE + u)
                act.wait_ge(s["probs_turned"], u + 1)
                if u >= 2:
                    act.wait_ge(s["pv_done"], u - 1)
                kbs = u % 2 + 1
                nc.scalar.activation(probsT[:, u % 2].rearrange("p (a k) q -> p a k q", a=2)[:, :, 0:kbs, :],
                                     bank[6][:, :].rearrange("p (a k q) -> p a k q", a=2, k=2)[:, :, 0:kbs, :],
                                     ACT.Copy).then_inc(s["probsT_ready"], 1)

            act.wait_ge(s["block_out"], NB)
            for t_ in (sig_a, sig_c):
                v = t_.rearrange("p j t -> p (j t)")
                nc.scalar.activation(v, v, ACT.Sigmoid).then_inc(s["gates_sig"], 1)
            for m in range(4):
                act.wait_ge(s["ln_step"], 5 + m)
                nc.scalar.activation(silu_sig[:, m, :], conv[:, m, :], ACT.Sigmoid).then_inc(s["silu_arg"], 1)

            def ple_out(t, first_bank):
                act.wait_ge(s["proj_done"], t + 1)
                for n in range(2):
                    last = nc.scalar.activation(ple_v[:, t, n * HALF:(n + 1) * HALF], bank[first_bank + n][:, :],
                                                ACT.Copy)
                last.then_inc(s["ple_ready"], 1)

            def bf16_part(t, part, ready, count):
                act.wait_ge(s[ready], count)
                nc.scalar.activation(x_parts[:, t, part, :], rows_ffn[t], ACT.Copy).then_inc(s["part_a"], 1)

            act.wait_ge(s["h_mid"], 2)
            square(0, rows_ffn[0])
            act.wait_ge(s["pple_turned"], 1)
            nc.scalar.activation(pT.rearrange("p k t -> p (k t)"), bank[3][:, :], ACT.Copy).then_inc(s["pT_ready"], 1)
            act.wait_ge(s["wo_done"], NT)
            bf16_part(0, 0, "normed", NT + 1)
            act.wait_ge(s["h_mid"], 4)
            square(1, rows_ffn[1])
            bf16_part(0, 1, "part_step", 1)
            ple_out(0, 2)
            bf16_part(1, 0, "normed", NT + 2)
            for t in range(NT):
                if t:
                    bf16_part(1, 1, "part_step", 2)
                act.wait_ge(s["f_neg"], t + 1)
                nc.scalar.activation(rest[:, t, :], rest[:, t, :], ACT.Exp).then_inc(s["route_exp"], 1)
            ple_out(1, 4)

            def first():
                act_selT(act, 0, 0)
                act.wait_ge(s["gatesT_done"], 1)
                nc.scalar.activation(gatesT, bank[3][0:E, 0:T], ACT.Copy).then_inc(s["gatesT_ready"], 1)

            def one(i, e, b):
                act_sigmoid(act, i)
                act_selT(act, i + 1, 1 - b)
                act_hT(act, i)
                act_y(act, i, b)

            def last_one():
                act_sigmoid(act, E - 1)
                act_hT(act, E - 1)
                act_y(act, E - 1, 1)

            over_passes(act, first, one, last_one)

            def further(i, e, chunk):
                act_selT(act, i, 0)
                act_sigmoid(act, i)
                act_hT(act, i)
                act_y(act, i, 0)

            overflow(act, further)

            for t in range(NT):
                act.wait_ge(s["tail_h"], 2 * t + 2)
                square(t, tok_tmp[:, t, :])

            def gate_half(t, n, pg_count):
                act.wait_ge(s["tail_pg"], pg_count)
                act.wait_ge(s["rstd"], 2 * NT + t + 1)
                nc.scalar.activation(tok_tmp2[:, t, n * HALF:(n + 1) * HALF], acc_bank[t][n][:, :], ACT.Sigmoid,
                                     scale=stat[:, 4 + t:5 + t]).then_inc(s["tail_sig"], 1)

            def square_half(t, n):
                act.wait_ge(s["tail_row"], 2 * t + n + 1)
                half = slice(n * HALF, (n + 1) * HALF)
                nc.scalar.activation(tok_tmp2[:, t, half], h[:, t, half], ACT.Square,
                                     accum_out=stat[:, 8 + 2 * t + n:9 + 2 * t + n]).then_inc(s["tail_sq"], 1)

            gate_half(0, 0, 1)
            gate_half(0, 1, 1)
            for n in range(2):
                square_half(0, n)
            for n in range(2):
                gate_half(1, n, 2 + n)
                square_half(1, n)
            act.wait_ge(s["rstd"], 3 * NT + 2)
            act.wait_ge(s["tail_gain"], 4)
            nc.scalar.activation(tok_tmp[:, 1, HALF:D], tok_tmp[:, 1, HALF:D], ACT.Copy,
                                 scale=stat[:, 5:6]).then_inc(s["last_ready"], 1)

        @block.vector
        def _(dve):
            def mean_square(t0, t1, count):
                dve.wait_ge(s["sumsq"], count)
                nc.vector.tensor_scalar(stat[:, 2 + t0:2 + t1], stat[:, t0:t1], 1.0 / D, RMS_EPS, ALU.mult,
                                        ALU.add).then_inc(s["mean_sq"], 1)

            def normalise(t, count, rows):
                dve.wait_ge(s["rstd"], count)
                nc.vector.tensor_scalar(rows[t], h[:, t, :], stat[:, 4 + t:5 + t], None,
                                        ALU.mult).then_inc(s["normed"], 1)

            def take_turned(g, gain, count):
                t, half = g // 2, g % 2
                dve.wait_ge(s["x_turned"], count)
                nc.vector.tensor_tensor(hnT[:, half * 4:half * 4 + 4, t * P:(t + 1) * P],
                                        bank[4 + g][:, :].rearrange("p (c q) -> p c q", c=4),
                                        bcast(gain[:, half * 4:half * 4 + 4], P), ALU.mult).then_inc(s["hnT_ready"], 1)

            for t in range(NT):
                mean_square(t, t + 1, t + 1)
            for t in range(NT):
                normalise(t, t + 1, rows_in)
            dve.wait_ge(s["params_turned"], 1)
            nc.vector.tensor_copy(params[:], bank[0][:, 0:36 + 4 * TAPS]).then_inc(s["params_ready"], 1)
            dve.wait_ge(s["params_ready"], 1)
            for g in range(4):
                take_turned(g, g_mix, g + 1)

            dve.wait_ge(s["consts"], N_CONST)
            nc.vector.memset(cum_base[0:H, :], 1.0).then_inc(s["cum_steps"], 1)
            nc.vector.memset(cum_key[32:32 + H, :], 1.0).then_inc(s["cum_steps"], 1)

            def convolve(b):
                dve.wait_ge(s["block_out"], 2 * b + 2)
                z = z_pad[:, 2 * b:2 * b + 2, PAD:]
                nc.vector.tensor_tensor(z, z, glu_sig, ALU.mult).then_inc(s["z_ready"], 1)
                dve.wait_ge(s["z_ready"], b + 1)
                for j in range(TAPS):
                    for m in (2 * b, 2 * b + 1):
                        n = 2 * TAPS * b + 2 * j + m % 2
                        if j:
                            dve.wait_ge(s["conv_step"], n - 1)
                            ins = nc.vector.scalar_tensor_tensor(out=conv[:, m, :], in0=z_pad[:, m, j:j + T],
                                                                 scalar=tap(j, m), in1=conv[:, m, :], op0=ALU.mult,
                                                                 op1=ALU.add)
                        else:
                            ins = nc.vector.tensor_scalar(conv[:, m, :], z_pad[:, m, 0:T], tap(0, m), cb[:, m:m + 1],
                                                          ALU.mult, ALU.add)
                        ins.then_inc(s["conv_step"], 1)

            convolve(0)

            dve.wait_ge(s["forget_done"], 1)
            nc.vector.tensor_scalar(f_tmp[:, 0, :], bank[2][0:H, 0:T], b_f[:, 0:1], None,
                                    ALU.add).then_inc(s["f_steps"], 1)
            dve.wait_ge(s["f_steps"], 1)
            nc.vector.tensor_scalar(f_tmp[:, 1, :], f_tmp[:, 0, :], 0.0, None, ALU.min).then_inc(s["f_steps"], 1)
            nc.vector.scalar_tensor_tensor(out=f_tmp[:, 2, :], in0=f_tmp[:, 0, :], scalar=-1.0, in1=f_tmp[:, 0, :],
                                           op0=ALU.mult, op1=ALU.max).then_inc(s["f_steps"], 1)
            dve.wait_ge(s["f_ln"], 1)
            nc.vector.tensor_tensor(f_tmp[:, 5, :], f_tmp[:, 1, :], f_tmp[:, 4, :],
                                    ALU.subtract).then_inc(s["f_steps"], 1)
            dve.wait_ge(s["f_steps"], 4)
            dve.wait_ge(s["cum_steps"], 2)
            nc.vector.tensor_tensor_scan(f_tmp[:, 0, :], cum_base[0:H, :], f_tmp[:, 5, :], 0.0, ALU.mult,
                                         ALU.add).then_inc(s["f_steps"], 1)
            dve.wait_ge(s["f_steps"], 5)
            nc.vector.tensor_scalar(cum_base[32:32 + H, :], f_tmp[:, 0, :], 1.0 / SCALE, None,
                                    ALU.mult).then_inc(s["cum_steps"], 1)
            nc.vector.tensor_scalar(cum_key[0:H, :], f_tmp[:, 0, :], -1.0 / SCALE, None,
                                    ALU.mult).then_inc(s["cum_steps"], 1)
            dve.wait_ge(s["cum_steps"], 4)

            def spread(hp):
                if hp >= 2:
                    dve.wait_ge(s["scores_done"], 2 * (hp - 1))
                for hh in range(2):
                    last = nc.vector.tensor_scalar(cum_q[:, hp % 2, hh, :], cum_base, head_hot[:, 2 * hp + hh:2 * hp + hh + 1],
                                                   None, ALU.mult)
                last.then_inc(s["cum_q_ready"], 1)

            spread(0)
            spread(1)
            convolve(1)

            def softmax(u):
                b, hp, qb = u % 2, u // 2, u % 2
                nk = (qb + 1) * P
                dve.wait_ge(s["scores_done"], u + 1)
                nc.vector.tensor_reduce(sm_stat[:, b, 0:2],
                                        bank[4 + b][:, :].rearrange("p (a k) -> p a k", a=2)[:, :, 0:nk], AX_X,
                                        ALU.max).then_inc(s["rows_recip"], 1)
                dve.wait_ge(s["rows_recip"], 2 * u + 1)
                nc.vector.tensor_scalar(sm_stat[:, b, 2:4], sm_stat[:, b, 0:2], -SCALE, None,
                                        ALU.mult).then_inc(s["row_max"], 1)
                if qb and hp + 2 < 4:
                    spread(hp + 2)
                dve.wait_ge(s["probs_exp"], 2 * u + 2)
                nc.vector.reciprocal(sm_stat[:, b, 0:2], sm_stat[:, b, 4:6]).then_inc(s["rows_recip"], 1)
                dve.wait_ge(s["rows_recip"], 2 * u + 2)
                for hh in range(2):
                    last = nc.vector.tensor_scalar(probs[:, b, hh, 0:nk], probs[:, b, hh, 0:nk],
                                                   sm_stat[:, b, hh:hh + 1], None, ALU.mult)
                last.then_inc(s["probs_norm"], 1)
                if u:
                    take_attention(dve, u - 1)

            def ln_stats():
                for t in range(NT):
                    dve.wait_ge(s["conv_turned"], t + 1)
                    nc.vector.bn_stats(stat[:, 8 + 6 * t:14 + 6 * t], bank[2 + t][:, :]).then_inc(s["ln_step"], 1)
                dve.wait_ge(s["ln_step"], 2)
                for t in range(NT):
                    last = nc.vector.bn_aggr(stat[:, 20 + 2 * t:22 + 2 * t], stat[:, 8 + 6 * t:14 + 6 * t])
                last.then_inc(s["ln_step"], 1)
                dve.wait_ge(s["ln_step"], 3)
                nc.vector.tensor_scalar(stat[:, 26:28], stat[:, 20:24].rearrange("p (t v) -> p t v", v=2)[:, :, 1],
                                        LN_EPS, None, ALU.add).then_inc(s["ln_step"], 1)

            def ln_apply():
                dve.wait_ge(s["ln_pow"], 1)
                dve.wait_ge(s["scores_done"], 8)
                for t in range(NT):
                    nc.vector.tensor_scalar(ln_out[:, t, :], bank[2 + t][:, :], stat[:, 20 + 2 * t:21 + 2 * t],
                                            stat[:, 28 + t:29 + t], ALU.subtract, ALU.mult).then_inc(s["ln_ready"], 1)

            for u in range(8):
                softmax(u)
                if u == 5:
                    ln_stats()
                if u == 6:
                    ln_apply()
            take_attention(dve, 7)
            for m in range(4):
                dve.wait_ge(s["ln_back"], m // 2 + 1)
                nc.vector.tensor_scalar(conv[:, m, :], bank[2 + m // 2][:, (m % 2) * T:(m % 2 + 1) * T],
                                        lg[:, m:m + 1], lb[:, m:m + 1], ALU.mult, ALU.add).then_inc(s["ln_step"], 1)
            dve.wait_ge(s["silu_arg"], 4)
            dve.wait_ge(s["ln_step"], 8)
            nc.vector.tensor_tensor(conv, conv, silu_sig, ALU.mult).then_inc(s["silu_ready"], 1)

            dve.wait_ge(s["branch_a"], 1)
            dve.wait_ge(s["gates_sig"], 2)
            for m in range(4):
                v = sig_a[:, 2 * m:2 * m + 2, :].rearrange("p j t -> p (j t)")
                nc.vector.tensor_tensor(v, v, bank[4 + m][:, :], ALU.mult).then_inc(s["merge_step"], 1)
            for m in range(4):
                va = sig_a[:, 2 * m:2 * m + 2, :].rearrange("p j t -> p (j t)")
                vc = sig_c[:, 2 * m:2 * m + 2, :].rearrange("p j t -> p (j t)")
                dve.wait_ge(s["branch_c"], m + 1)
                nc.vector.tensor_tensor(vc, vc, bank[m][:, :], ALU.mult).then_inc(s["merge_step"], 1)
                dve.wait_ge(s["merge_step"], 5 + m)
                nc.vector.tensor_tensor(va, va, vc, ALU.add).then_inc(s["merged"], 1)

            bstep = [0]

            def link(ins, name, count):
                count[0] += 1
                ins.then_inc(s[name], 1)
                dve.wait_ge(s[name], count[0])

            dve.wait_ge(bias_dma, 16 * 6)
            link(nc.vector.tensor_copy(bias3, bias_in), "bias_part", bstep)
            link(nc.vector.tensor_tensor(bias_in, bias_in, bias3, ALU.subtract), "bias_part", bstep)
            link(nc.vector.tensor_copy(bias3[E:2 * E], bias_in[E:2 * E]), "bias_part", bstep)
            link(nc.vector.tensor_copy(bias3[2 * E:3 * E], bias_in[2 * E:3 * E]), "bias_part", bstep)
            link(nc.vector.tensor_tensor(bias_in[2 * E:3 * E], bias_in[2 * E:3 * E], bias3[2 * E:3 * E],
                                         ALU.subtract), "bias_part", bstep)
            nc.vector.tensor_copy(bias3[2 * E:3 * E], bias_in[2 * E:3 * E]).then_inc(s["bias_ready"], 1)

            rstep = [0]

            def route(ins):
                link(ins, "route_step", rstep)

            def top(t):
                lg_ = bank[t][:, 0:E]
                dve.wait_ge(s["logits_done"], t + 1)
                route(nc.vector.max(top8[:, t, :], lg_))
                route(nc.vector.tensor_scalar(above[:, t, :], lg_, top8[:, t, 3:4], None, ALU.is_gt))
                route(nc.vector.tensor_scalar(ties[:, t, :], lg_, top8[:, t, 3:4], None, ALU.is_equal))
                route(nc.vector.reduce_sum(stat[:, 6 + t:7 + t], above[:, t, :], AX_X))

            def choose(t):
                route(nc.vector.tensor_tensor_scan(tie_no[:, t, :], ones_e[:, t, :], ties[:, t, :],
                                                   stat[:, 6 + t:7 + t], ALU.mult, ALU.add))
                route(nc.vector.scalar_tensor_tensor(out=ties[:, t, :], in0=tie_no[:, t, :], scalar=4.0,
                                                     in1=ties[:, t, :], op0=ALU.is_le, op1=ALU.mult))
                nc.vector.tensor_tensor(routed[:, t, :], above[:, t, :], ties[:, t, :],
                                        ALU.add).then_inc(s["routed_ready"], 1)
                nc.vector.tensor_scalar(rest[:, t, :], bank[t][:, 0:E], top8[:, t, 0:1], None,
                                        ALU.subtract).then_inc(s["f_neg"], 1)

            def weigh(t):
                dve.wait_ge(s["route_exp"], t + 1)
                dve.wait_ge(s["routed_ready"], t + 1)
                route(nc.vector.tensor_tensor(gate_w[:, t, :], rest[:, t, :], routed[:, t, :], ALU.mult))
                route(nc.vector.reduce_sum(stat[:, 6 + t:7 + t], gate_w[:, t, :], AX_X))
                route(nc.vector.reciprocal(stat[:, 24 + t:25 + t], stat[:, 6 + t:7 + t]))
                route(nc.vector.tensor_scalar(gate_w[:, t, :], gate_w[:, t, :], stat[:, 24 + t:25 + t], None,
                                              ALU.mult))

            def add_mixers(t):
                dve.wait_ge(s["wo_done"], t + 1)
                for n in range(2):
                    v = h[:, t, n * HALF:(n + 1) * HALF]
                    nc.vector.tensor_tensor(v, v, bank[4 + 2 * t + n][:, :], ALU.add).then_inc(s["h_mid"], 1)

            def take_rows(t):
                for g in (2 * t, 2 * t + 1):
                    take_turned(g, g_ffn, 5 + g)

            def second_part(t):
                dve.wait_ge(s["part_a"], 2 * t + 1)
                nc.vector.tensor_tensor(rows_ffn[t], rows_ffn[t], x_parts[:, t, 0, :],
                                        ALU.subtract).then_inc(s["part_step"], 1)

            def third_part(t):
                dve.wait_ge(s["part_a"], 2 * t + 2)
                nc.vector.tensor_tensor(x_parts[:, t, 2, :], rows_ffn[t], x_parts[:, t, 1, :],
                                        ALU.subtract).then_inc(s["parts_ready"], 1)

            route(nc.vector.memset(ones_e, 1.0))
            add_mixers(0)
            mean_square(0, 1, NT + 1)
            normalise(0, NT + 1, rows_ffn)
            take_rows(0)
            add_mixers(1)
            second_part(0)
            mean_square(1, 2, NT + 2)
            top(0)
            normalise(1, NT + 2, rows_ffn)
            choose(0)
            take_rows(1)
            third_part(0)
            second_part(1)
            weigh(0)
            top(1)
            choose(1)
            third_part(1)
            dve.wait_ge(s["rank_done"], 1)
            route(nc.vector.scalar_tensor_tensor(out=ranks[:], in0=bank[2][:, 0:NT * E].rearrange("p (t e) -> p t e", t=NT),
                                                 scalar=1.0, in1=routed[:], op0=ALU.add, op1=ALU.mult))
            nc.vector.tensor_scalar(ranks[:], ranks[:], -1.0, None, ALU.add).then_inc(s["ranks_ready"], 1)
            dve.wait_ge(s["ranks_ready"], 1)

            def first():
                dve_select(dve, 0, 0, 0, 0, 2)
                weigh(1)
                route(nc.vector.tensor_copy(gates3[:, :, :, 0], gate_w))
                route(nc.vector.tensor_tensor(rest, gate_w, gates3[:, :, :, 0], ALU.subtract))
                route(nc.vector.tensor_copy(gates3[:, :, :, 1], rest))
                route(nc.vector.tensor_tensor(gates3[:, :, :, 2], rest, gates3[:, :, :, 1], ALU.subtract))
                nc.vector.memset(flag_f[:], 0.0).then_inc(s["gates3_ready"], 1)
                dve_take(dve, 0, 0)
                dve.wait_ge(s["gates3_ready"], 1)
                route(nc.vector.reduce_max(flag_f[:], bank[2][0:1, 2 * E:3 * E], AX_X))
                nc.vector.tensor_copy(flag[:], flag_f[:]).then_inc(s["flag_ready"], 1)

            def one(i, e, b):
                dve_select(dve, i + 1, e + 1, 1 - b, 0, 2)
                dve_activate(dve, i)
                dve_take(dve, i + 1, 1 - b)

            over_passes(dve, first, one, lambda: dve_activate(dve, E - 1))

            def further(i, e, chunk):
                dve_select(dve, i, e, 0, chunk, 1)
                dve_take(dve, i, 0)
                dve_activate(dve, i)

            overflow(dve, further, lambda: dve.wait_ge(s["combined"], E * CHUNKS))

            def half_of(x_, t, n):
                return x_[:, t, n * HALF:(n + 1) * HALF]

            for t, done, count in ((0, "tile_combined", 1), (1, "combined", E)):
                dve.wait_ge(s[done], count)
                for n in range(2):
                    nc.vector.tensor_tensor(half_of(h, t, n), half_of(h, t, n), acc_bank[t][n][:, :],
                                            ALU.add).then_inc(s["tail_h"], 1)
                for g in (2 * t, 2 * t + 1):
                    take_turned(g, g_ple, 9 + g)
                mean_square(t, t + 1, 2 * NT + t + 1)
            dve.wait_ge(final_dma, 16)
            for t in range(NT):
                for n in range(2):
                    q = 2 * t + n
                    dve.wait_ge(s["tail_sig"], q + 1)
                    nc.vector.tensor_tensor(half_of(tok_tmp2, t, n), half_of(tok_tmp2, t, n), half_of(ple_v, t, n),
                                            ALU.mult).then_inc(s["tail_step"], 1)
                    dve.wait_ge(s["tail_step"], q + 1)
                    nc.vector.tensor_tensor(half_of(h, t, n), half_of(h, t, n), half_of(tok_tmp2, t, n),
                                            ALU.add).then_inc(s["tail_row"], 1)
                    dve.wait_ge(s["tail_row"], q + 1)
                    nc.vector.tensor_tensor(half_of(tok_tmp, t, n), half_of(h, t, n),
                                            g_final[:, n * HALF:(n + 1) * HALF], ALU.mult).then_inc(s["tail_gain"], 1)
                    dve.wait_ge(s["tail_sq"], q + 1)
                    if n:
                        dve.wait_ge(s["tail_mean"], t + 1)
                    more = stat[:, 12 + t:13 + t] if n else RMS_EPS
                    nc.vector.tensor_scalar(stat[:, 2 + t:3 + t] if n else stat[:, 12 + t:13 + t],
                                            stat[:, 8 + q:9 + q], 1.0 / D, more, ALU.mult,
                                            ALU.add).then_inc(s["mean_sq" if n else "tail_mean"], 1)
                dve.wait_ge(s["rstd"], 3 * NT + t + 1)
                for n in range(2 if t == 0 else 1):
                    dve.wait_ge(s["tail_gain"], 2 * t + n + 1)
                    nc.vector.tensor_scalar(half_of(tok_tmp, t, n), half_of(tok_tmp, t, n), stat[:, 4 + t:5 + t],
                                            None, ALU.mult).then_inc(s["out_ready"], 1)


_INS = ["x", "p", "norm_mix", "w_in", "b_forget", "w_attn_out", "conv_w", "conv_b", "conv_ln_g", "conv_ln_b",
        "w_conv_out", "w_o", "norm_ffn", "w_router", "b_router", "w_gate", "b_gate", "w_up", "b_up",
        "w_down", "b_down", "norm_ple", "w_ple_gate", "w_ple_proj", "norm_final"]


def kernel(**inputs):
    import numpy as _np
    import concourse.bacc as _bacc
    from concourse.bass_utils import run_bass_kernel_spmd as _run

    nc = _bacc.Bacc("TRN2", target_bir_lowering=False, num_devices=1)
    arrays, args = {}, []
    for name in _INS:
        a = _np.ascontiguousarray(inputs[name])
        arrays[f"in_{name}"] = a
        args.append(nc.dram_tensor(f"in_{name}", a.shape, mybir.dt.from_np(a.dtype), kind="ExternalInput").ap())
    shape = tuple(inputs["x"].shape)
    args.append(nc.dram_tensor("out_block", shape, F32, kind="ExternalOutput").ap())
    build_block(nc, *args)
    return _run(nc, [arrays], core_ids=[0]).results[0]["out_block"]
```

```python
from contextlib import ExitStack

import concourse.bass as bass
from concourse import mybir

F32 = mybir.dt.float32
BF16 = mybir.dt.bfloat16
I32 = mybir.dt.int32
FR = mybir.dt.float32r
ALU = mybir.AluOpType
ACT = mybir.ActivationFunctionType
AX_X = mybir.AxisListType.X

P = 128
NEG_INF = -1e30
RMS_EPS = 1e-6
LN_EPS = 1e-5
SWIGLU_LIMIT = 7.0
SWIGLU_ALPHA = 1.702


def build_block(nc, x, p, norm_mix, w_in, b_forget, w_attn_out, conv_w, conv_b, conv_ln_g, conv_ln_b,
                w_conv_out, w_o, norm_ffn, w_router, b_router, w_gate, b_gate, w_up, b_up,
                w_down, b_down, norm_ple, w_ple_gate, w_ple_proj, norm_final, out):
    _, T, D = x.shape
    E = w_router.shape[2]
    H = b_forget.shape[1]
    AW = w_attn_out.shape[1]
    CW = w_conv_out.shape[1]
    TAPS = conv_w.shape[1]
    PLE = w_ple_proj.shape[1]
    HD = AW // H
    NT, KD, KA, KP = T // P, D // P, AW // P, PLE // P
    HALF = D // 2
    SCALE = float(HD) ** -0.5
    SLOTS = 64
    CHUNKS = T // SLOTS
    BLK = 256
    RING = 12
    FRONT = 8
    PER_MAT = RING // 3
    assert (NT, KD, KA, KP, E, H, HD) == (2, 8, 4, 2, 32, 8, 64) and w_gate.shape[3] == D and CW == AW

    col_q, col_k, col_v, col_f = 0, AW, 2 * AW, 3 * AW
    col_ca = col_f + H
    col_cg = col_ca + CW
    col_ga = col_cg + CW
    col_gc = col_ga + D
    BLOCKS = [("ca", 0), ("cg", 0), ("ca", 1), ("cg", 1), ("q", 0), ("k", 0), ("q", 1), ("k", 1), ("v", 0), ("v", 1)]
    FIRST_GATE = len(BLOCKS)
    BLOCKS += [("ga", b) for b in range(4)] + [("gc", b) for b in range(4)]
    NB = len(BLOCKS)
    COL0 = {"q": col_q, "k": col_k, "v": col_v, "ca": col_ca, "cg": col_cg, "ga": col_ga, "gc": col_gc}
    AO_SLOT, CO_SLOT = NB % FRONT, (NB + 2) % FRONT
    assert AO_SLOT == 2 and CO_SLOT == 4

    with ExitStack() as ctx:
        def sb(name, shape, dt):
            return ctx.enter_context(nc.sbuf_tensor(name, shape, dt))

        def sem(name):
            return ctx.enter_context(nc.semaphore(name))

        with ExitStack() as front:
            w_parts_a = front.enter_context(nc.sbuf_tensor("w_parts_a", [P, 2, 2, 2048], FR))
            w_parts_b = front.enter_context(nc.sbuf_tensor("w_parts_b", [P, 1, 2, 2048], FR))
            x_parts_r = front.enter_context(nc.sbuf_tensor("x_parts_r", [P, 2, KD, T], FR))
            ring_parts = front.enter_context(nc.sbuf_tensor("ring_parts", [P, FRONT, 2048], FR))
            attn_parts = front.enter_context(nc.sbuf_tensor("attn_parts", [P, 2, KA, T], FR))
        wide = sb("wide", [P, 8192], F32)
        ring_high = sb("ring_high", [P, RING - FRONT, 2048], F32)
        ring_low = sb("ring_low", [P, FRONT, 2048], F32)
        hnT = sb("hnT", [P, KD, T], F32)
        reg_a = sb("reg_a", [P, 3072], F32)
        reg_b = sb("reg_b", [P, 2048], F32)
        reg_c = sb("reg_c", [P, 1024], F32)
        reg_d = sb("reg_d", [P, 2176], F32)
        reg_e = sb("reg_e", [P, 4096], F32)
        reg_f = sb("reg_f", [P, 1536], F32)
        h = sb("h", [P, NT, D], F32)

        def view(reg, lo, hi, spec, **kw):
            return reg[:, lo:hi].rearrange(spec, **kw)

        def ring_slot(c):
            return ring_low[:, c, :] if c < FRONT else ring_high[:, c - FRONT, :]

        def w_part(n, part):
            buf = w_parts_b[:, 0, part, :] if n % 3 == 2 else w_parts_a[:, n % 3, part, :]
            return buf.rearrange("p (k c) -> p k c", k=KD)

        def low_part(eng, ops, n, done):
            eng.wait_ge(s["w_high"], n)
            ops.tensor_tensor(w_part(n, 1), ring_low[:, n % FRONT, :].rearrange("p (k c) -> p k c", k=KD), w_part(n, 0),
                              ALU.subtract).then_inc(s[done], 1)

        conv_parts = x_parts_r[:, :, 0:KA, :]
        OUT_SLOT, OUT_HIGH = (AO_SLOT, CO_SLOT), (6, 0)

        def out_part(m, part):
            first = OUT_HIGH[m] if part == 0 else OUT_SLOT[m]
            return ring_parts[:, first:first + 2, :].rearrange("p s (k n) -> p (s k) n", n=D)

        def out_low(eng, ops, m, half, done):
            eng.wait_ge(s["out_high"], 2 * m + half + 1)
            ops.tensor_tensor(ring_parts[:, OUT_SLOT[m] + half, :], ring_low[:, OUT_SLOT[m] + half, :],
                              ring_parts[:, OUT_HIGH[m] + half, :], ALU.subtract).then_inc(s[done], 1)

        def gate_part(c, part):
            return ring_parts[:, (c + PER_MAT) if part == 0 else c, :]

        def gate_low(eng, ops, c, tiles, done):
            eng.wait_ge(s["pg_high"], c + 1)
            cols = slice(tiles[0] * D, (tiles[-1] + 1) * D)
            ops.tensor_tensor(gate_part(c, 1)[:, cols], ring_low[:, c, cols], gate_part(c, 0)[:, cols],
                              ALU.subtract).then_inc(s[done], 1)

        V_LOW = 2

        def wait_low(eng, n):
            if n == 0:
                eng.wait_ge(s["block_done"], 1)
            elif n <= V_LOW:
                eng.wait_ge(s["w_low_v"], n)
            else:
                eng.wait_ge(s["w_low_p"], n - V_LOW)

        w_o_sb = view(wide, 0, 8192, "p (k n) -> p k n", k=KD)
        x_parts = wide[:, 0:3072].bitcast(BF16).rearrange("p (t s d) -> p t s d", t=NT, s=3)
        xT = view(wide, 3072, 3584, "p (k s) -> p k s", k=KD)
        g_clip = wide[:, 3584:4096]
        g_sig = wide[:, 4096:4608]
        u_clip = wide[:, 4608:5120]
        hT = view(wide, 5120, 5632, "p (j s) -> p j s", j=4)
        y_sb = wide[:, 5632:6144]
        selT = view(wide, 6144, 6656, "p (b t) -> p b t", b=2)
        h_act = wide[:, 6656:7168]
        g_final = wide[:, 7168:8192]

        qT = view(reg_a, 0, 1024, "p (j t) -> p j t", j=KA)
        kT = view(reg_a, 1024, 2048, "p (j t) -> p j t", j=KA)
        v_sb = view(reg_a, 2048, 3072, "p (t c) -> p t c", t=NT)
        ln_out = view(reg_a, 1024, 2048, "p (t c) -> p t c", t=NT)
        b_down_sb = reg_a[0:E, 0:1024]
        gatesT = reg_a[0:E, 1024:1280]
        bias3 = reg_a[0:3 * E, 2048:3072].bitcast(BF16)

        glu_sig = view(reg_b, 0, 512, "p (j t) -> p j t", j=2)
        f_tmp = reg_b[0:H, 512:2048].rearrange("p (n t) -> p n t", n=6)
        probs = view(reg_b, 0, 1024, "p (b h k) -> p b h k", b=2, h=2)
        probsT = view(reg_b, 1024, 2048, "p (b j q) -> p b j q", b=2, j=4)
        ple_v = view(reg_b, 0, 2048, "p (t d) -> p t d", t=NT)

        taps_in = reg_c[0:TAPS, 0:CW]
        p_sb = view(reg_c, 0, 512, "p (t d) -> p t d", t=NT)
        pT = view(reg_c, 512, 1024, "p (k t) -> p k t", k=KP)

        PAD = TAPS - 1
        ZW = PAD + T
        z_pad = view(reg_d, 0, 4 * ZW, "p (j t) -> p j t", j=4)
        conv = view(reg_d, 4 * ZW, 4 * ZW + 1024, "p (j t) -> p j t", j=4)
        silu_sig = view(reg_d, 0, 1024, "p (j t) -> p j t", j=4)
        bias_in = reg_d[0:3 * E, 0:2048]

        sig_a = view(reg_e, 0, 2048, "p (j t) -> p j t", j=KD)
        sig_c = view(reg_e, 2048, 4096, "p (j t) -> p j t", j=KD)
        w_proj_sb = view(wide, 4096, 6144, "p (k n) -> p k n", k=KP)
        tok_tmp = view(reg_e, 0, 2048, "p (t d) -> p t d", t=NT)
        tok_tmp2 = view(reg_e, 2048, 4096, "p (t d) -> p t d", t=NT)

        rows_in = [tok_tmp[:, t, :] for t in range(NT)]
        rows_ffn = [reg_a[:, 1024:2048], reg_b[:, 1024:2048]]

        cum_base = reg_f[:, 0:256]
        cum_key = reg_f[:, 256:512]
        cum_q = view(reg_f, 512, 1536, "p (b h t) -> p b h t", b=2, h=2)

        kept_gate = {E - 3: [(0, 2, reg_e[:, 2048:4096])],
                     E - 2: [(0, 2, reg_d[:, 0:2048]), (2, 1, reg_f[:, 512:1536]), (3, 1, wide[:, 7168:8192])],
                     E - 1: [(0, 2, reg_e[:, 0:2048]), (2, 2, hnT[:, :, :].rearrange("p k t -> p (k t)"))]}
        kept_chunks = {e: sum(tiles for _, tiles, _ in pieces) // 2 for e, pieces in kept_gate.items()}

        def missed(i, c):
            return sum(e < i and c < n for e, n in kept_chunks.items())

        ident = sb("ident", [P, P], F32)
        ident_b = sb("ident_b", [P, P], BF16)
        causal_b = sb("causal_b", [P, P], BF16)
        before_b = sb("before_b", [P, P], BF16)
        ones_b = sb("ones_b", [P, P], BF16)
        ones_r = sb("ones_r", [1, P], F32)
        head_hot = sb("head_hot", [P, H], F32)
        params_in = sb("params_in", [36, P], F32)
        params = sb("params", [P, 36 + 4 * TAPS], F32)
        w_f = sb("w_f", [P, KD, H], F32)
        b_f = sb("b_f", [H, 1], F32)
        w_router_sb = sb("w_router_sb", [P, KD, E], F32)
        b_router_sb = sb("b_router_sb", [P, E], F32)
        slot_id = sb("slot_id", [P, CHUNKS, 2, SLOTS], BF16)
        expert_hot = sb("expert_hot", [3 * E, E], F32)
        hot = sb("hot", [3 * E, 2, SLOTS], BF16)
        sel = sb("sel", [P, 2, NT, 2, SLOTS], BF16)
        ranks = sb("ranks", [P, NT, E], F32)
        gates3 = sb("gates3", [P, NT, E, 3], BF16)
        gate_slot = sb("gate_slot", [P, 2], F32)
        gate_parts = sb("gate_parts", [P, 3], F32)
        stat = sb("stat", [P, 32], F32)
        mhalf = sb("mhalf", [P, 2], F32)
        sm_stat = sb("sm_stat", [P, 2, 6], F32)
        top8 = sb("top8", [P, NT, 8], F32)
        flag = sb("flag", [1, 1], I32)
        flag_f = sb("flag_f", [1, 1], F32)
        g_mix, g_ffn, g_ple = params[:, 0:8], params[:, 8:16], params[:, 16:24]
        cb, lg, lb = params[:, 24:28], params[:, 28:32], params[:, 32:36]

        ones_e, above, ties, tie_no, gate_w, rest, logits = (
            view(reg_f, n * NT * E, (n + 1) * NT * E, "p (t e) -> p t e", t=NT) for n in range(7))
        routed = sb("routed", [P, NT, E], BF16)

        def tap(j, m):
            return params[:, 36 + m * TAPS + j:37 + m * TAPS + j]

        bank = [ctx.enter_context(nc.psum_tensor(f"bank{i}", [P, HALF], F32)) for i in range(8)]
        acc_bank = [[bank[0], bank[1]], [bank[2], bank[3]]]
        bank_g, bank_u, bank_y, bank_x = bank[4:8]
        ple_bank = [[bank[4], bank[5]], [bank[0], bank[1]]]
        pieces = [(0, bank[0], 0, HALF), (0, bank[1], HALF, HALF),
                  (1, bank[2], 0, HALF), (1, bank[3], HALF, HALF // 2), (1, bank[4], HALF + HALF // 2, HALF // 2)]

        params_dma, forget_dma, wo_dma, p_dma, proj_dma = [sem(n) for n in (
            "params_dma", "forget_dma", "wo_dma", "p_dma", "proj_dma")]
        bias_dma, bdown_dma, final_dma, router_dma, out_dma = [sem(n) for n in (
            "bias_dma", "bdown_dma", "final_dma", "router_dma", "out_dma")]
        block_dma = [sem(f"block_dma{n}") for n in range(NB)]
        x_dma = [sem(f"x_dma{t}") for t in range(NT)]
        ao_dma, co_dma, kept_dma = sem("ao_dma"), sem("co_dma"), sem("kept_dma")
        chunk_dma = [sem(f"chunk_dma{n}") for n in range(RING)]
        pgate_dma = [sem(f"pgate_dma{n}") for n in range(PER_MAT)]
        names = []
        names += "consts params_turned params_ready sumsq mean_sq rstd normed x_turned hnT_ready".split()
        names += ("x_high x_low w_high w_low_v w_low_p attn_high conv_high out_high out_low_p out_low_v "
                  "pg_high pg_low_p pg_low_v").split()
        names += "block_done block_out forget_done f_neg f_exp f_ln f_steps cum_steps cum_q_ready z_ready".split()
        names += ("head_scored scores_done row_max probs_exp probs_norm rows_recip probs_turned "
                  "probsT_ready pv_done attn_ready").split()
        names += "conv_step conv_turned ln_step ln_pow ln_ready ln_back silu_arg silu_out silu_ready".split()
        names += "gates_sig branch_a branch_c merge_step merged wo_tiles wo_done h_mid".split()
        names += "pple_turned pT_ready proj_done ple_ready".split()
        names += ("part_step part_a parts_ready logits_done routed_ready gates3_ready route_step rank_done "
                  "ranks_ready route_exp gatesT_done gatesT_ready flag_ready first_rows bias_part "
                  "bias_ready").split()
        names += ("sel_ready gathered xT_ready gslot_ready selT_ready gclip_ready gsig_ready gglu uclip "
                  "h_ready turned hT_ready y_ready combined chunk_used tile_combined").split()
        names += ("tail_h tail_pg tail_sig tail_step tail_row tail_sq tail_gain tail_mean out_ready "
                  "last_ready").split()
        s = {n: sem(n) for n in names}

        def bcast(ap, n):
            return ap.unsqueeze(len(ap.shape)).broadcast_to(list(ap.shape) + [n])

        N_CONST = 21
        N_PARAM = 7
        WARM = 11
        w_in_k = w_in[0].rearrange("(k p) n -> p k n", p=P)
        mats = [w_gate, w_up, w_down]
        ROWS = D // PER_MAT


        def load_chunks(sp, i, e, first_chunk=0):
            for c in range(first_chunk, RING):
                if not isinstance(i, int) or i > 0:
                    sp.wait_ge(s["chunk_used"], (i - 1) * RING + (c + 1))
                rows = mats[c // PER_MAT][0, e, (c % PER_MAT) * ROWS:(c % PER_MAT + 1) * ROWS, :]
                sp.dma_start(ring_slot(c).rearrange("p (k n) -> p k n", n=D),
                             rows.rearrange("(k p) n -> p k n", p=P)).then_inc(chunk_dma[c], 16)

        def pe_gather(pe, i, b):
            pe.wait_ge(s["sel_ready"], i + 1)
            for k in range(KD):
                for n in range(3 * NT):
                    t, part = n // 3, n % 3
                    last = nc.tensor.matmul(bank_x[:, k * SLOTS:(k + 1) * SLOTS], x_parts[:, t, part, k * P:(k + 1) * P],
                                            sel[:, b, t, 0, :], start=n == 0, stop=n == 3 * NT - 1)
            return last

        def pe_gather_gates(i, e, b):
            for t in range(NT):
                nc.tensor.transpose(bank_y[:, t * 64:(t + 1) * 64].bitcast(BF16),
                                    sel[:, b, t].rearrange("p a s -> p (a s)"), ident_b[:])
            for t in range(NT):
                last = nc.tensor.matmul(bank_y[:, 256:259], sel[:, b, t].rearrange("p a s -> p (a s)"),
                                        gates3[:, t, e, :], start=t == 0, stop=t == NT - 1)
            last.then_inc(s["gathered"], 1)

        def pe_expand(pe, i, b, which, kept=(), before=0):
            dst = bank_u if which else bank_g
            for n in range(2):
                nc.tensor.matmul(dst[n * 64:(n + 1) * 64, :], hot[:, b, :],
                                 bias3[:, which * D + n * HALF:which * D + (n + 1) * HALF], start=True, stop=False)
            if not which:
                pe.wait_ge(s["xT_ready"], i + 1)
            place = {first + k: (at, k * D) for first, tiles, at in kept for k in range(tiles)}
            for c in range(PER_MAT):
                slot = which * PER_MAT + c
                if 2 * c in place:
                    pe.wait_ge(kept_dma, 16 * sum(len(pieces) for pieces in kept_gate.values()))
                else:
                    pe.wait_ge(chunk_dma[slot], (i + 1 - missed(before, slot)) * 16)
                for kk in range(2):
                    at, col = place.get(2 * c + kk, (ring_slot(slot), kk * D))
                    for n in range(2):
                        last = nc.tensor.matmul(dst[n * 64:(n + 1) * 64, :], xT[:, 2 * c + kk, :],
                                                at[:, col + n * HALF:col + (n + 1) * HALF],
                                                start=False, stop=c == PER_MAT - 1 and kk == 1)
                last.then_inc(s["chunk_used"], 1)

        def pe_turn(pe, i):
            pe.wait_ge(s["h_ready"], i + 1)
            for j in range(4):
                last = nc.tensor.transpose(bank_u[:, j * P:(j + 1) * P], h_act[:, j * P:(j + 1) * P], ident[:])
            last.then_inc(s["turned"], 1)

        def pe_down(pe, i, prepared):
            pe.wait_ge(s["hT_ready"], i + 1)
            pe.wait_ge(s["selT_ready"], prepared)
            pe.wait_ge(s["gslot_ready"], prepared)
            for c in range(PER_MAT):
                slot = 2 * PER_MAT + c
                pe.wait_ge(chunk_dma[slot], (i + 1) * 16)
                for kk in range(2):
                    k = 2 * c + kk
                    for n in range(2):
                        last = nc.tensor.matmul(bank_y[n * 64:(n + 1) * 64, :],
                                                hT[:, k % 4, (k // 4) * 64:(k // 4 + 1) * 64],
                                                ring_slot(slot)[:, kk * D + n * HALF:kk * D + (n + 1) * HALF],
                                                start=k == 0, stop=k == KD - 1)
                last.then_inc(s["chunk_used"], 1)

        def pe_combine_tile(pe, i, b, t):
            pe.wait_ge(s["y_ready"], i + 1)
            for n in range(2):
                last = nc.tensor.matmul(acc_bank[t][n][:, :], selT[n * 64:(n + 1) * 64, b, t * P:(t + 1) * P],
                                        y_sb[n * 64:(n + 1) * 64, :], start=False, stop=True,
                                        skip_group_check=True)
            return last

        def pe_combine(pe, i, b):
            pe_combine_tile(pe, i, b, 0)
            pe_combine_tile(pe, i, b, 1).then_inc(s["combined"], 1)

        def pe_stay_warm(times):
            for _ in range(times):
                nc.tensor.matmul(bank_x[:, :], ident_b[:], ident_b[:].unsqueeze(1).broadcast_to([P, 4, P]),
                                 start=True, stop=True)

        def dve_select(dve, i, e, b, chunk, back):
            if not isinstance(i, int) or i >= back:
                dve.wait_ge(s["gathered"], i - (back - 1))
                dve.wait_ge(s["chunk_used"], (i - back) * RING + 2 * PER_MAT)
            nc.vector.tensor_scalar(hot[:, b, :], expert_hot[:, bass.ds(e, 1)].broadcast_to([3 * E, SLOTS]), 1.0, None,
                                    ALU.mult)
            for t in range(NT):
                last = nc.vector.tensor_scalar(sel[:, b, t].rearrange("p a s -> p (a s)"),
                                               slot_id[:, chunk].rearrange("p a s -> p (a s)"),
                                               ranks[:, t, bass.ds(e, 1)], None, ALU.is_equal)
            last.then_inc(s["sel_ready"], 1)

        def dve_take(dve, i, b, ready="gathered"):
            dve.wait_ge(s[ready], i + 1)
            nc.vector.tensor_tensor(xT, bank_x[:, :].rearrange("p (k s) -> p k s", k=KD), bcast(g_ffn, SLOTS),
                                    ALU.mult).then_inc(s["xT_ready"], 1)

        def dve_activate(dve, i):
            dve.wait_ge(s["chunk_used"], i * RING + PER_MAT)
            nc.vector.tensor_scalar(g_clip, bank_g[:, :], SWIGLU_LIMIT, None, ALU.min).then_inc(s["gclip_ready"], 1)
            dve.wait_ge(s["gsig_ready"], i + 1)
            nc.vector.tensor_tensor(g_clip, g_clip, g_sig, ALU.mult).then_inc(s["gglu"], 1)
            dve.wait_ge(s["chunk_used"], i * RING + 2 * PER_MAT)
            nc.vector.tensor_scalar(u_clip, bank_u[:, :], SWIGLU_LIMIT, -SWIGLU_LIMIT, ALU.min,
                                    ALU.max).then_inc(s["uclip"], 1)
            dve.wait_ge(s["uclip"], i + 1)
            dve.wait_ge(s["gglu"], i + 1)
            nc.vector.scalar_tensor_tensor(out=h_act, in0=u_clip, scalar=1.0, in1=g_clip, op0=ALU.add,
                                           op1=ALU.mult).then_inc(s["h_ready"], 1)

        def act_sigmoid(act, i):
            act.wait_ge(s["gclip_ready"], i + 1)
            nc.scalar.activation(g_sig, g_clip, ACT.Sigmoid, scale=SWIGLU_ALPHA).then_inc(s["gsig_ready"], 1)

        def act_selT(act, i, b):
            act.wait_ge(s["gathered"], i + 1)
            nc.scalar.activation(selT[:, b, :], bank_y[:, 0:P].bitcast(BF16), ACT.Copy).then_inc(s["selT_ready"], 1)
            nc.scalar.activation(gate_parts[:], bank_y[:, 256:259], ACT.Copy,
                                 accum_out=gate_slot[:, b:b + 1]).then_inc(s["gslot_ready"], 1)

        def act_hT(act, i):
            act.wait_ge(s["turned"], i + 1)
            nc.scalar.activation(hT.rearrange("p j s -> p (j s)"), bank_u[:, :], ACT.Copy).then_inc(s["hT_ready"], 1)

        def act_y(act, i, b):
            act.wait_ge(s["chunk_used"], (i + 1) * RING)
            act.wait_ge(s["gslot_ready"], i + 1)
            nc.scalar.activation(y_sb, bank_y[:, :], ACT.Copy, scale=gate_slot[:, b:b + 1]).then_inc(s["y_ready"], 1)

        def attention_at(u, part):
            return attn_parts[:, part, u // 2, (u % 2) * P:(u % 2 + 1) * P]

        def take_attention(dve, u):
            dve.wait_ge(s["attn_high"], u + 1)
            nc.vector.tensor_tensor(attention_at(u, 1), bank[7][:, 0:P], attention_at(u, 0),
                                    ALU.subtract).then_inc(s["attn_ready"], 1)

        def third_half(eng, ops, n):
            half = slice(n * HALF, (n + 1) * HALF)
            eng.wait_ge(s["part_a"], 2 * NT)
            ops.tensor_tensor(x_parts[:, 1, 2, half], rows_ffn[1][:, half], x_parts[:, 1, 1, half],
                              ALU.subtract).then_inc(s["parts_ready"], 1)

        def over_passes(eng, first, body, last, pairs=E // 2 - 1):
            first()
            with eng.Fori(0, pairs) as pair:
                body(pair * 2 + 1, pair * 2 + 1, 1)
                body(pair * 2 + 2, pair * 2 + 2, 0)
            last()

        def overflow(eng, body, end=None):
            eng.wait_ge(s["flag_ready"], 1)
            n = eng.value_load(flag[0:1, 0:1], min_val=0, max_val=T)
            with eng.If(n > SLOTS):
                with eng.Fori(0, E) as e:
                    for chunk in range(1, CHUNKS):
                        body(e * (CHUNKS - 1) + (E + chunk - 1), e, chunk)
                if end:
                    end()
            with eng.Else():
                pass

        block = ctx.enter_context(nc.Block())

        @block.sync
        def _(sp):
            row = 0
            for v, n in ((norm_mix, KD), (norm_ffn, KD), (norm_ple, KD), (conv_b, 4), (conv_ln_g, 4), (conv_ln_b, 4)):
                sp.dma_start(params_in[row:row + n, :], v[0].rearrange("(c p) -> c p", p=P)).then_inc(params_dma, 16)
                row += n
            sp.dma_start(taps_in, conv_w[0]).then_inc(params_dma, 16)

            def load_block(n):
                kind, b = BLOCKS[n]
                c0 = COL0[kind] + b * BLK
                if n >= FRONT:
                    wait_low(sp, n - FRONT)
                sp.dma_start(ring_low[:, n % FRONT, :].rearrange("p (k c) -> p k c", k=KD),
                             w_in_k[:, :, c0:c0 + BLK]).then_inc(block_dma[n], 16)

            for n in range(FRONT):
                load_block(n)
                if n == 1:
                    sp.dma_start(w_f[:], w_in_k[:, :, col_f:col_f + H]).then_inc(forget_dma, 16)
                    sp.dma_start(b_f[:], b_forget[0].rearrange("(h a) -> h a", a=1)).then_inc(forget_dma, 16)
            sp.dma_start(w_router_sb[:], w_router[0].rearrange("(k p) e -> p k e", p=P)).then_inc(router_dma, 16)
            sp.dma_start(b_router_sb[:], b_router[0].rearrange("(a e) -> a e", a=1).partition_broadcast(P)
                         ).then_inc(router_dma, 16)
            for n in range(FRONT, NB):
                load_block(n)
            for slot, src, got in ((AO_SLOT, w_attn_out, ao_dma), (CO_SLOT, w_conv_out, co_dma)):
                wait_low(sp, FRONT + slot + 1)
                sp.dma_start(ring_low[:, slot:slot + 2, :].rearrange("p s (k n) -> p (s k) n", n=D),
                             src[0].rearrange("(k p) n -> p k n", p=P)).then_inc(got, 16)
            for half in range(2):
                sp.wait_ge(s["block_done"], NB - 2 + half)
                rows = slice(half * 4, half * 4 + 4)
                sp.dma_start(w_o_sb[:, rows, :], w_o[0].rearrange("(k p) n -> p k n", p=P)[:, rows, :]
                             ).then_inc(wo_dma, 16)
            def load_first(c):
                rows = mats[c // PER_MAT][0, 0, (c % PER_MAT) * ROWS:(c % PER_MAT + 1) * ROWS, :]
                sp.dma_start(ring_slot(c).rearrange("p (k n) -> p k n", n=D),
                             rows.rearrange("(k p) n -> p k n", p=P)).then_inc(chunk_dma[c], 16)

            sp.wait_ge(s["block_done"], NB)
            for c in (8, 9):
                load_first(c)
            sp.wait_ge(s["silu_ready"], 1)
            for part in range(3):
                for m, bias in enumerate((b_gate, b_up)):
                    sp.dma_start(bias_in[part * E:(part + 1) * E, m * D:(m + 1) * D], bias[0]).then_inc(bias_dma, 16)
            for c in [2, 3, 6, 7, 0, 1, 4, 5, 10, 11]:
                if c == AO_SLOT:
                    sp.wait_ge(s["branch_a"], 1)
                    sp.dma_start(p_sb, p[0, 0].rearrange("(t p) d -> p t d", p=P)).then_inc(p_dma, 16)
                    sp.dma_start(b_down_sb, b_down[0]).then_inc(bdown_dma, 16)
                if c == 0:
                    sp.wait_ge(s["branch_c"], 4)
                load_first(c)
            sp.wait_ge(s["wo_tiles"], 1)
            sp.dma_start(w_proj_sb, w_ple_proj[0].rearrange("(k p) n -> p k n", p=P)).then_inc(proj_dma, 16)
            places_free = {E - 3: [("merged", 4)],
                           E - 2: [("bias_ready", 1), ("scores_done", 8), ("wo_done", NT)],
                           E - 1: [("wo_done", NT), ("logits_done", NT)]}
            for e, kept in kept_gate.items():
                for (first_tile, tiles, place), (done, count) in zip(kept, places_free[e]):
                    sp.wait_ge(s[done], count)
                    rows = w_gate[0, e, first_tile * P:(first_tile + tiles) * P, :]
                    sp.dma_start(place.rearrange("p (k n) -> p k n", n=D),
                                 rows.rearrange("(k p) n -> p k n", p=P)).then_inc(kept_dma, 16)
            with sp.Fori(1, E - 3) as i:
                load_chunks(sp, i, i)
            for i in kept_gate:
                load_chunks(sp, i, i, kept_chunks[i])
            overflow(sp, lambda i, e, chunk: load_chunks(sp, i, e),
                     lambda: sp.wait_ge(s["chunk_used"], E * CHUNKS * RING))
            for c in range(PER_MAT):
                sp.wait_ge(s["chunk_used"], (E - 1) * RING + c + 1)
                sp.dma_start(ring_slot(c).rearrange("p (k n) -> p k n", n=D),
                             w_ple_gate[0, c * ROWS:(c + 1) * ROWS, :].rearrange("(k p) n -> p k n", p=P)
                             ).then_inc(pgate_dma[c], 16)
            sp.dma_start(g_final, norm_final.rearrange("(a d) -> a d", a=1).partition_broadcast(P)
                         ).then_inc(final_dma, 16)
            sp.wait_ge(s["out_ready"], 2)
            sp.dma_start(out[0, 0:P, :], tok_tmp[:, 0, :]).then_inc(out_dma, 16)
            for n, done, count in ((0, "out_ready", 3), (1, "last_ready", 1)):
                sp.wait_ge(s[done], count)
                half = slice(n * HALF, (n + 1) * HALF)
                sp.dma_start(out[0, P:T, half], tok_tmp[:, 1, half]).then_inc(out_dma, 16)
            sp.wait_ge(out_dma, 16 * 3)

        @block.gpsimd
        def _(pool):
            n = [0]

            def const(ins):
                n[0] += 1
                ins.then_inc(s["consts"], 1)
                pool.wait_ge(s["consts"], n[0])

            def masked(t, op, fill, base, pattern, mult):
                const(nc.gpsimd.affine_select(out=t, in_=t, compare_op=op, fill=fill, base=base, pattern=pattern,
                                              channel_multiplier=mult))

            const(nc.gpsimd.memset(mhalf[:], -0.5))
            for t in (ident, ident_b):
                const(nc.gpsimd.memset(t[:], 0.0))
                masked(t[:], ALU.not_equal, 1.0, 0, [[-1, P]], 1)
            def power(ready, count, out, in_, done):
                pool.wait_ge(s[ready], count)
                nc.gpsimd.tensor_tensor(out, in_, mhalf[:, 0:out.shape[1]], ALU.pow).then_inc(s[done], 1)

            def power_rows(norm):
                for t in range(NT):
                    power("mean_sq", norm * NT + t + 1, stat[:, 4 + t:5 + t], stat[:, 2 + t:3 + t], "rstd")

            power_rows(0)
            const(nc.gpsimd.memset(ones_b[:], 1.0))
            const(nc.gpsimd.memset(ones_r[:], 1.0))
            const(nc.gpsimd.memset(z_pad[:, :, 0:PAD], 0.0))
            const(nc.gpsimd.memset(head_hot[:], 0.0))
            masked(head_hot[:], ALU.not_equal, 1.0, 0, [[-1, H]], 1)
            masked(head_hot[:], ALU.not_equal, 1.0, -32, [[-1, H]], 1)
            const(nc.gpsimd.memset(causal_b[:], 0.0))
            masked(causal_b[:], ALU.is_ge, NEG_INF, 0, [[-1, P]], 1)
            const(nc.gpsimd.memset(before_b[:], 1.0))
            masked(before_b[:], ALU.is_gt, 0.0, 0, [[1, P]], -1)
            const(nc.gpsimd.iota(slot_id[:].rearrange("p c a s -> p (c a s)"),
                                 pattern=[[SLOTS, CHUNKS], [0, 2], [1, SLOTS]], base=0, channel_multiplier=0,
                                 allow_small_or_imprecise_dtypes=True))
            const(nc.gpsimd.memset(expert_hot[:], 0.0))
            for part in range(3):
                masked(expert_hot[:], ALU.not_equal, 1.0, -part * E, [[-1, E]], 1)
            const(nc.gpsimd.memset(reg_f[:, 0:512], 0.0))
            assert n[0] == N_CONST, n[0]

            for n in range(V_LOW + 1, NB):
                low_part(pool, nc.gpsimd, n, "w_low_p")
            power("ln_step", 4, stat[:, 28:30], stat[:, 26:28], "ln_pow")
            for m in range(2):
                out_low(pool, nc.gpsimd, m, 0, "out_low_p")
            power_rows(1)
            pool.wait_ge(s["part_a"], 2 * NT - 1)
            nc.gpsimd.tensor_tensor(rows_ffn[1], rows_ffn[1], x_parts[:, 1, 0, :],
                                    ALU.subtract).then_inc(s["part_step"], 1)
            third_half(pool, nc.gpsimd, 0)
            for c in range(PER_MAT):
                gate_low(pool, nc.gpsimd, c, (0,) if c else (0, 1), "pg_low_p")
            power_rows(2)
            power_rows(3)

        @block.tensor
        def _(pe):
            pe.wait_ge(s["consts"], 5)
            pe_stay_warm(WARM)
            pe.wait_ge(params_dma, 16 * N_PARAM)
            nc.tensor.transpose(bank[0][:, 0:36], params_in[:], ident[0:36, 0:36])
            for m in range(4):
                last = nc.tensor.transpose(bank[0][:, 36 + m * TAPS:36 + (m + 1) * TAPS],
                                           taps_in[:, m * P:(m + 1) * P], ident[0:TAPS, 0:TAPS])
            last.then_inc(s["params_turned"], 1)

            for g in range(2 * NT):
                t, half = g // 2, g % 2
                pe.wait_ge(s["normed"], t + 1)
                for c in range(4):
                    k = half * 4 + c
                    last = nc.tensor.transpose(bank[4 + g][:, c * P:(c + 1) * P], rows_in[t][:, k * P:(k + 1) * P],
                                               ident[:])
                last.then_inc(s["x_turned"], 1)

            def project(n):
                kind, _ = BLOCKS[n]
                dst = bank[n % 2]
                pe.wait_ge(block_dma[n], 16)
                if n >= 2:
                    pe.wait_ge(s["block_out"], n - 1)
                else:
                    pe.wait_ge(s["params_ready"], 1)
                w = [w_part(n, part) for part in range(2)]
                x_ = [x_parts_r[:, part] for part in range(2)]
                if n == 0:
                    w, x_, products = [ring_low[:, 0, :].rearrange("p (k c) -> p k c", k=KD)], [hnT[:]], [(0, 0)]
                else:
                    pe.wait_ge(s["x_low"], 2)
                    wait_low(pe, n)
                    products = [(0, 0), (0, 1), (1, 0)]
                for j in range(2):
                    for k in range(KD):
                        for q, (wp, xp) in enumerate(products):
                            a, b = w[wp][:, k, j * P:(j + 1) * P], x_[xp][:, k, :]
                            if kind == "v":
                                a, b = x_[xp][:, k, j * P:(j + 1) * P], w[wp][:, k, :]
                            last = nc.tensor.matmul(dst[:, j * BLK:(j + 1) * BLK], a, b, start=k == 0 and q == 0,
                                                    stop=k == KD - 1 and q == len(products) - 1)
                last.then_inc(s["block_done"], 1)

            pe.wait_ge(s["hnT_ready"], 4)
            for n in range(4):
                project(n)
            pe.wait_ge(forget_dma, 16 * 2)
            for k in range(KD):
                last = nc.tensor.matmul(bank[2][0:H, 0:T], w_f[:, k, :], hnT[:, k, :], start=k == 0, stop=k == KD - 1)
            last.then_inc(s["forget_done"], 1)
            for n in range(4, FIRST_GATE):
                project(n)

            def scores(u, hh):
                hp, qb = u // 2, u % 2
                dst = bank[4 + u % 2]
                nk = (qb + 1) * P
                if hh:
                    pe.wait_ge(s["head_scored"], u + 1)
                else:
                    pe.wait_ge(s["cum_q_ready"], hp + 1)
                    if u == 0:
                        pe.wait_ge(s["block_out"], FIRST_GATE - 2)
                    if u >= 2:
                        pe.wait_ge(s["probs_exp"], 2 * (u - 1))
                row = slice(hh * HD, (hh + 1) * HD)
                o = dst[:, hh * 256:hh * 256 + nk]
                nc.tensor.matmul(o, qT[row, hp, qb * P:(qb + 1) * P], kT[row, hp, 0:nk], start=True, stop=False)
                nc.tensor.matmul(o, cum_q[:, hp % 2, hh, qb * P:(qb + 1) * P], cum_key[:, 0:nk],
                                 start=False, stop=False)
                nc.tensor.matmul(dst[:, hh * 256 + qb * P:hh * 256 + nk], ident_b[:], causal_b[:], start=False,
                                 stop=True).then_inc(s["scores_done" if hh else "head_scored"], 1)

            def turn_probs(u):
                qb = u % 2
                pe.wait_ge(s["probs_norm"], u + 1)
                if u >= 1:
                    pe.wait_ge(s["probsT_ready"], u)
                for hh in range(2):
                    for kb in range(qb + 1):
                        last = nc.tensor.transpose(bank[6][:, (2 * hh + kb) * P:(2 * hh + kb + 1) * P],
                                                   probs[:, u % 2, hh, kb * P:(kb + 1) * P], ident[:])
                last.then_inc(s["probs_turned"], 1)

            def attend(u):
                hp, qb = u // 2, u % 2
                pe.wait_ge(s["probsT_ready"], u + 1)
                if u >= 1:
                    pe.wait_ge(s["attn_ready"], u)
                for kb in range(qb + 1):
                    for hh in range(2):
                        last = nc.tensor.matmul(bank[7][hh * HD:(hh + 1) * HD, 0:P],
                                                v_sb[:, kb, hp * P + hh * HD:hp * P + (hh + 1) * HD],
                                                probsT[:, u % 2, 2 * hh + kb, :], start=kb == 0, stop=kb == qb)
                last.then_inc(s["pv_done"], 1)

            def conv_to_tokens():
                pe.wait_ge(s["conv_step"], 4 * TAPS)
                for t in range(NT):
                    for m in range(4):
                        last = nc.tensor.transpose(bank[2 + t][:, m * P:(m + 1) * P], conv[:, m, t * P:(t + 1) * P],
                                                   ident[:])
                    last.then_inc(s["conv_turned"], 1)

            def conv_to_channels():
                pe.wait_ge(s["ln_ready"], 2)
                for m in range(4):
                    for t in range(NT):
                        last = nc.tensor.transpose(bank[2 + m // 2][:, (m % 2) * T + t * P:(m % 2) * T + (t + 1) * P],
                                                   ln_out[:, t, m * P:(m + 1) * P], ident[:])
                    if m % 2:
                        last.then_inc(s["ln_back"], 1)

            scores(0, 0)
            scores(0, 1)
            for u in range(8):
                project(FIRST_GATE + u)
                if u < 7:
                    scores(u + 1, 0)
                turn_probs(u)
                if u < 7:
                    scores(u + 1, 1)
                if u >= 1:
                    attend(u - 1)
                if u == 5:
                    conv_to_tokens()
            conv_to_channels()
            attend(7)

            def branch(first_bank, mat, parts, ready, counts, done):
                for m in range(KD):
                    for k in range(KA):
                        if m == 0:
                            pe.wait_ge(s["out_low_p" if k < 2 else "out_low_v"], mat + 1)
                            pe.wait_ge(s[ready], counts[k])
                        for q, (wp, xp) in enumerate(((0, 0), (0, 1), (1, 0))):
                            last = nc.tensor.matmul(bank[first_bank + m // 2][:, (m % 2) * T:(m % 2 + 1) * T],
                                                    out_part(mat, wp)[:, k, m * P:(m + 1) * P], parts[:, xp, k, :],
                                                    start=k == 0 and q == 0, stop=k == KA - 1 and q == 2)
                    if m % 2 and done == "branch_c":
                        last.then_inc(s[done], 1)
                if done == "branch_a":
                    last.then_inc(s[done], 1)

            branch(4, 0, attn_parts, "attn_ready", (2, 4, 6, 8), "branch_a")
            pe.wait_ge(s["block_out"], NB)
            branch(0, 1, conv_parts, "silu_ready", (1,) * KA, "branch_c")
            pe.wait_ge(wo_dma, 32)
            pe.wait_ge(s["merge_step"], 4)

            def project_out(t, pairs):
                for d in pairs:
                    pe.wait_ge(s["merged"], d + 1)
                    for k in (2 * d, 2 * d + 1):
                        for n in range(2):
                            last = nc.tensor.matmul(bank[4 + 2 * t + n][:, :], sig_a[:, k, t * P:(t + 1) * P],
                                                    w_o_sb[:, k, n * HALF:(n + 1) * HALF], start=k == 0,
                                                    stop=k == KD - 1)
                return last

            def turn_rows(t, half, ready, count):
                pe.wait_ge(s[ready], count)
                for c in range(4):
                    k = half * 4 + c
                    last = nc.tensor.transpose(bank[4 + 2 * t + half][:, c * P:(c + 1) * P],
                                               h[:, t, k * P:(k + 1) * P], ident[:])
                last.then_inc(s["x_turned"], 1)

            def route_logits(t, half):
                pe.wait_ge(s["hnT_ready"], 5 + 2 * t + half)
                for k in range(4 * half, 4 * half + 4):
                    last = nc.tensor.matmul(bank[t][:, 0:E], hnT[:, k, t * P:(t + 1) * P], w_router_sb[:, k, :],
                                            start=k == 0, stop=k == KD - 1)
                if half:
                    last.then_inc(s["logits_done"], 1)

            def ple_project(t, steps):
                for n, k in steps:
                    last = nc.tensor.matmul(ple_bank[t][n][:, :], pT[:, k, t * P:(t + 1) * P],
                                            w_proj_sb[:, k, n * HALF:(n + 1) * HALF], start=k == 0, stop=k == KP - 1)
                return last

            ple_steps = [(n, k) for n in range(2) for k in range(KP)]
            project_out(0, range(4)).then_inc(s["wo_done"], 1)
            pe.wait_ge(p_dma, 16)
            for k in range(KP):
                for t in range(NT):
                    last = nc.tensor.transpose(bank[3][:, k * T + t * P:k * T + (t + 1) * P],
                                               p_sb[:, t, k * P:(k + 1) * P], ident[:])
            last.then_inc(s["pple_turned"], 1)
            project_out(1, range(2))
            for half in range(2):
                turn_rows(0, half, "h_mid", half + 1)
            project_out(1, (2,)).then_inc(s["wo_tiles"], 1)
            project_out(1, (3,)).then_inc(s["wo_done"], 1)
            pe.wait_ge(router_dma, 32)
            route_logits(0, 0)
            turn_rows(1, 0, "h_mid", 3)
            turn_rows(1, 1, "h_mid", 4)
            route_logits(0, 1)
            route_logits(1, 0)
            route_logits(1, 1)
            pe.wait_ge(s["pT_ready"], 1)
            pe.wait_ge(proj_dma, 16)
            ple_project(0, ple_steps).then_inc(s["proj_done"], 1)
            pe.wait_ge(s["routed_ready"], 2)
            nc.tensor.matmul(bank[2][:, 0:E], before_b[:], routed[:, 0, :], start=True, stop=True)
            nc.tensor.matmul(bank[2][:, E:2 * E], ones_b[:], routed[:, 0, :], start=True, stop=False)
            nc.tensor.matmul(bank[2][:, E:2 * E], before_b[:], routed[:, 1, :], start=False, stop=True)
            for t in range(NT):
                last = nc.tensor.matmul(bank[2][0:1, 2 * E:3 * E], ones_b[:, 0:1], routed[:, t, :], start=t == 0,
                                        stop=t == NT - 1)
            last.then_inc(s["rank_done"], 1)
            ple_project(1, ple_steps[:2])

            def gather(i, e, b):
                pe_gather(pe, i, b)
                pe_gather_gates(i, e, b)

            def start_sums():
                pe.wait_ge(s["ple_ready"], 2)
                pe.wait_ge(s["gatesT_ready"], 1)
                pe.wait_ge(s["flag_ready"], 1)
                pe.wait_ge(bdown_dma, 16)
                for t in range(NT):
                    for n in range(2):
                        nc.tensor.matmul(acc_bank[t][n][:, :], gatesT[:, t * P:(t + 1) * P],
                                         b_down_sb[:, n * HALF:(n + 1) * HALF], start=True, stop=True)

            def first_pass():
                pe.wait_ge(s["parts_ready"], 3)
                pe_gather(pe, 0, 0).then_inc(s["first_rows"], 1)
                ple_project(1, ple_steps[2:3])
                pe.wait_ge(s["ple_ready"], 1)
                pe.wait_ge(s["bias_ready"], 1)
                pe_expand(pe, 0, 0, 0)
                pe.wait_ge(s["gates3_ready"], 1)
                pe_gather_gates(0, 0, 0)
                for t in range(NT):
                    last = nc.tensor.transpose(bank[3][0:E, t * P:(t + 1) * P], gate_w[:, t, :], ident[:])
                last.then_inc(s["gatesT_done"], 1)
                ple_project(1, ple_steps[3:]).then_inc(s["proj_done"], 1)
                pe_expand(pe, 0, 0, 1)
                pe.wait_ge(s["gslot_ready"], 1)
                gather(1, 1, 1)
                pe_turn(pe, 0)
                pe_down(pe, 0, 2)
                start_sums()

            def one(i, e, b, kept=(), before=0):
                pe_expand(pe, i, b, 0, kept, before)
                pe_expand(pe, i, b, 1)
                pe_combine(pe, i - 1, 1 - b)
                gather(i + 1, e + 1, 1 - b)
                pe_turn(pe, i)
                pe_down(pe, i, i + 2)

            def last_one():
                i, b = E - 1, 1
                pe_expand(pe, i, b, 0, kept_gate[i], i)
                pe_expand(pe, i, b, 1)
                pe_combine_tile(pe, i - 1, 0, 0)
                pe_turn(pe, i)
                pe_combine_tile(pe, i - 1, 0, 1).then_inc(s["combined"], 1)
                pe_down(pe, i, E)
                pe_stay_warm(3)
                pe_combine_tile(pe, i, b, 0).then_inc(s["tile_combined"], 1)
                pe_combine_tile(pe, i, b, 1).then_inc(s["combined"], 1)

            def last_three():
                one(E - 3, E - 3, 1, kept_gate[E - 3], E - 3)
                one(E - 2, E - 2, 0, kept_gate[E - 2], E - 2)
                last_one()

            over_passes(pe, first_pass, one, last_three, pairs=E // 2 - 2)

            def further(i, e, chunk):
                gather(i, e, 0)
                pe_expand(pe, i, 0, 0, before=E)
                pe_expand(pe, i, 0, 1)
                pe_turn(pe, i)
                pe_down(pe, i, i + 1)
                pe_combine(pe, i, 0)

            overflow(pe, further)

            def turn_tail(t):
                for half in range(2):
                    turn_rows(t, half, "tail_h", 2 * t + half + 1)

            def ple_gate(piece, k):
                t, dst, col, width = piece
                for q, (xp, wp) in enumerate(((0, 0), (0, 1), (1, 0))):
                    lo = (k % 2) * D + col
                    last = nc.tensor.matmul(dst[:, 0:width], x_parts_r[:, xp, k, t * P:(t + 1) * P],
                                            gate_part(k // 2, wp)[:, lo:lo + width],
                                            start=k == 0 and q == 0, stop=k == KD - 1 and q == 2)
                return last

            turn_tail(0)
            pe_stay_warm(10)
            for k in range(KD):
                if k == 4:
                    turn_tail(1)
                pe.wait_ge(s["pg_low_p"], k // 2 + 1)
                if k >= 2:
                    pe.wait_ge(s["pg_low_v"], k // 2)
                if k % 4 == 0:
                    pe.wait_ge(s["x_low"], 3 + k // 4)
                for piece in pieces[:2]:
                    last = ple_gate(piece, k)
                    if k == KD - 1:
                        last.then_inc(s["tail_pg"], 1)
            for piece in pieces[2:]:
                for k in range(KD):
                    if piece is pieces[2] and k % 4 == 0:
                        pe.wait_ge(s["x_low"], 5 + k // 4)
                    last = ple_gate(piece, k)
                last.then_inc(s["tail_pg"], 1)

        @block.scalar
        def _(act):
            for t in range(NT):
                act.dma_start(h[:, t, :], x[0, t * P:(t + 1) * P, :]).then_inc(x_dma[t], 16)

            def square(t, dump):
                nc.scalar.activation(dump, h[:, t, :], ACT.Square, accum_out=stat[:, t:t + 1]).then_inc(s["sumsq"], 1)

            for t in range(NT):
                act.wait_ge(x_dma[t], 16)
                square(t, tok_tmp[:, t, :])
            act.wait_ge(s["params_ready"], 1)
            act.wait_ge(s["x_turned"], 2)
            for c in range(4):
                last = nc.scalar.activation(hnT[:, 4 + c, 0:P], bank[5][:, c * P:(c + 1) * P], ACT.Copy,
                                            scale=g_mix[:, 4 + c:5 + c])
            last.then_inc(s["hnT_ready"], 1)

            F_AFTER = 5

            def high_part(n):
                act.wait_ge(block_dma[n], 16)
                if n > 3:
                    act.wait_ge(s["block_done"], n - 2)
                nc.scalar.activation(w_part(n, 0), ring_low[:, n % FRONT, :].rearrange("p (k c) -> p k c", k=KD),
                                     ACT.Copy).then_inc(s["w_high"], 1)

            act.wait_ge(s["hnT_ready"], 4)
            for half in range(2):
                rows = slice(half * 4, half * 4 + 4)
                nc.scalar.activation(x_parts_r[:, 0, rows, :], hnT[:, rows, :], ACT.Copy).then_inc(s["x_high"], 1)
            for n in range(1, 4):
                high_part(n)

            def read_out(n):
                kind, b = BLOCKS[n]
                act.wait_ge(s["block_done"], n + 1)
                src = bank[n % 2][:, :].rearrange("p (j t) -> p j t", j=2)
                if kind == "v":
                    dst = v_sb[:, :, b * BLK:(b + 1) * BLK]
                elif kind == "ca":
                    dst = z_pad[:, 2 * b:2 * b + 2, PAD:]
                elif kind == "cg":
                    dst = glu_sig
                else:
                    dst = {"q": qT, "k": kT, "ga": sig_a, "gc": sig_c}[kind][:, 2 * b:2 * b + 2, :]
                if kind == "cg" and b:
                    act.wait_ge(s["z_ready"], b)
                nc.scalar.activation(dst, src, ACT.Sigmoid if kind == "cg" else ACT.Copy).then_inc(s["block_out"], 1)

            for n in range(FIRST_GATE):
                read_out(n)
                if n:
                    high_part(n + 3)
                if n == F_AFTER:
                    act.wait_ge(s["f_steps"], 3)
                    nc.scalar.activation(f_tmp[:, 3, :], f_tmp[:, 2, :], ACT.Exp, scale=-1.0).then_inc(s["f_exp"], 1)
                    act.wait_ge(s["f_exp"], 1)
                    nc.scalar.activation(f_tmp[:, 4, :], f_tmp[:, 3, :], ACT.Ln, bias=1.0).then_inc(s["f_ln"], 1)

            def attention_high(u):
                act.wait_ge(s["pv_done"], u + 1)
                nc.scalar.activation(attention_at(u, 0), bank[7][:, 0:P], ACT.Copy).then_inc(s["attn_high"], 1)

            def out_high(m, half):
                act.wait_ge((ao_dma, co_dma)[m], 16)
                wait_low(act, FRONT + OUT_HIGH[m] + half if OUT_HIGH[m] else NB - 2 + half)
                nc.scalar.activation(ring_parts[:, OUT_HIGH[m] + half, :], ring_low[:, OUT_SLOT[m] + half, :],
                                     ACT.Copy).then_inc(s["out_high"], 1)

            for u in range(8):
                nk = (u % 2 + 1) * P
                act.wait_ge(s["row_max"], u + 1)
                if u >= 2:
                    act.wait_ge(s["probs_turned"], u - 1)
                for hh in range(2):
                    nc.scalar.activation(probs[:, u % 2, hh, 0:nk], bank[4 + u % 2][:, hh * 256:hh * 256 + nk],
                                         ACT.Exp, bias=sm_stat[:, u % 2, 2 + hh:3 + hh], scale=SCALE,
                                         accum_out=sm_stat[:, u % 2, 4 + hh:5 + hh]).then_inc(s["probs_exp"], 1)
                read_out(FIRST_GATE + u)
                act.wait_ge(s["probs_turned"], u + 1)
                if u >= 2:
                    act.wait_ge(s["pv_done"], u - 1)
                kbs = u % 2 + 1
                nc.scalar.activation(probsT[:, u % 2].rearrange("p (a k) q -> p a k q", a=2)[:, :, 0:kbs, :],
                                     bank[6][:, :].rearrange("p (a k q) -> p a k q", a=2, k=2)[:, :, 0:kbs, :],
                                     ACT.Copy).then_inc(s["probsT_ready"], 1)
                if u:
                    attention_high(u - 1)
                if FIRST_GATE + u + 3 < NB:
                    high_part(FIRST_GATE + u + 3)
                if u >= 5:
                    for m, half in {5: [(0, 0), (0, 1)], 6: [(1, 0)], 7: [(1, 1)]}[u]:
                        out_high(m, half)
            attention_high(7)

            for m in range(4):
                act.wait_ge(s["ln_step"], 5 + m)
                nc.scalar.activation(silu_sig[:, m, :], conv[:, m, :], ACT.Sigmoid).then_inc(s["silu_arg"], 1)
            act.wait_ge(s["silu_out"], 1)
            nc.scalar.activation(conv_parts[:, 0], conv, ACT.Copy).then_inc(s["conv_high"], 1)
            act.wait_ge(s["block_out"], NB)
            for t_ in (sig_a, sig_c):
                v = t_.rearrange("p j t -> p (j t)")
                nc.scalar.activation(v, v, ACT.Sigmoid).then_inc(s["gates_sig"], 1)

            def ple_out(t):
                act.wait_ge(s["proj_done"], t + 1)
                for n in range(2):
                    last = nc.scalar.activation(ple_v[:, t, n * HALF:(n + 1) * HALF], ple_bank[t][n][:, :], ACT.Copy)
                last.then_inc(s["ple_ready"], 1)

            def bf16_part(t, part, ready, count):
                act.wait_ge(s[ready], count)
                nc.scalar.activation(x_parts[:, t, part, :], rows_ffn[t], ACT.Copy).then_inc(s["part_a"], 1)

            def route_exp(t):
                act.wait_ge(s["f_neg"], t + 1)
                nc.scalar.activation(rest[:, t, :], rest[:, t, :], ACT.Exp).then_inc(s["route_exp"], 1)

            act.wait_ge(s["h_mid"], 2)
            square(0, rows_ffn[0])
            act.wait_ge(s["pple_turned"], 1)
            nc.scalar.activation(pT.rearrange("p k t -> p (k t)"), bank[3][:, :], ACT.Copy).then_inc(s["pT_ready"], 1)
            act.wait_ge(s["x_turned"], 5)
            bf16_part(0, 0, "normed", NT + 1)
            bf16_part(0, 1, "part_step", 1)
            act.wait_ge(s["h_mid"], 4)
            square(1, rows_ffn[1])
            bf16_part(1, 0, "normed", NT + 2)
            route_exp(0)
            bf16_part(1, 1, "part_step", 2)
            route_exp(1)
            ple_out(0)

            def first_pass():
                act.wait_ge(s["proj_done"], 2)
                act_sigmoid(act, 0)
                act_selT(act, 0, 0)
                act.wait_ge(s["gatesT_done"], 1)
                nc.scalar.activation(gatesT, bank[3][0:E, 0:T], ACT.Copy).then_inc(s["gatesT_ready"], 1)
                ple_out(1)
                act_selT(act, 1, 1)
                act_hT(act, 0)
                act_y(act, 0, 0)

            def one(i, e, b):
                act_sigmoid(act, i)
                act_selT(act, i + 1, 1 - b)
                act_hT(act, i)
                act_y(act, i, b)

            def last_one():
                act_sigmoid(act, E - 1)
                act_hT(act, E - 1)
                act_y(act, E - 1, 1)

            over_passes(act, first_pass, one, last_one)

            def further(i, e, chunk):
                act_selT(act, i, 0)
                act_sigmoid(act, i)
                act_hT(act, i)
                act_y(act, i, 0)

            overflow(act, further)

            def gate_high(c):
                act.wait_ge(pgate_dma[c], 16)
                nc.scalar.activation(gate_part(c, 0), ring_low[:, c, :], ACT.Copy).then_inc(s["pg_high"], 1)

            def rows_high(g):
                t, half = g // 2, g % 2
                act.wait_ge(s["hnT_ready"], 9 + g)
                at = (slice(None), slice(half * 4, half * 4 + 4), slice(t * P, (t + 1) * P))
                nc.scalar.activation(x_parts_r[:, 0][at], hnT[at], ACT.Copy).then_inc(s["x_high"], 1)

            gate_high(0)
            gate_high(1)
            rows_high(0)
            rows_high(1)
            gate_high(2)
            act.wait_ge(s["tail_h"], 2)
            square(0, tok_tmp[:, 0, :])
            gate_high(3)
            rows_high(2)
            rows_high(3)
            act.wait_ge(s["tail_h"], 4)
            square(1, tok_tmp[:, 1, :])

            def gate_piece(q):
                t, src, col, width = pieces[q]
                act.wait_ge(s["tail_pg"], q + 1)
                act.wait_ge(s["rstd"], 2 * NT + t + 1)
                nc.scalar.activation(tok_tmp2[:, t, col:col + width], src[:, 0:width], ACT.Sigmoid,
                                     scale=stat[:, 4 + t:5 + t]).then_inc(s["tail_sig"], 1)

            def square_piece(q):
                t, _, col, width = pieces[q]
                act.wait_ge(s["tail_row"], q + 1)
                nc.scalar.activation(tok_tmp2[:, t, col:col + width], h[:, t, col:col + width], ACT.Square,
                                     accum_out=stat[:, 8 + q:9 + q]).then_inc(s["tail_sq"], 1)

            gate_piece(0)
            gate_piece(1)
            square_piece(0)
            square_piece(1)
            for q in range(2, len(pieces)):
                gate_piece(q)
                square_piece(q)
            act.wait_ge(s["rstd"], 3 * NT + 2)
            act.wait_ge(s["tail_gain"], len(pieces))
            nc.scalar.activation(tok_tmp[:, 1, HALF:D], tok_tmp[:, 1, HALF:D], ACT.Copy,
                                 scale=stat[:, 5:6]).then_inc(s["last_ready"], 1)

        @block.vector
        def _(dve):
            def mean_square(t0, t1, count):
                dve.wait_ge(s["sumsq"], count)
                nc.vector.tensor_scalar(stat[:, 2 + t0:2 + t1], stat[:, t0:t1], 1.0 / D, RMS_EPS, ALU.mult,
                                        ALU.add).then_inc(s["mean_sq"], 1)

            def normalise(t, count, rows):
                dve.wait_ge(s["rstd"], count)
                nc.vector.tensor_scalar(rows[t], h[:, t, :], stat[:, 4 + t:5 + t], None,
                                        ALU.mult).then_inc(s["normed"], 1)

            def take_turned(g, gain, count):
                t, half = g // 2, g % 2
                dve.wait_ge(s["x_turned"], count)
                nc.vector.tensor_tensor(hnT[:, half * 4:half * 4 + 4, t * P:(t + 1) * P],
                                        bank[4 + g][:, :].rearrange("p (c q) -> p c q", c=4),
                                        bcast(gain[:, half * 4:half * 4 + 4], P), ALU.mult).then_inc(s["hnT_ready"], 1)

            for t in range(NT):
                mean_square(t, t + 1, t + 1)
                if t == NT - 1:
                    dve.wait_ge(s["params_turned"], 1)
                    nc.vector.tensor_copy(params[:], bank[0][:, 0:36 + 4 * TAPS]).then_inc(s["params_ready"], 1)
                normalise(t, t + 1, rows_in)
            dve.wait_ge(s["params_ready"], 1)
            for g in (0, 2, 3):
                take_turned(g, g_mix, g + 1)

            for half in range(2):
                dve.wait_ge(s["x_high"], half + 1)
                rows = slice(half * 4, half * 4 + 4)
                nc.vector.tensor_tensor(x_parts_r[:, 1, rows, :], hnT[:, rows, :], x_parts_r[:, 0, rows, :],
                                        ALU.subtract).then_inc(s["x_low"], 1)
            for n in range(1, V_LOW + 1):
                low_part(dve, nc.vector, n, "w_low_v")

            dve.wait_ge(s["consts"], N_CONST)
            nc.vector.memset(cum_base[0:H, :], 1.0).then_inc(s["cum_steps"], 1)
            nc.vector.memset(cum_key[32:32 + H, :], 1.0).then_inc(s["cum_steps"], 1)

            def glu(b):
                dve.wait_ge(s["block_out"], 2 * b + 2)
                z = z_pad[:, 2 * b:2 * b + 2, PAD:]
                nc.vector.tensor_tensor(z, z, glu_sig, ALU.mult).then_inc(s["z_ready"], 1)
                dve.wait_ge(s["z_ready"], b + 1)

            def convolve(b, taps):
                for j in taps:
                    for m in (2 * b, 2 * b + 1):
                        n = 2 * TAPS * b + 2 * j + m % 2
                        if j:
                            dve.wait_ge(s["conv_step"], n - 1)
                            ins = nc.vector.scalar_tensor_tensor(out=conv[:, m, :], in0=z_pad[:, m, j:j + T],
                                                                 scalar=tap(j, m), in1=conv[:, m, :], op0=ALU.mult,
                                                                 op1=ALU.add)
                        else:
                            ins = nc.vector.tensor_scalar(conv[:, m, :], z_pad[:, m, 0:T], tap(0, m), cb[:, m:m + 1],
                                                          ALU.mult, ALU.add)
                        ins.then_inc(s["conv_step"], 1)

            glu(0)
            convolve(0, range(TAPS))

            dve.wait_ge(s["forget_done"], 1)
            nc.vector.tensor_scalar(f_tmp[:, 0, :], bank[2][0:H, 0:T], b_f[:, 0:1], None,
                                    ALU.add).then_inc(s["f_steps"], 1)
            dve.wait_ge(s["f_steps"], 1)
            nc.vector.tensor_scalar(f_tmp[:, 1, :], f_tmp[:, 0, :], 0.0, None, ALU.min).then_inc(s["f_steps"], 1)
            nc.vector.scalar_tensor_tensor(out=f_tmp[:, 2, :], in0=f_tmp[:, 0, :], scalar=-1.0, in1=f_tmp[:, 0, :],
                                           op0=ALU.mult, op1=ALU.max).then_inc(s["f_steps"], 1)
            dve.wait_ge(s["f_ln"], 1)
            nc.vector.tensor_tensor(f_tmp[:, 5, :], f_tmp[:, 1, :], f_tmp[:, 4, :],
                                    ALU.subtract).then_inc(s["f_steps"], 1)
            dve.wait_ge(s["f_steps"], 4)
            dve.wait_ge(s["cum_steps"], 2)
            nc.vector.tensor_tensor_scan(f_tmp[:, 0, :], cum_base[0:H, :], f_tmp[:, 5, :], 0.0, ALU.mult,
                                         ALU.add).then_inc(s["f_steps"], 1)
            dve.wait_ge(s["f_steps"], 5)
            nc.vector.tensor_scalar(cum_base[32:32 + H, :], f_tmp[:, 0, :], 1.0 / SCALE, None,
                                    ALU.mult).then_inc(s["cum_steps"], 1)
            nc.vector.tensor_scalar(cum_key[0:H, :], f_tmp[:, 0, :], -1.0 / SCALE, None,
                                    ALU.mult).then_inc(s["cum_steps"], 1)
            dve.wait_ge(s["cum_steps"], 4)

            def spread(hp):
                if hp >= 2:
                    dve.wait_ge(s["scores_done"], 2 * (hp - 1))
                for hh in range(2):
                    last = nc.vector.tensor_scalar(cum_q[:, hp % 2, hh, :], cum_base, head_hot[:, 2 * hp + hh:2 * hp + hh + 1],
                                                   None, ALU.mult)
                last.then_inc(s["cum_q_ready"], 1)

            spread(0)
            spread(1)
            TAPS_FIRST, TAPS_UNIT = 15, 4
            glu(1)
            convolve(1, range(TAPS_FIRST))

            def softmax(u):
                b, hp, qb = u % 2, u // 2, u % 2
                nk = (qb + 1) * P
                dve.wait_ge(s["scores_done"], u + 1)
                nc.vector.tensor_reduce(sm_stat[:, b, 0:2],
                                        bank[4 + b][:, :].rearrange("p (a k) -> p a k", a=2)[:, :, 0:nk], AX_X,
                                        ALU.max).then_inc(s["rows_recip"], 1)
                dve.wait_ge(s["rows_recip"], 2 * u + 1)
                nc.vector.tensor_scalar(sm_stat[:, b, 2:4], sm_stat[:, b, 0:2], -SCALE, None,
                                        ALU.mult).then_inc(s["row_max"], 1)
                if qb and hp + 2 < 4:
                    spread(hp + 2)
                dve.wait_ge(s["probs_exp"], 2 * u + 2)
                nc.vector.reciprocal(sm_stat[:, b, 0:2], sm_stat[:, b, 4:6]).then_inc(s["rows_recip"], 1)
                dve.wait_ge(s["rows_recip"], 2 * u + 2)
                for hh in range(2):
                    last = nc.vector.tensor_scalar(probs[:, b, hh, 0:nk], probs[:, b, hh, 0:nk],
                                                   sm_stat[:, b, hh:hh + 1], None, ALU.mult)
                last.then_inc(s["probs_norm"], 1)
                if u == 6:
                    out_low(dve, nc.vector, 0, 1, "out_low_v")
                if u:
                    take_attention(dve, u - 1)

            def ln_stats():
                for t in range(NT):
                    dve.wait_ge(s["conv_turned"], t + 1)
                    nc.vector.bn_stats(stat[:, 8 + 6 * t:14 + 6 * t], bank[2 + t][:, :]).then_inc(s["ln_step"], 1)
                dve.wait_ge(s["ln_step"], 2)
                for t in range(NT):
                    last = nc.vector.bn_aggr(stat[:, 20 + 2 * t:22 + 2 * t], stat[:, 8 + 6 * t:14 + 6 * t])
                last.then_inc(s["ln_step"], 1)
                dve.wait_ge(s["ln_step"], 3)
                nc.vector.tensor_scalar(stat[:, 26:28], stat[:, 20:24].rearrange("p (t v) -> p t v", v=2)[:, :, 1],
                                        LN_EPS, None, ALU.add).then_inc(s["ln_step"], 1)

            def ln_apply():
                dve.wait_ge(s["ln_pow"], 1)
                dve.wait_ge(s["scores_done"], 8)
                for t in range(NT):
                    nc.vector.tensor_scalar(ln_out[:, t, :], bank[2 + t][:, :], stat[:, 20 + 2 * t:21 + 2 * t],
                                            stat[:, 28 + t:29 + t], ALU.subtract, ALU.mult).then_inc(s["ln_ready"], 1)

            for u in range(8):
                softmax(u)
                convolve(1, range(min(TAPS, TAPS_FIRST + TAPS_UNIT * u), min(TAPS, TAPS_FIRST + TAPS_UNIT * (u + 1))))
                if u == 5:
                    ln_stats()
                if u == 6:
                    ln_apply()
            take_attention(dve, 7)
            for m in range(4):
                dve.wait_ge(s["ln_back"], m // 2 + 1)
                nc.vector.tensor_scalar(conv[:, m, :], bank[2 + m // 2][:, (m % 2) * T:(m % 2 + 1) * T],
                                        lg[:, m:m + 1], lb[:, m:m + 1], ALU.mult, ALU.add).then_inc(s["ln_step"], 1)
            out_low(dve, nc.vector, 1, 1, "out_low_v")
            dve.wait_ge(s["silu_arg"], 4)
            dve.wait_ge(s["ln_step"], 8)
            nc.vector.tensor_tensor(conv, conv, silu_sig, ALU.mult).then_inc(s["silu_out"], 1)
            dve.wait_ge(s["conv_high"], 1)
            nc.vector.tensor_tensor(conv_parts[:, 1], conv, conv_parts[:, 0], ALU.subtract).then_inc(s["silu_ready"], 1)

            dve.wait_ge(s["branch_a"], 1)
            dve.wait_ge(s["gates_sig"], 2)
            for m in range(4):
                v = sig_a[:, 2 * m:2 * m + 2, :].rearrange("p j t -> p (j t)")
                nc.vector.tensor_tensor(v, v, bank[4 + m][:, :], ALU.mult).then_inc(s["merge_step"], 1)
            def merge(m):
                va = sig_a[:, 2 * m:2 * m + 2, :].rearrange("p j t -> p (j t)")
                vc = sig_c[:, 2 * m:2 * m + 2, :].rearrange("p j t -> p (j t)")
                dve.wait_ge(s["branch_c"], m + 1)
                nc.vector.tensor_tensor(vc, vc, bank[m][:, :], ALU.mult).then_inc(s["merge_step"], 1)
                dve.wait_ge(s["merge_step"], 5 + m)
                nc.vector.tensor_tensor(va, va, vc, ALU.add).then_inc(s["merged"], 1)

            def link(ins, name, count):
                count[0] += 1
                ins.then_inc(s[name], 1)
                dve.wait_ge(s[name], count[0])

            bstep = [0]
            dve.wait_ge(bias_dma, 16 * 6)
            link(nc.vector.tensor_copy(bias3, bias_in), "bias_part", bstep)
            merge(0)
            link(nc.vector.tensor_tensor(bias_in, bias_in, bias3, ALU.subtract), "bias_part", bstep)
            merge(1)
            link(nc.vector.tensor_copy(bias3[E:2 * E], bias_in[E:2 * E]), "bias_part", bstep)
            link(nc.vector.tensor_copy(bias3[2 * E:3 * E], bias_in[2 * E:3 * E]), "bias_part", bstep)
            merge(2)
            link(nc.vector.tensor_tensor(bias_in[2 * E:3 * E], bias_in[2 * E:3 * E], bias3[2 * E:3 * E],
                                         ALU.subtract), "bias_part", bstep)
            merge(3)
            nc.vector.tensor_copy(bias3[2 * E:3 * E], bias_in[2 * E:3 * E]).then_inc(s["bias_ready"], 1)

            rstep = [0]

            def route(ins):
                link(ins, "route_step", rstep)

            def top(t):
                lg_ = logits[:, t, :]
                dve.wait_ge(s["rstd"], NT + t + 1)
                dve.wait_ge(s["logits_done"], t + 1)
                dve.wait_ge(router_dma, 32)
                route(nc.vector.scalar_tensor_tensor(out=lg_, in0=bank[t][:, 0:E], scalar=stat[:, 4 + t:5 + t],
                                                     in1=b_router_sb[:], op0=ALU.mult, op1=ALU.add))
                route(nc.vector.max(top8[:, t, :], lg_))
                route(nc.vector.tensor_scalar(above[:, t, :], lg_, top8[:, t, 3:4], None, ALU.is_gt))
                route(nc.vector.tensor_scalar(ties[:, t, :], lg_, top8[:, t, 3:4], None, ALU.is_equal))
                route(nc.vector.reduce_sum(stat[:, 6 + t:7 + t], above[:, t, :], AX_X))

            def choose(t):
                route(nc.vector.tensor_tensor_scan(tie_no[:, t, :], ones_e[:, t, :], ties[:, t, :],
                                                   stat[:, 6 + t:7 + t], ALU.mult, ALU.add))
                route(nc.vector.scalar_tensor_tensor(out=ties[:, t, :], in0=tie_no[:, t, :], scalar=4.0,
                                                     in1=ties[:, t, :], op0=ALU.is_le, op1=ALU.mult))
                nc.vector.tensor_tensor(routed[:, t, :], above[:, t, :], ties[:, t, :],
                                        ALU.add).then_inc(s["routed_ready"], 1)
                nc.vector.tensor_scalar(rest[:, t, :], logits[:, t, :], top8[:, t, 0:1], None,
                                        ALU.subtract).then_inc(s["f_neg"], 1)

            def weigh(t):
                dve.wait_ge(s["route_exp"], t + 1)
                dve.wait_ge(s["routed_ready"], t + 1)
                route(nc.vector.tensor_tensor(gate_w[:, t, :], rest[:, t, :], routed[:, t, :], ALU.mult))
                route(nc.vector.reduce_sum(stat[:, 6 + t:7 + t], gate_w[:, t, :], AX_X))
                route(nc.vector.reciprocal(stat[:, 24 + t:25 + t], stat[:, 6 + t:7 + t]))
                route(nc.vector.tensor_scalar(gate_w[:, t, :], gate_w[:, t, :], stat[:, 24 + t:25 + t], None,
                                              ALU.mult))

            def add_mixers(t):
                dve.wait_ge(s["wo_done"], t + 1)
                for n in range(2):
                    v = h[:, t, n * HALF:(n + 1) * HALF]
                    nc.vector.tensor_tensor(v, v, bank[4 + 2 * t + n][:, :], ALU.add).then_inc(s["h_mid"], 1)

            def take_rows(t):
                for g in (2 * t, 2 * t + 1):
                    take_turned(g, g_ffn, 5 + g)

            route(nc.vector.memset(ones_e, 1.0))
            add_mixers(0)
            mean_square(0, 1, NT + 1)
            normalise(0, NT + 1, rows_ffn)
            take_rows(0)
            dve.wait_ge(s["part_a"], 1)
            nc.vector.tensor_tensor(rows_ffn[0], rows_ffn[0], x_parts[:, 0, 0, :],
                                    ALU.subtract).then_inc(s["part_step"], 1)
            dve.wait_ge(s["part_a"], 2)
            nc.vector.tensor_tensor(x_parts[:, 0, 2, :], rows_ffn[0], x_parts[:, 0, 1, :],
                                    ALU.subtract).then_inc(s["parts_ready"], 1)
            add_mixers(1)
            take_rows(1)
            mean_square(1, 2, NT + 2)
            normalise(1, NT + 2, rows_ffn)
            top(0)
            choose(0)
            top(1)
            choose(1)
            dve.wait_ge(s["rank_done"], 1)
            route(nc.vector.scalar_tensor_tensor(out=ranks[:], in0=bank[2][:, 0:NT * E].rearrange("p (t e) -> p t e", t=NT),
                                                 scalar=1.0, in1=routed[:], op0=ALU.add, op1=ALU.mult))
            nc.vector.tensor_scalar(ranks[:], ranks[:], -1.0, None, ALU.add).then_inc(s["ranks_ready"], 1)
            dve.wait_ge(s["ranks_ready"], 1)

            def first():
                dve_select(dve, 0, 0, 0, 0, 2)
                third_half(dve, nc.vector, 1)
                weigh(0)
                weigh(1)
                dve_take(dve, 0, 0, "first_rows")
                route(nc.vector.tensor_copy(gates3[:, :, :, 0], gate_w))
                route(nc.vector.tensor_tensor(rest, gate_w, gates3[:, :, :, 0], ALU.subtract))
                route(nc.vector.tensor_copy(gates3[:, :, :, 1], rest))
                route(nc.vector.tensor_tensor(gates3[:, :, :, 2], rest, gates3[:, :, :, 1], ALU.subtract))
                nc.vector.memset(flag_f[:], 0.0).then_inc(s["gates3_ready"], 1)
                dve.wait_ge(s["gates3_ready"], 1)
                route(nc.vector.reduce_max(flag_f[:], bank[2][0:1, 2 * E:3 * E], AX_X))
                nc.vector.tensor_copy(flag[:], flag_f[:]).then_inc(s["flag_ready"], 1)

            def one(i, e, b):
                dve_select(dve, i + 1, e + 1, 1 - b, 0, 2)
                dve_activate(dve, i)
                dve_take(dve, i + 1, 1 - b)

            def first_pass():
                first()
                one(0, 0, 0)

            over_passes(dve, first_pass, one, lambda: dve_activate(dve, E - 1))

            def further(i, e, chunk):
                dve_select(dve, i, e, 0, chunk, 1)
                dve_take(dve, i, 0)
                dve_activate(dve, i)

            overflow(dve, further, lambda: dve.wait_ge(s["combined"], E * CHUNKS))

            def half_of(x_, t, n):
                return x_[:, t, n * HALF:(n + 1) * HALF]

            def add_experts(t, done, count):
                dve.wait_ge(s[done], count)
                for n in range(2):
                    nc.vector.tensor_tensor(half_of(h, t, n), half_of(h, t, n), acc_bank[t][n][:, :],
                                            ALU.add).then_inc(s["tail_h"], 1)

            def rows_low(g):
                t, half = g // 2, g % 2
                dve.wait_ge(s["x_high"], 3 + g)
                at = (slice(None), slice(half * 4, half * 4 + 4), slice(t * P, (t + 1) * P))
                nc.vector.tensor_tensor(x_parts_r[:, 1][at], hnT[at], x_parts_r[:, 0][at],
                                        ALU.subtract).then_inc(s["x_low"], 1)

            add_experts(0, "tile_combined", 1)
            take_turned(0, g_ple, 9)
            take_turned(1, g_ple, 10)
            rows_low(0)
            rows_low(1)
            add_experts(1, "combined", E)
            for c in range(1, PER_MAT):
                gate_low(dve, nc.vector, c, (1,), "pg_low_v")
            take_turned(2, g_ple, 11)
            take_turned(3, g_ple, 12)
            rows_low(2)
            rows_low(3)
            for t in range(NT):
                mean_square(t, t + 1, 2 * NT + t + 1)
            dve.wait_ge(final_dma, 16)
            for q, (t, _, col, width) in enumerate(pieces):
                part = slice(col, col + width)
                gate, row, result = tok_tmp2[:, t, part], h[:, t, part], tok_tmp[:, t, part]
                dve.wait_ge(s["tail_sig"], q + 1)
                nc.vector.tensor_tensor(gate, gate, ple_v[:, t, part], ALU.mult).then_inc(s["tail_step"], 1)
                dve.wait_ge(s["tail_step"], q + 1)
                nc.vector.tensor_tensor(row, row, gate, ALU.add).then_inc(s["tail_row"], 1)
                dve.wait_ge(s["tail_row"], q + 1)
                nc.vector.tensor_tensor(result, row, g_final[:, part], ALU.mult).then_inc(s["tail_gain"], 1)
                dve.wait_ge(s["tail_sq"], q + 1)
                so_far = RMS_EPS
                if col:
                    dve.wait_ge(s["tail_mean"], q - t)
                    so_far = stat[:, 12 + q:13 + q]
                row_done = col + width == D
                nc.vector.tensor_scalar(stat[:, 2 + t:3 + t] if row_done else stat[:, 13 + q:14 + q],
                                        stat[:, 8 + q:9 + q], 1.0 / D, so_far, ALU.mult,
                                        ALU.add).then_inc(s["mean_sq" if row_done else "tail_mean"], 1)
                if row_done:
                    dve.wait_ge(s["rstd"], 3 * NT + t + 1)
                    for n in range(2 if t == 0 else 1):
                        dve.wait_ge(s["tail_gain"], n + 1 if t == 0 else 3)
                        nc.vector.tensor_scalar(half_of(tok_tmp, t, n), half_of(tok_tmp, t, n), stat[:, 4 + t:5 + t],
                                                None, ALU.mult).then_inc(s["out_ready"], 1)


_INS = ["x", "p", "norm_mix", "w_in", "b_forget", "w_attn_out", "conv_w", "conv_b", "conv_ln_g", "conv_ln_b",
        "w_conv_out", "w_o", "norm_ffn", "w_router", "b_router", "w_gate", "b_gate", "w_up", "b_up",
        "w_down", "b_down", "norm_ple", "w_ple_gate", "w_ple_proj", "norm_final"]


def kernel(**inputs):
    import numpy as _np
    import concourse.bacc as _bacc
    from concourse.bass_utils import run_bass_kernel_spmd as _run

    nc = _bacc.Bacc("TRN2", target_bir_lowering=False, num_devices=1)
    arrays, args = {}, []
    for name in _INS:
        a = _np.ascontiguousarray(inputs[name])
        arrays[f"in_{name}"] = a
        args.append(nc.dram_tensor(f"in_{name}", a.shape, mybir.dt.from_np(a.dtype), kind="ExternalInput").ap())
    shape = tuple(inputs["x"].shape)
    args.append(nc.dram_tensor("out_block", shape, F32, kind="ExternalOutput").ap())
    build_block(nc, *args)
    return _run(nc, [arrays], core_ids=[0]).results[0]["out_block"]
```
